# Optimizing a Trainium2 kernel written in Bass

```python
import math
import jax, jax.numpy as jnp
from jax import lax
import numpy as np

D_MODEL = 1024
BATCH = 1
SEQ = 256
DEPTH = 2

EPS = 1e-6
RET_HEADS = 4
RET_DK = 128
RET_DV = 128
RET_CHUNK = 128
ROPE_BASE = 10000.0
DA_PATTERNS = ((128, 1), (512, 4), (2048, 16))
DA_HEADS_PER_GROUP = 4
DA_HEADS = DA_HEADS_PER_GROUP * len(DA_PATTERNS)
DA_DH = 64
ML_HEADS = 4
ML_DK = 64
ML_DV = 128
ML_CHUNK = 128
ML_CONV = 4
D_FF = 2816
N_EXPERTS = 8
TOP_K = 2
D_FF_EXPERT = 3584

SPLIT_SIZES = (RET_HEADS * RET_DK, RET_HEADS * RET_DK, RET_HEADS * RET_DV, RET_HEADS * RET_DV,
               DA_HEADS * DA_DH, DA_HEADS * DA_DH, DA_HEADS * DA_DH,
               ML_HEADS * ML_DK, ML_HEADS * ML_DK, ML_HEADS * ML_DV, ML_HEADS * ML_DV, ML_HEADS, ML_HEADS,
               D_MODEL, D_MODEL, D_MODEL)
P_IN = sum(SPLIT_SIZES)

kernel_name = 'hybrid_gated_retention_dilattn_mlstm_moe'

def rms_norm(x, w):
    xf = x.astype(jnp.float32)
    y = xf * lax.rsqrt(jnp.mean(xf * xf, axis=-1, keepdims=True) + EPS)
    return (y * w.astype(jnp.float32)).astype(x.dtype)

def head_rms(x, w):
    xf = x.astype(jnp.float32)
    return xf * lax.rsqrt(jnp.mean(xf * xf, axis=-1, keepdims=True) + EPS) * w.astype(jnp.float32)

def rotary(x, pos):
    half = x.shape[-1] // 2
    inv = jnp.power(ROPE_BASE, -jnp.arange(half, dtype=jnp.float32) / half)
    ang = pos.astype(jnp.float32)[:, None] * inv[None, :]
    cos = jnp.cos(ang)[None, :, None, :]
    sin = jnp.sin(ang)[None, :, None, :]
    xf = x.astype(jnp.float32)
    x1, x2 = xf[..., :half], xf[..., half:]
    return jnp.concatenate([x1 * cos - x2 * sin, x1 * sin + x2 * cos], axis=-1)

def to_chunks(t, c):
    b, s = t.shape[:2]
    t = t.reshape((b, s // c, c) + t.shape[2:])
    return jnp.swapaxes(jnp.swapaxes(t, 0, 1), 2, 3)

def from_chunks(t):
    t = jnp.swapaxes(jnp.swapaxes(t, 2, 3), 0, 1)
    b, n, c = t.shape[:3]
    return t.reshape((b, n * c) + t.shape[3:])

def retention(q, k, v):
    B, S, H, DK = q.shape
    DV = v.shape[-1]
    C = RET_CHUNK
    q = q.astype(jnp.float32)
    k = k.astype(jnp.float32) * (DK ** -0.5)
    v = v.astype(jnp.float32)
    log_gamma = jnp.log1p(-jnp.exp2(-5.0 - jnp.arange(H, dtype=jnp.float32)))
    idx = jnp.arange(C, dtype=jnp.float32)
    rel = idx[:, None] - idx[None, :]
    intra = jnp.where(rel >= 0, jnp.exp(log_gamma[:, None, None] * jnp.maximum(rel, 0.0)), 0.0)
    q_dec = jnp.exp(log_gamma[:, None] * (idx + 1.0))[None, :, :, None]
    k_dec = jnp.exp(log_gamma[:, None] * (C - 1.0 - idx))[None, :, :, None]
    c_dec = jnp.exp(log_gamma * C)[None, :, None, None]

    def step(state, blk):
        qb, kb, vb = blk
        scores = jnp.einsum('bhik,bhjk->bhij', qb, kb) * intra
        out = (jnp.einsum('bhij,bhjv->bhiv', scores, vb)
               + jnp.einsum('bhik,bhkv->bhiv', qb, state) * q_dec)
        state = state * c_dec + jnp.einsum('bhjk,bhjv->bhkv', kb * k_dec, vb)
        return state, out

    state0 = jnp.zeros((B, H, DK, DV), jnp.float32)
    _, out = lax.scan(step, state0, (to_chunks(q, C), to_chunks(k, C), to_chunks(v, C)))
    return from_chunks(out)

def dilated_group(q, k, v, window, dilation):
    B, S, Hg, Dh = q.shape
    M = window // dilation
    L = -(-S // dilation)
    L = -(-L // M) * M
    nb = L // M
    S_pad = L * dilation

    def to_sub(t):
        t = jnp.pad(t, ((0, 0), (0, S_pad - S), (0, 0), (0, 0)))
        t = t.reshape(B, L, dilation, Hg, Dh).transpose(0, 2, 3, 1, 4)
        return t.reshape(B, dilation, Hg, nb, M, Dh)

    def with_prev(t):
        prev = jnp.pad(t[:, :, :, :-1], ((0, 0), (0, 0), (0, 0), (1, 0), (0, 0), (0, 0)))
        return jnp.concatenate([prev, t], axis=4)

    qs = to_sub(q)
    kk = with_prev(to_sub(k))
    vv = with_prev(to_sub(v))
    s = jnp.einsum('brhnqd,brhnkd->brhnqk', qs, kk) * (Dh ** -0.5)
    qi = jnp.arange(M)[:, None]
    kj = jnp.arange(2 * M)[None, :]
    dist = qi + M - kj
    band = (dist >= 0) & (dist <= M)
    first = (jnp.arange(nb)[:, None, None] == 0) & (kj[None] < M)
    valid = band[None] & jnp.logical_not(first)
    s = jnp.where(valid, s, -jnp.inf)
    m = jnp.max(s, axis=-1, keepdims=True)
    p = jnp.exp(s - m)
    l = jnp.sum(p, axis=-1, keepdims=True)
    o = jnp.einsum('brhnqk,brhnkd->brhnqd', p, vv) / l
    lse = (m + jnp.log(l))[..., 0]
    o = o.reshape(B, dilation, Hg, L, Dh).transpose(0, 3, 1, 2, 4).reshape(B, S_pad, Hg, Dh)[:, :S]
    lse = lse.reshape(B, dilation, Hg, L).transpose(0, 3, 1, 2).reshape(B, S_pad, Hg)[:, :S]
    return o, lse

def dilated_attention(q, k, v):
    outs, lses = [], []
    for g, (window, dilation) in enumerate(DA_PATTERNS):
        sl = slice(g * DA_HEADS_PER_GROUP, (g + 1) * DA_HEADS_PER_GROUP)
        o, lse = dilated_group(q[:, :, sl], k[:, :, sl], v[:, :, sl], window, dilation)
        outs.append(o)
        lses.append(lse)
    outs = jnp.stack(outs, axis=0)
    w = jax.nn.softmax(jnp.stack(lses, axis=0), axis=0)
    return jnp.sum(w[..., None] * outs, axis=0)

def causal_dwconv(x, w):
    K, ch = w.shape
    return lax.conv_general_dilated(x, w[:, None, :].astype(x.dtype), window_strides=(1,),
                                    padding=((K - 1, 0),), dimension_numbers=('NWC', 'WIO', 'NWC'),
                                    feature_group_count=ch)

def mlstm(q, k, v, i_pre, f_pre):
    B, S, H, DK = q.shape
    DV = v.shape[-1]
    C = ML_CHUNK
    q = q.astype(jnp.float32)
    k = k.astype(jnp.float32) * (DK ** -0.5)
    v = v.astype(jnp.float32)
    ig = i_pre.astype(jnp.float32)
    logf = jax.nn.log_sigmoid(f_pre.astype(jnp.float32))
    causal = jnp.tril(jnp.ones((C, C), dtype=bool))

    def step(carry, blk):
        Cm, nm, mm = carry
        qb, kb, vb, ib, fb = blk
        b = jnp.cumsum(fb, axis=-1)
        D = jnp.where(causal, b[..., :, None] - b[..., None, :] + ib[..., None, :], -jnp.inf)
        inter = b + mm[..., None]
        m = jnp.maximum(inter, jnp.max(D, axis=-1))
        Dw = jnp.exp(D - m[..., None])
        wi = jnp.exp(inter - m)
        s = jnp.einsum('bhid,bhjd->bhij', qb, kb) * Dw
        num = jnp.einsum('bhij,bhjv->bhiv', s, vb) + wi[..., None] * jnp.einsum('bhid,bhdv->bhiv', qb, Cm)
        den = jnp.sum(s, axis=-1) + wi * jnp.einsum('bhid,bhd->bhi', qb, nm)
        h = num / jnp.maximum(jnp.abs(den), jnp.exp(-m))[..., None]
        m_new = m[..., -1]
        wk = jnp.exp(b[..., -1:] - b + ib - m_new[..., None])
        wc = jnp.exp(b[..., -1] + mm - m_new)
        Cm = wc[..., None, None] * Cm + jnp.einsum('bhj,bhjd,bhjv->bhdv', wk, kb, vb)
        nm = wc[..., None] * nm + jnp.einsum('bhj,bhjd->bhd', wk, kb)
        return (Cm, nm, m_new), h

    carry0 = (jnp.zeros((B, H, DK, DV), jnp.float32), jnp.zeros((B, H, DK), jnp.float32),
              jnp.zeros((B, H), jnp.float32))
    _, out = lax.scan(step, carry0, (to_chunks(q, C), to_chunks(k, C), to_chunks(v, C),
                                     to_chunks(ig, C), to_chunks(logf, C)))
    return from_chunks(out)

def hybrid_mixer(h, w_in, ret_norm_w, da_q_norm_w, da_k_norm_w, ml_conv_w, ml_i_bias, ml_f_bias,
                 ml_norm_w, w_br_ret, w_br_da, w_br_ml, w_out, pos):
    B, S, _ = h.shape
    dt = h.dtype
    z = h @ w_in
    offsets = np.cumsum(np.array(SPLIT_SIZES))[:-1].tolist()
    (rq, rk, rv, rg, dq, dk, dv, mq, mk, mv, mo, mi, mf, g_ret, g_da, g_ml) = jnp.split(z, offsets, axis=-1)

    r_out = retention(rotary(rq.reshape(B, S, RET_HEADS, RET_DK), pos),
                      rotary(rk.reshape(B, S, RET_HEADS, RET_DK), pos),
                      rv.reshape(B, S, RET_HEADS, RET_DV))
    r_out = head_rms(r_out, ret_norm_w.reshape(RET_HEADS, RET_DV)).reshape(B, S, RET_HEADS * RET_DV)
    o_ret = (r_out * jax.nn.silu(rg.astype(jnp.float32))).astype(dt)

    qa = head_rms(dq.reshape(B, S, DA_HEADS, DA_DH), da_q_norm_w)
    ka = head_rms(dk.reshape(B, S, DA_HEADS, DA_DH), da_k_norm_w)
    va = dv.reshape(B, S, DA_HEADS, DA_DH).astype(jnp.float32)
    o_da = dilated_attention(qa, ka, va).reshape(B, S, DA_HEADS_PER_GROUP * DA_DH).astype(dt)

    qk = jax.nn.silu(causal_dwconv(jnp.concatenate([mq, mk], axis=-1), ml_conv_w))
    mq_c, mk_c = jnp.split(qk, 2, axis=-1)
    m_out = mlstm(mq_c.reshape(B, S, ML_HEADS, ML_DK), mk_c.reshape(B, S, ML_HEADS, ML_DK),
                  mv.reshape(B, S, ML_HEADS, ML_DV), mi + ml_i_bias, mf + ml_f_bias)
    m_out = head_rms(m_out, ml_norm_w.reshape(ML_HEADS, ML_DV)).reshape(B, S, ML_HEADS * ML_DV)
    o_ml = (m_out * jax.nn.sigmoid(mo.astype(jnp.float32))).astype(dt)

    y = (jax.nn.sigmoid(g_ret) * (o_ret @ w_br_ret)
         + jax.nn.sigmoid(g_da) * (o_da @ w_br_da)
         + jax.nn.sigmoid(g_ml) * (o_ml @ w_br_ml))
    return y @ w_out

def swiglu(h, w_gate, w_up, w_down):
    return (jax.nn.silu(h @ w_gate) * (h @ w_up)) @ w_down

def moe_swiglu(h, w_router, b_router, w_gate, w_up, w_down):
    B, S, D = h.shape
    ht = h.reshape(B * S, D)
    logits = (ht @ w_router).astype(jnp.float32) + b_router.astype(jnp.float32)
    top_v, top_i = lax.top_k(logits, TOP_K)
    probs = jax.nn.softmax(top_v, axis=-1)
    gates = jnp.sum(jax.nn.one_hot(top_i, N_EXPERTS, dtype=jnp.float32) * probs[..., None], axis=1)
    out = jnp.zeros((B * S, D), jnp.float32)
    for e in range(N_EXPERTS):
        a = jax.nn.silu(ht @ w_gate[e]) * (ht @ w_up[e])
        out = out + gates[:, e:e + 1] * (a @ w_down[e]).astype(jnp.float32)
    return out.astype(h.dtype).reshape(B, S, D)

def setup_inputs(seed: int = 0) -> dict:
    key = jax.random.key(seed)
    ks = jax.random.split(key, 24)
    f32 = jnp.float32

    def nrm(k, shape, scale):
        return jax.random.normal(k, shape, f32) * scale

    n_dense = (DEPTH + 1) // 2
    n_moe = DEPTH // 2
    ret_w = RET_HEADS * RET_DV
    da_out = DA_HEADS_PER_GROUP * DA_DH
    ml_w = ML_HEADS * ML_DV
    return {
        'x': nrm(ks[0], (BATCH, SEQ, D_MODEL), 1.0),
        'norm1_w': 1.0 + nrm(ks[1], (DEPTH, D_MODEL), 0.05),
        'w_in': nrm(ks[2], (DEPTH, D_MODEL, P_IN), D_MODEL ** -0.5),
        'ret_norm_w': 1.0 + nrm(ks[3], (DEPTH, ret_w), 0.05),
        'da_q_norm_w': 1.0 + nrm(ks[4], (DEPTH, DA_DH), 0.05),
        'da_k_norm_w': 1.0 + nrm(ks[5], (DEPTH, DA_DH), 0.05),
        'ml_conv_w': nrm(ks[6], (DEPTH, ML_CONV, 2 * ML_HEADS * ML_DK), ML_CONV ** -0.5),
        'ml_i_bias': nrm(ks[7], (DEPTH, ML_HEADS), 0.1),
        'ml_f_bias': jnp.linspace(3.0, 6.0, ML_HEADS, dtype=f32)[None, :] + nrm(ks[8], (DEPTH, ML_HEADS), 0.1),
        'ml_norm_w': 1.0 + nrm(ks[9], (DEPTH, ml_w), 0.05),
        'w_br_ret': nrm(ks[10], (DEPTH, ret_w, D_MODEL), ret_w ** -0.5),
        'w_br_da': nrm(ks[11], (DEPTH, da_out, D_MODEL), da_out ** -0.5),
        'w_br_ml': nrm(ks[12], (DEPTH, ml_w, D_MODEL), ml_w ** -0.5),
        'w_out': nrm(ks[13], (DEPTH, D_MODEL, D_MODEL), D_MODEL ** -0.5),
        'norm2_w': 1.0 + nrm(ks[14], (DEPTH, D_MODEL), 0.05),
        'ffn_w_gate': nrm(ks[15], (n_dense, D_MODEL, D_FF), D_MODEL ** -0.5),
        'ffn_w_up': nrm(ks[16], (n_dense, D_MODEL, D_FF), D_MODEL ** -0.5),
        'ffn_w_down': nrm(ks[17], (n_dense, D_FF, D_MODEL), D_FF ** -0.5),
        'moe_w_router': nrm(ks[18], (n_moe, D_MODEL, N_EXPERTS), D_MODEL ** -0.5),
        'moe_b_router': nrm(ks[19], (n_moe, N_EXPERTS), 0.01),
        'moe_w_gate': nrm(ks[20], (n_moe, N_EXPERTS, D_MODEL, D_FF_EXPERT), D_MODEL ** -0.5),
        'moe_w_up': nrm(ks[21], (n_moe, N_EXPERTS, D_MODEL, D_FF_EXPERT), D_MODEL ** -0.5),
        'moe_w_down': nrm(ks[22], (n_moe, N_EXPERTS, D_FF_EXPERT, D_MODEL), D_FF_EXPERT ** -0.5),
    }

def reference(x, norm1_w, w_in, ret_norm_w, da_q_norm_w, da_k_norm_w, ml_conv_w, ml_i_bias, ml_f_bias,
              ml_norm_w, w_br_ret, w_br_da, w_br_ml, w_out, norm2_w, ffn_w_gate, ffn_w_up, ffn_w_down,
              moe_w_router, moe_b_router, moe_w_gate, moe_w_up, moe_w_down):
    pos = jnp.arange(x.shape[1], dtype=jnp.int32)
    for layer in range(DEPTH):
        h = rms_norm(x, norm1_w[layer])
        x = x + hybrid_mixer(h, w_in[layer], ret_norm_w[layer], da_q_norm_w[layer], da_k_norm_w[layer],
                             ml_conv_w[layer], ml_i_bias[layer], ml_f_bias[layer], ml_norm_w[layer],
                             w_br_ret[layer], w_br_da[layer], w_br_ml[layer], w_out[layer], pos)
        h = rms_norm(x, norm2_w[layer])
        j = layer // 2
        if layer % 2 == 0:
            x = x + swiglu(h, ffn_w_gate[j], ffn_w_up[j], ffn_w_down[j])
        else:
            x = x + moe_swiglu(h, moe_w_router[j], moe_b_router[j], moe_w_gate[j], moe_w_up[j], moe_w_down[j])
    return x


_drawn_inputs = setup_inputs


def setup_inputs(seed=0):
    import zlib

    import numpy as np

    out = dict(_drawn_inputs(seed))
    spreads = {}
    factors = {'da_q_norm_w': 7.983, 'da_k_norm_w': 4.295, 'ml_i_bias': 64.0, 'moe_b_router': 3.716}
    for name, (base, spread) in spreads.items():
        noise = np.random.default_rng([zlib.crc32(name.encode()), seed]).standard_normal(out[name].shape)
        drawn = base * np.exp(spread * noise) if base else spread * noise
        out[name] = __import__('jax').numpy.asarray(drawn.astype(out[name].dtype))
    for name, factor in factors.items():
        out[name] = (out[name] * factor).astype(out[name].dtype)
    return out
```

```python
from contextlib import ExitStack

import numpy as np
import concourse.bass as bass
from concourse import mybir

F32 = mybir.dt.float32
F32R = mybir.dt.float32r
I32 = mybir.dt.int32
ALU = mybir.AluOpType
ACT = mybir.ActivationFunctionType
AX = mybir.AxisListType.X

P = 128
D = 1024
KD = D // P
S = 256
TT = S // P
DEPTH = 2
EPS = 1e-6
RH, RDV = 4, 128
GROUPS = ((128, 1), (512, 4), (2048, 16))
NG = len(GROUPS)
GH, DH = 4, 64
NH = NG * GH
MH, MDK, MDV = 4, 64, 128
TAPS = 4
FF = 2816
NE, FE = 8, 3584
C = 512
SLOT = 4 * C
KH = KD // 2
BLK = 3 * P

IN_DV_END = 2048 + 3 * NH * DH
IN_QK = IN_DV_END
IN_MV = IN_QK + 2 * MH * MDK
IN_GATES = IN_MV + 2 * MH * MDV
IN_G = IN_GATES + 2 * MH
P_IN = IN_G + 3 * D
Z_RV, Z_RG, Z_DQ = 1024, 1536, 2048
Z_DK = Z_DQ + NH * DH
Z_DV = Z_DK + NH * DH
Z_MV = IN_DV_END
Z_MO = Z_MV + MH * MDV
Z_G = Z_MO + MH * MDV
ZW = Z_G + 3 * D

RING_A, RING_B, RING_L = 4, 6, 2
N_LOOP = 8
N_G = 6
A_SLOTS = 2 + 2 * N_LOOP + 6 + 2 * N_G + 2 + 1 + 2 + 4
F_CHUNKS = FF // C
F_SLOTS = 6 * (F_CHUNKS + 1)
E_CHUNKS = FE // C
E_SLOTS = 6 * E_CHUNKS
F_TILES = TT * (F_CHUNKS + 1)
F_SUMS = 2 * F_TILES
E_SUMS = 2 * E_CHUNKS + 2 * TT
EXTRA = TT * S // P - 1
ITEMS = NE + EXTRA
CAP = P

CONST = {}
SMALL = {}


def _place(table, parts):
    at = 0
    for name, width in parts:
        table[name] = (at, at + width)
        at += width
    return at


N_CONST = _place(CONST, [("ident", P), ("rot", 2 * TT * 64), ("decay", RH * BLK), ("damask", NG * BLK),
                         ("mlmask", BLK), ("tri", P), ("ones", P), ("iota", P), ("sel", MH * P)])
N_SMALL = _place(SMALL, [("norm1", DEPTH * KD), ("norm2", DEPTH * KD), ("retn", DEPTH * 4), ("mln", DEPTH * 4),
                         ("qn", DEPTH), ("kn", DEPTH), ("conv", DEPTH * 4 * TAPS), ("ib", DEPTH), ("fb", DEPTH),
                         ("rb", NE), ("gates", DEPTH * KD * 8), ("router", KD * NE)])


def build(nc, a):
    with ExitStack() as ctx:
        def sb(name, shape, dt=F32):
            return ctx.enter_context(nc.sbuf_tensor("sb_" + name, shape, dt))

        def sem(name):
            return ctx.enter_context(nc.semaphore(name))

        const = sb("const", [P, N_CONST])
        small = sb("small", [P, N_SMALL])
        x = sb("x", [P, TT, D])
        ringa = sb("ringa", [P, RING_A, SLOT])
        z = sb("z", [P, TT, ZW])
        whi = sb("whi", [P, RING_L, SLOT], F32R)
        wlo = sb("wlo", [P, RING_L, SLOT], F32R)
        hhi = sb("hhi", [P, KD, S], F32R)
        hlo = sb("hlo", [P, KD, S], F32R)
        ahi = sb("ahi", [P, 4, S], F32R)
        alo = sb("alo", [P, 4, S], F32R)
        w1 = sb("w1", [P, TT * D])
        w2 = sb("w2", [P, GH * BLK])
        w4a = sb("w4a", [P, 4, S + TAPS - 1])
        w4b = sb("w4b", [P, 4, S])
        rows = sb("rows", [MH, 3, S])
        st = sb("st", [P, 448])
        root = sb("root", [P, 128])
        eid = sb("eid", [1, 16], I32)
        ps = ctx.enter_context(nc.psum_tensor("ps", [P, 8, 512], F32))

        def con(name):
            return const[:, CONST[name][0]:CONST[name][1]]

        def par(name, at, n=1):
            return small[:, SMALL[name][0] + at:SMALL[name][0] + at + n]

        zf = z[:, :, :].rearrange("p t n -> p (t n)")
        ident, tri, ones, iota = con("ident"), con("tri"), con("ones"), con("iota")
        rot = con("rot").rearrange("p (t f d) -> p t f d", t=TT, f=2)
        decay = con("decay").rearrange("p (h n) -> p h n", h=RH)
        damask = con("damask").rearrange("p (g n) -> p g n", g=NG)
        mlmask = con("mlmask")

        def stat(at, n):
            return st[:, at:at + n]
        ss2, rstd2 = stat(0, 2), stat(2, 2)
        z8 = stat(4, 16).rearrange("p (t n) -> p t n", t=TT)
        ccol = stat(20, 8).rearrange("p (t h) -> p t h", t=TT)
        emcol = stat(28, 8)
        rss, rrs = stat(36, 8), stat(44, 8)
        mss, mrs, mden = stat(52, 8), stat(60, 8), stat(68, 8)
        dss = stat(76, 48).rearrange("p (t n) -> p t n", t=TT)
        drs = stat(124, 48).rearrange("p (t n) -> p t n", t=TT)
        dneg = stat(172, 24).rearrange("p (g t h) -> p g t h", g=NG, t=TT)
        dl = stat(196, 24).rearrange("p (g t h) -> p g t h", g=NG, t=TT)
        dco = stat(220, 24).rearrange("p (g t h) -> p g t h", g=NG, t=TT)
        dtmp = stat(244, 8)
        lg = stat(252, 16).rearrange("p (t n) -> p t n", t=TT)
        m1 = stat(268, 16).rearrange("p (t n) -> p t n", t=TT)
        m2 = stat(284, 16).rearrange("p (t n) -> p t n", t=TT)
        rt = stat(300, 16).rearrange("p (t n) -> p t n", t=TT)
        v12 = stat(316, 8).rearrange("p (t n) -> p t n", t=TT)
        posx = stat(324, 24).rearrange("p (t n) -> p t n", t=TT)
        gatex = stat(348, 24).rearrange("p (t n) -> p t n", t=TT)
        cnt, big, rank = stat(372, 8), stat(380, 8), stat(388, 8)
        eidf = stat(396, 16)
        selx = stat(412, 8)
        rtmp = stat(420, 16).rearrange("p (t n) -> p t n", t=TT)

        blk2 = w2[:, :].rearrange("p (h n) -> p h n", h=4)
        blkz = z[:, :, 0:2 * BLK].rearrange("p t (h n) -> p t h n", h=2)
        blkm = z[:, :, 2 * BLK:4 * BLK].rearrange("p t (h n) -> p t h n", h=2)
        qk = w1[:, :].rearrange("p (c s) -> p c s", s=S)
        w1t = w1[:, :].rearrange("p (t n) -> p t n", t=TT)
        big1 = w1[:, 0:TT * 512].rearrange("p (t n) -> p t n", t=TT)
        big2 = w1[:, TT * 512:].rearrange("p (t n) -> p t n", t=TT)
        rowt = w2[0:MH, :].rearrange("p (r s) -> p r s", s=S)
        ringb = zf[:, 0:RING_B * SLOT].rearrange("p (r n) -> p r n", r=RING_B)
        spare = zf[:, RING_B * SLOT:]
        act_sb = spare[:, 0:TT * C].rearrange("p (t n) -> p t n", t=TT)
        y_sb = z[:, :, Z_G:Z_G + D]
        sil_sb = spare[:, TT * C:2 * TT * C].rearrange("p (t n) -> p t n", t=TT)
        yacc = spare[:, 2 * TT * C:2 * TT * C + D]
        pick = spare[:, 3072:3072 + TT * CAP].rearrange("p (t n) -> p t n", t=TT)
        pickg = spare[:, 3328:3328 + TT * CAP].rearrange("p (t n) -> p t n", t=TT)
        spread = spare[:, 3584:3584 + S]

        raw_a = [sem(f"raw_a{i}") for i in range(RING_A)]
        raw_b = [sem(f"raw_b{i}") for i in range(RING_B)]
        hi_done = sem("hi_done")
        lo_pool = sem("lo_pool")
        lo_dve = sem("lo_dve")
        used = sem("used")
        consts_in, x_in, out_done = sem("consts_in"), sem("x_in"), sem("out_done")
        dve_chain, act_chain = sem("dve_chain"), sem("act_chain")
        tok_ready = sem("tok_ready")
        ht_turned, ht_hi, ht_lo = sem("ht_turned"), sem("ht_hi"), sem("ht_lo")
        yt_turned = sem("yt_turned")
        conv_pad, conv_y, conv_act = (sem(n) for n in ("conv_pad", "conv_y", "conv_act"))
        z8_mm, z8_sb, row_t, row_abs, row_exp, row_ln, rows_ok = (
            sem(n) for n in ("z8_mm", "z8_sb", "row_t", "row_abs", "row_exp", "row_ln", "rows_ok"))
        col_t, col_sb, col_exp = sem("col_t"), sem("col_sb"), sem("col_exp")
        z_out, g_out = sem("z_out"), sem("g_out")
        rg_act, mo_act, rotated = sem("rg_act"), sem("mo_act"), sem("rotated")
        rqk_t, rqk_sb, rsc_mm, rsc_sb, rpv_mm, rpv_sq, ro_out = (
            sem(n) for n in ("rqk_t", "rqk_sb", "rsc_mm", "rsc_sb", "rpv_mm", "rpv_sq", "ro_out"))
        dsq, dsum, dn_ok = sem("dsq"), sem("dsum"), sem("dn_ok")
        dqk_t, dqk_sb, dsc_mm, dsc_sb, dexp, dp_t, dp_sb, dpv_mm, dpv_sb = (
            sem(n) for n in ("dqk_t", "dqk_sb", "dsc_mm", "dsc_sb", "dexp", "dp_t", "dp_sb", "dpv_mm", "dpv_sb"))
        dln, dlse, dwt, do_out = sem("dln"), sem("dlse"), sem("dwt"), sem("do_out")
        msel_mm, mdw_in, mdw, msc_mm, msc_sb, mpv_mm, mh_sb, msq, mo_out = (
            sem(n) for n in ("msel_mm", "mdw_in", "mdw", "msc_mm", "msc_sb", "mpv_mm", "mh_sb", "msq", "mo_out"))
        ot_t, ot_hi, ot_lo, br_half, br_out = (sem(n) for n in ("ot_t", "ot_hi", "ot_lo", "br_half", "br_out"))
        sig_ok, x_end = sem("sig_ok"), sem("x_end")
        silu, a_ok, a_t, a_hi, a_lo, d_out = (sem(n) for n in ("silu", "a_ok", "a_t", "a_hi", "a_lo", "d_out"))
        lg_mm, lg_e, lg_d, sel_ok, cnt_mm, route_ok = (
            sem(n) for n in ("lg_mm", "lg_e", "lg_d", "sel_ok", "cnt_mm", "route_ok"))
        pick_ok, gather_mm, gt_hi, gt_lo, spread_t, spread_sb, scat_mm, y_zero = (
            sem(n) for n in ("pick_ok", "gather_mm", "gt_hi", "gt_lo", "spread_t", "spread_sb", "scat_mm", "y_zero"))

        def number(layer, phase, s, r=0):
            at = layer * (A_SLOTS + F_SLOTS) + (A_SLOTS if phase == "B" else 0) + s
            return r * (RING_A if phase == "A" else RING_B) + at

        def ordinal(layer, phase, s):
            return layer * (A_SLOTS if phase == "A" else F_SLOTS) + s

        def lane(layer, phase, s):
            return number(layer, phase, s) % RING_L

        def ring(phase):
            return (RING_A, raw_a, ringa[:, :, :]) if phase == "A" else (RING_B, raw_b, ringb)

        def raw_slot(layer, phase, s):
            n, _, tile = ring(phase)
            return tile[:, ordinal(layer, phase, s) % n, :]

        def lo_count(layer, phase, s, r=0):
            if phase == "A":
                return lo_pool, r * RING_A + (layer * (A_SLOTS + F_SLOTS // 3) + s + 1)
            six, v = s // 6, s % 6
            if v % 3 == 2:
                return lo_pool, r * 2 + ((layer + 1) * A_SLOTS + layer * (F_SLOTS // 3) + 2 * six + v // 3 + 1)
            return lo_dve, r * 4 + (layer * (F_SLOTS // 3 * 2) + 4 * six + 2 * (v // 3) + v % 3 + 1)

        def wait_lo(eng, layer, phase, s, r=0):
            eng.wait_ge(*lo_count(layer, phase, s, r))

        def wait_split(eng, layer, phase, s, r=0):
            size = ring(phase)[0]
            if number(layer, phase, s) < size:
                return
            if phase == "A" and s < size:
                if layer == 0:
                    eng.wait_ge(*lo_count(0, "A", s - size))
                else:
                    eng.wait_ge(*lo_count(0, "B", F_SLOTS - 1))
                    eng.wait_ge(*lo_count(0, "B", F_SLOTS - 2))
            elif phase == "B" and layer == 0 and s < size:
                eng.wait_ge(*lo_count(0, "A", A_SLOTS + s - size))
            else:
                eng.wait_ge(*lo_count(layer, phase, s - size, r))

        def hi_of(act, layer, phase, s, r=0):
            size, sems, _ = ring(phase)
            o = ordinal(layer, phase, s)
            act.wait_ge(sems[o % size], (r + (o // size + 1)) * 16)
            if number(layer, phase, s) >= RING_L:
                act.wait_ge(used, number(layer, phase, s, r) + 1 - RING_L)
            n = width(layer, phase, s)
            nc.scalar.activation(whi[:, lane(layer, phase, s), 0:n], raw_slot(layer, phase, s)[:, 0:n],
                                 ACT.Copy).then_inc(hi_done, 1)

        def lo_of(eng, layer, phase, s, r=0):
            eng.wait_ge(hi_done, number(layer, phase, s, r) + 1)
            k, n = lane(layer, phase, s), width(layer, phase, s)
            eng.tensor_tensor(wlo[:, k, 0:n], raw_slot(layer, phase, s)[:, 0:n], whi[:, k, 0:n].bitcast(F32),
                              ALU.subtract).then_inc(lo_count(layer, phase, s)[0], 1)

        def wait_used(eng, layer, phase, s, r=0):
            eng.wait_ge(used, number(layer, phase, s, r) + 1)

        Q_HALF, Q_MV, Q_MO, Q_G = N_LOOP, N_LOOP + 1, N_LOOP + 2, N_LOOP + 3
        N_Q = Q_G + N_G
        S_BR = 2 + 2 * N_Q

        def chunk(q):
            if q < N_LOOP:
                return q * C, q * C, C
            if q == Q_HALF:
                return N_LOOP * C, N_LOOP * C, IN_DV_END - N_LOOP * C
            if q <= Q_MO:
                return IN_MV + (q - Q_MV) * C, Z_MV + (q - Q_MV) * C, C
            return IN_G + (q - Q_G) * C, Z_G + (q - Q_G) * C, C

        HALF = FF - F_CHUNKS * C

        def width(layer, phase, s):
            if phase == "A" and 2 <= s < S_BR:
                return KH * chunk((s - 2) // 2)[2]
            if phase == "B" and layer == 0 and s >= F_SLOTS - 8:
                return KH * HALF if s < F_SLOTS - 4 else (SLOT if s < F_SLOTS - 2 else HALF // P * C)
            return SLOT

        block = ctx.enter_context(nc.Block())

        @block.sync
        def _(sp):
            def load(layer, phase, s, src, r=0, k=KH):
                wait_split(sp, layer, phase, s, r)
                size, sems, _ = ring(phase)
                dst = raw_slot(layer, phase, s)[:, 0:width(layer, phase, s)].rearrange("p (k n) -> p k n", k=k)
                sp.dma_start(dst, src).then_inc(sems[ordinal(layer, phase, s) % size], 16)

            def part(w, k0, kn, c0, n):
                return w[k0 * P:(k0 + kn) * P, c0:c0 + n].rearrange("(k p) n -> p k n", p=P)

            def run(w, k0, kn, c0, n):
                return w[k0 * P:(k0 + kn) * P, bass.ds(c0, n)].rearrange("(k p) n -> p k n", p=P)

            sp.dma_start(x[:, :, :], a["x"].rearrange("b (t p) d -> p (b t) d", p=P)).then_inc(x_in, 16)
            sp.dma_start(const[:, :], a["const"]).then_inc(consts_in, 16)
            sp.dma_start(small[:, :], a["small"]).then_inc(consts_in, 16)

            for layer in range(DEPTH):
                w_in = a["w_in"][layer]
                for h in range(2):
                    load(layer, "A", h, part(w_in, KH * h, KH, IN_QK, C))
                for s in range(4):
                    load(layer, "A", 2 + s, part(w_in, KH * (s % 2), KH, s // 2 * C, C))
                with sp.Fori(0, N_LOOP // 2 - 1) as i:
                    for s in range(4):
                        load(layer, "A", 6 + s, run(w_in, KH * (s % 2), KH, i * (2 * C) + (2 + s // 2) * C, C), r=i)
                for q in range(N_LOOP, N_Q):
                    c0, _, n = chunk(q)
                    for h in range(2):
                        load(layer, "A", 2 + 2 * q + h, part(w_in, KH * h, KH, c0, n))
                for h in range(2):
                    load(layer, "A", S_BR + h, part(a["w_br_ret"][layer], 0, 4, h * C, C))
                load(layer, "A", S_BR + 2, part(a["w_br_da"][layer], 0, 2, 0, D), k=2)
                for h in range(2):
                    load(layer, "A", S_BR + 3 + h, part(a["w_br_ml"][layer], 0, 4, h * C, C))
                for s in range(4):
                    load(layer, "A", S_BR + 5 + s, part(a["w_out"][layer], KH * (s % 2), KH, s // 2 * C, C))

                sp.wait_ge(yt_turned, 4 * (layer + 1))
                if layer == 0:
                    gu, wd = (a["ffn_w_gate"][0], a["ffn_w_up"][0]), a["ffn_w_down"][0]
                    for s in range(4):
                        load(0, "B", s, part(gu[s // 2], KH * (s % 2), KH, 0, C))
                    for s in range(4):
                        load(0, "B", 4 + s, part(gu[s // 2], KH * (s % 2), KH, C, C))
                    for h in range(2):
                        load(0, "B", 8 + h, part(wd, 0, 4, h * C, C))
                    with sp.Fori(0, F_CHUNKS - 2) as i:
                        for s in range(4):
                            load(0, "B", 10 + s, run(gu[s // 2], KH * (s % 2), KH, i * C + 2 * C, C), r=i)
                        for h in range(2):
                            load(0, "B", 14 + h, wd[bass.ds(i * C + C, C), h * C:(h + 1) * C]
                                 .rearrange("(k p) n -> p k n", p=P), r=i)
                    s0 = F_SLOTS - 8
                    for s in range(4):
                        load(0, "B", s0 + s, part(gu[s // 2], KH * (s % 2), KH, F_CHUNKS * C, HALF))
                    for h in range(2):
                        load(0, "B", s0 + 4 + h, part(wd, 4 * (F_CHUNKS - 1), 4, h * C, C))
                    for h in range(2):
                        load(0, "B", s0 + 6 + h, part(wd, 4 * F_CHUNKS, HALF // P, h * C, C), k=HALF // P)
                else:
                    sp.wait_ge(route_ok, 1)
                    items = sp.value_load(eid[0:1, 15:16], min_val=NE, max_val=ITEMS)
                    with sp.Fori(0, items) as j:
                        e = sp.value_load(eid[0:1, bass.ds(j, 1)], min_val=0, max_val=NE - 1)
                        gu = [a[n][0].rearrange("e d f -> (e d) f") for n in ("moe_w_gate", "moe_w_up")]
                        wd = a["moe_w_down"][0].rearrange("e f d -> (e f) d")

                        def from_gu(s, c0):
                            return gu[s // 2][bass.ds(e * D + KH * (s % 2) * P, KH * P), c0].rearrange(
                                "(k p) n -> p k n", p=P)

                        def from_d(h, f0):
                            return wd[bass.ds(f0, C), h * C:(h + 1) * C].rearrange("(k p) n -> p k n", p=P)

                        for s in range(4):
                            load(1, "B", s, from_gu(s, slice(0, C)), r=j * E_CHUNKS)
                        with sp.Fori(0, E_CHUNKS - 1) as i:
                            for s in range(4):
                                load(1, "B", 4 + s, from_gu(s, bass.ds(i * C + C, C)), r=j * E_CHUNKS + i)
                            for h in range(2):
                                load(1, "B", 8 + h, from_d(h, e * FE + i * C), r=j * E_CHUNKS + i)
                        for h in range(2):
                            load(1, "B", E_SLOTS - 2 + h, from_d(h, e * FE + (E_CHUNKS - 1) * C), r=j * E_CHUNKS)
            sp.wait_ge(x_end, 1)
            sp.dma_start(a["out"].rearrange("b (t p) d -> p (b t) d", p=P), x[:, :, :]).then_inc(out_done, 16)
            sp.wait_ge(out_done, 16)

        @block.gpsimd
        def _(pool):
            for layer in range(DEPTH):
                for s in range(2):
                    lo_of(pool, layer, "A", s)
                with pool.Fori(0, N_LOOP // 2) as i:
                    for s in range(4):
                        lo_of(pool, layer, "A", 2 + s, i)
                for s in range(2 + 2 * N_LOOP, A_SLOTS):
                    lo_of(pool, layer, "A", s)
                if layer == 0:
                    with pool.Fori(0, F_CHUNKS - 1) as i:
                        for s in (2, 5):
                            lo_of(pool, 0, "B", s, i)
                    for s in range(6 * (F_CHUNKS - 1), F_SLOTS):
                        if s % 3 == 2:
                            lo_of(pool, 0, "B", s)
                else:
                    pool.wait_ge(route_ok, 1)
                    items = pool.value_load(eid[0:1, 15:16], min_val=NE, max_val=ITEMS)
                    with pool.Fori(0, items * E_CHUNKS) as i:
                        for s in (2, 5):
                            lo_of(pool, 1, "B", s, i)

        def pair(q):
            return 2 * (q % 2)

        @block.tensor
        def _(pe):
            def mm3(out, lh, ll, rh, rl, start, stop):
                nc.tensor.matmul(out, lh, rh, start=start, stop=False)
                nc.tensor.matmul(out, ll, rh, start=False, stop=False)
                return nc.tensor.matmul(out, lh, rl, start=False, stop=stop)

            def mm(out, l, r, start=True, stop=True):
                return nc.tensor.matmul(out, l, r, start=start, stop=stop)

            def turn(out, src):
                n = src.shape[0]
                return nc.tensor.transpose(out, src, ident[0:n, 0:n])

            def product(layer, phase, s, r, banks, lhs, rows0, first, last, n=C, k=KH):
                wait_lo(pe, layer, phase, s, r)
                ln = lane(layer, phase, s)
                hi = whi[:, ln, 0:k * n].rearrange("p (k n) -> p k n", k=k)
                lo = wlo[:, ln, 0:k * n].rearrange("p (k n) -> p k n", k=k)
                lh, ll = lhs
                for t, b in enumerate(banks):
                    for kk in range(k):
                        m = mm3(ps[:, b, 0:n], lh[:, rows0 + kk, t * P:(t + 1) * P],
                                      ll[:, rows0 + kk, t * P:(t + 1) * P], hi[:, kk, :], lo[:, kk, :],
                                      first and kk == 0, last and kk == k - 1)
                m.then_inc(used, 1)

            def turn_tokens(src, done):
                for b in range(4):
                    for kk in range(2):
                        for t in range(TT):
                            m = turn(ps[:, 4 + b, kk * S + t * P:kk * S + (t + 1) * P],
                                     src[:, t, (2 * b + kk) * P:(2 * b + kk + 1) * P])
                    m.then_inc(done, 1)

            pe.wait_ge(consts_in, 32)
            for layer in range(DEPTH):
                L = layer + 1

                pe.wait_ge(tok_ready, 2 * (3 * layer + 1))
                if layer > 0:
                    pe.wait_ge(d_out, 4 * (F_CHUNKS + 1))
                turn_tokens(w1t, ht_turned)
                pe.wait_ge(ht_lo, 4 * (3 * layer + 1))

                for s in range(2):
                    wait_lo(pe, layer, "A", s)
                    hi, lo = (w[:, lane(layer, "A", s), :].rearrange("p (k n) -> p k n", n=C) for w in (whi, wlo))
                    for c in range(4):
                        for kk in range(KH):
                            m = mm3(ps[:, c, 0:S], hi[:, kk, c * P:(c + 1) * P], lo[:, kk, c * P:(c + 1) * P],
                                    hhi[:, KH * s + kk, :], hlo[:, KH * s + kk, :],
                                    s == 0 and kk == 0, s == 1 and kk == KH - 1)
                    m.then_inc(used, 1)
                for t in range(TT):
                    for k in range(KD):
                        for part_, h in enumerate((hhi, hlo)):
                            m = mm(ps[:, 4, t * 8:t * 8 + 8], h[:, k, t * P:(t + 1) * P].bitcast(F32),
                                   par("gates", (layer * KD + k) * 8, 8),
                                   start=k == 0 and part_ == 0, stop=k == KD - 1 and part_ == 1)
                m.then_inc(z8_mm, 1)

                def z_chunk(q, h, r=0):
                    if h == 0:
                        if q < 2:
                            pe.wait_ge(conv_pad, L)
                        elif q <= Q_G + 1:
                            pe.wait_ge(z_out, r * 2 + (layer * Q_G + q - 1))
                        else:
                            pe.wait_ge(g_out, layer * N_G + q - 1 - Q_G)
                    b, n = pair(q), chunk(q)[2]
                    product(layer, "A", 2 + 2 * q + h, r, (b, b + 1), (hhi, hlo), KH * h, h == 0, h == 1, n)

                z_chunk(0, 0)
                z_chunk(0, 1)
                pe.wait_ge(z8_sb, L)
                for g in range(2):
                    for t in range(TT):
                        m = turn(ps[0:MH, 5, g * S + t * P:g * S + (t + 1) * P], z8[:, t, g * MH:(g + 1) * MH])
                m.then_inc(row_t, 1)
                z_chunk(1, 0)
                z_chunk(1, 1)
                with pe.Fori(0, N_LOOP // 2 - 1) as i:
                    for q in (2, 3):
                        z_chunk(q, 0, i)
                        z_chunk(q, 1, i)

                def ml_columns():
                    pe.wait_ge(rows_ok, L)
                    for g, row in enumerate((0, 2)):
                        for t in range(TT):
                            m = turn(ps[:, 7, g * 8 + t * 4:g * 8 + t * 4 + 4], rows[:, row, t * P:(t + 1) * P])
                    m.then_inc(col_t, 1)

                def ret_turn():
                    pe.wait_ge(rotated, L)
                    pe.wait_ge(col_sb, L)
                    for c in range(8):
                        for t in range(TT):
                            m = turn(ps[:, 4 + c // 2, c % 2 * S + t * P:c % 2 * S + (t + 1) * P],
                                     z[:, t, c * P:(c + 1) * P])
                    m.then_inc(rqk_t, 1)

                def ret_scores():
                    pe.wait_ge(rqk_sb, L)
                    for h in range(RH):
                        mm(ps[:, 4 + h, 0:S], qk[:, RH + h, 0:P], qk[:, h, :])
                        m = mm(ps[:, 4 + h, S:BLK], qk[:, RH + h, P:S], qk[:, h, P:S])
                    m.then_inc(rsc_mm, 1)

                def weighted(bank0, src, vcol, width, m_of=None):
                    for h in range(4):
                        o = slice(h * width, (h + 1) * width)
                        v = [z[:, t, vcol + h * width:vcol + (h + 1) * width] for t in range(TT)]
                        mm(ps[:, bank0, o], src(h)[:, 0:P], v[0])
                        mm(ps[:, bank0 + 1, o], src(h)[:, P:S], v[0], stop=False)
                        m = mm(ps[:, bank0 + 1, o], src(h)[:, S:BLK], v[1], start=False)
                    return m

                def ret_out():
                    pe.wait_ge(rsc_sb, L)
                    weighted(4, lambda h: blk2[:, h, :], Z_RV, RDV).then_inc(rpv_mm, 1)

                def da_turn(g):
                    if g == 0:
                        pe.wait_ge(dn_ok, L)
                        pe.wait_ge(ro_out, L)
                    else:
                        pe.wait_ge(dp_sb, layer * NG + g)
                    for b, col in enumerate((Z_DQ, Z_DK)):
                        for c in range(2):
                            for t in range(TT):
                                m = turn(ps[:, 4 + b, c * S + t * P:c * S + (t + 1) * P],
                                         z[:, t, col + (2 * g + c) * P:col + (2 * g + c + 1) * P])
                    m.then_inc(dqk_t, 1)

                def da_scores(g):
                    pe.wait_ge(dqk_sb, layer * NG + g + 1)
                    if g > 0:
                        pe.wait_ge(dpv_sb, layer * NG + g)
                    for h in range(GH):
                        r = slice(h % 2 * DH, (h % 2 + 1) * DH)
                        q, k = qk[r, h // 2, :], qk[r, 2 + h // 2, :]
                        mm(ps[:, 4 + h, 0:P], q[:, 0:P], k[:, 0:P])
                        m = mm(ps[:, 4 + h, P:BLK], q[:, P:S], k)
                    m.then_inc(dsc_mm, 1)

                def da_turn_p(g):
                    pe.wait_ge(dexp, layer * NG + g + 1)
                    for h in range(GH):
                        for j in range(3):
                            m = turn(ps[:, 4 + h, j * P:(j + 1) * P], blk2[:, h, j * P:(j + 1) * P])
                    m.then_inc(dp_t, 1)

                def da_out(g):
                    pe.wait_ge(dp_sb, layer * NG + g + 1)
                    weighted(6, lambda h: blkz[:, h // 2, h % 2, :], Z_DV + g * GH * DH, DH).then_inc(dpv_mm, 1)

                def ml_spread():
                    for h in range(MH):
                        m = mm(ps[:, 4 + h // 2, h % 2 * S:(h % 2 + 1) * S], con("sel")[0:MH, h * P:(h + 1) * P],
                               rows[:, 1, :])
                    m.then_inc(msel_mm, 1)

                def ml_scores():
                    pe.wait_ge(conv_act, L)
                    pe.wait_ge(mdw_in, L)
                    pe.wait_ge(dpv_sb, L * NG)
                    for h in range(MH):
                        r = slice(h % 2 * MDK, (h % 2 + 1) * MDK)
                        q, k = w4b[r, h // 2, :], w4b[r, 2 + h // 2, :]
                        mm(ps[:, 4 + h, 0:S], k[:, 0:P], q)
                        m = mm(ps[:, 4 + h, S:BLK], k[:, P:S], q[:, P:S])
                    m.then_inc(msc_mm, 1)

                def ml_out():
                    pe.wait_ge(msc_sb, L)
                    s = lambda h: blkm[:, h // 2, h % 2, :]
                    weighted(4, s, Z_MV, MDV)
                    one = ones[:, 0:1]
                    for h in range(MH):
                        mm(ps[:, 6, h:h + 1], s(h)[:, 0:P], one)
                        mm(ps[:, 6, MH + h:MH + h + 1], s(h)[:, P:S], one, stop=False)
                        m = mm(ps[:, 6, MH + h:MH + h + 1], s(h)[:, S:BLK], one, start=False)
                    m.then_inc(mpv_mm, 1)

                behind = {
                    (Q_HALF, 0): (ml_columns,), (Q_HALF, 1): (ret_turn,),
                    (Q_MV, 0): (ret_scores,), (Q_MV, 1): (ret_out,),
                    (Q_MO, 0): (lambda: da_turn(0),), (Q_MO, 1): (lambda: da_scores(0),),
                    (Q_G, 0): (lambda: da_turn_p(0),), (Q_G, 1): (lambda: da_turn(1), lambda: da_out(0)),
                    (Q_G + 1, 0): (lambda: da_scores(1),), (Q_G + 1, 1): (lambda: da_turn_p(1),),
                    (Q_G + 2, 0): (lambda: da_turn(2), lambda: da_out(1)), (Q_G + 2, 1): (lambda: da_scores(2),),
                    (Q_G + 3, 0): (lambda: da_turn_p(2),), (Q_G + 3, 1): (lambda: da_out(2), ml_spread),
                    (Q_G + 4, 0): (ml_scores,), (Q_G + 4, 1): (ml_out,),
                }
                for q in range(Q_HALF, N_Q):
                    for h in range(2):
                        z_chunk(q, h)
                        for step in behind.get((q, h), ()):
                            step()

                def turn_out(n, bank, col):
                    for kk in range(2):
                        for t in range(TT):
                            m = turn(ps[:, bank, kk * S + t * P:kk * S + (t + 1) * P],
                                     z[:, t, col + kk * P:col + (kk + 1) * P])
                    m.then_inc(ot_t, 1)
                pe.wait_ge(mo_out, L)
                pe.wait_ge(do_out, L)
                turn_out(0, 4, Z_RG)
                turn_out(1, 5, Z_RG + 2 * P)
                turn_out(2, 6, Z_DQ)
                turn_out(3, 7, Z_MO)
                pe.wait_ge(ot_lo, layer * 5 + 1)
                turn_out(4, 4, Z_MO + 2 * P)

                def branch(slot, bank, lhs):
                    product(layer, "A", S_BR + slot, 0, (bank, bank + 1), lhs, 0, True, True)
                pe.wait_ge(g_out, L * N_G)
                pe.wait_ge(ot_lo, layer * 5 + 2)
                branch(0, 0, (hhi, hlo))
                branch(1, 2, (hhi, hlo))
                pe.wait_ge(ot_lo, layer * 5 + 3)
                wait_lo(pe, layer, "A", S_BR + 2)
                ln = lane(layer, "A", S_BR + 2)
                hi, lo = (w[:, ln, :].rearrange("p (k n) -> p k n", k=2) for w in (whi, wlo))
                for half in range(2):
                    pe.wait_ge(br_out, layer * 6 + 1 + half)
                    for t in range(TT):
                        for kk in range(2):
                            m = mm3(ps[:, 2 * half + t, :], hhi[:, 4 + kk, t * P:(t + 1) * P],
                                    hlo[:, 4 + kk, t * P:(t + 1) * P], hi[:, kk, half * C:(half + 1) * C],
                                    lo[:, kk, half * C:(half + 1) * C], kk == 0, kk == 1)
                    m.then_inc(used if half else br_half, 1)
                pe.wait_ge(ot_lo, layer * 5 + 5)
                for half in range(2):
                    pe.wait_ge(br_out, layer * 6 + 3 + half)
                    branch(3 + half, 2 * half, (ahi, alo))

                pe.wait_ge(tok_ready, 2 * (3 * layer + 2))
                turn_tokens(y_sb, yt_turned)
                pe.wait_ge(ht_lo, 4 * (3 * layer + 2))
                for half in range(2):
                    pe.wait_ge(br_out, layer * 6 + 5 + half)
                    for kh in range(2):
                        product(layer, "A", S_BR + 5 + 2 * half + kh, 0, (2 * half, 2 * half + 1), (hhi, hlo),
                                KH * kh, kh == 0, kh == 1)

                pe.wait_ge(tok_ready, 2 * (3 * layer + 3))
                turn_tokens(w1t, ht_turned)
                pe.wait_ge(ht_lo, 4 * (3 * layer + 3))
                if layer == 0:
                    def f_gate(s, i, r=0, n=C):
                        if s > 0:
                            pe.wait_ge(silu, i * 2)
                        for h in range(2):
                            product(0, "B", s + h, r, (0, 1), (hhi, hlo), KH * h, h == 0, h == 1, n)

                    def f_up(s, i, r=0, n=C):
                        if s > 2:
                            pe.wait_ge(a_ok, i * 2)
                        for h in range(2):
                            product(0, "B", s + h, r, (2, 3), (hhi, hlo), KH * h, h == 0, h == 1, n)

                    def f_turn(i, n=4, first=False):
                        pe.wait_ge(a_ok, i * 2 + 2)
                        if not first:
                            pe.wait_ge(d_out, i * 4)
                        for t in range(TT):
                            for k in range(n):
                                m = turn(ps[:, 4 + t, k * P:(k + 1) * P], act_sb[:, t, k * P:(k + 1) * P])
                            m.then_inc(a_t, 1)

                    def f_down(s, i, r=0, k=4):
                        pe.wait_ge(a_lo, i * 2 + 2)
                        for h in range(2):
                            product(0, "B", s + h, r, (6 - 2 * h, 7 - 2 * h), (ahi, alo), 0, True, True, k=k)

                    f_gate(0, 0)
                    f_up(2, 0)
                    f_gate(4, 1)
                    f_turn(0, first=True)
                    f_up(6, 1)
                    f_down(8, 0)
                    with pe.Fori(0, F_CHUNKS - 2) as i:
                        f_gate(10, i + 2, i)
                        f_turn(i + 1)
                        f_up(12, i + 2, i)
                        f_down(14, i + 1, i)
                    s = F_SLOTS - 8
                    f_gate(s, F_CHUNKS, n=HALF)
                    f_turn(F_CHUNKS - 1)
                    f_up(s + 2, F_CHUNKS, n=HALF)
                    f_down(s + 4, F_CHUNKS - 1)
                    f_turn(F_CHUNKS, n=HALF // P)
                    f_down(s + 6, F_CHUNKS, k=HALF // P)
                    continue

                for t in range(TT):
                    for k in range(KD):
                        for part_, h in enumerate((hhi, hlo)):
                            m = mm(ps[:, 0, t * NE:(t + 1) * NE], h[:, k, t * P:(t + 1) * P].bitcast(F32),
                                   par("router", k * NE, NE), start=k == 0 and part_ == 0, stop=k == KD - 1 and part_ == 1)
                m.then_inc(lg_mm, 1)
                pe.wait_ge(sel_ok, 1)
                mm(ps[:, 1, 0:NE], tri, rt[:, 0, :])
                mm(ps[:, 1, NE:2 * NE], tri, rt[:, 1, :], stop=False)
                mm(ps[:, 1, NE:2 * NE], ones, rt[:, 0, :], start=False)
                mm(ps[:, 1, 2 * NE:3 * NE], ones, rt[:, 0, :], stop=False)
                mm(ps[:, 1, 2 * NE:3 * NE], ones, rt[:, 1, :], start=False).then_inc(cnt_mm, 1)

                def e_gate(s, n, r):
                    pe.wait_ge(silu, n + F_TILES)
                    for h in range(2):
                        product(1, "B", s + h, r, (0,), (hhi, hlo), KH * h, h == 0, h == 1)

                def e_up(s, n, r):
                    pe.wait_ge(a_ok, n + F_TILES)
                    for h in range(2):
                        product(1, "B", s + h, r, (1,), (hhi, hlo), KH * h, h == 0, h == 1)

                def e_turn(n, d):
                    pe.wait_ge(a_ok, n + (F_TILES + 1))
                    pe.wait_ge(a_lo, n + F_TILES)
                    pe.wait_ge(d_out, d)
                    for k in range(4):
                        m = turn(ps[:, 2, k * P:(k + 1) * P], act_sb[:, 0, k * P:(k + 1) * P])
                    m.then_inc(a_t, 1)

                def e_down(s, n, d, r):
                    pe.wait_ge(a_lo, n + (F_TILES + 1))
                    pe.wait_ge(d_out, d)
                    for h in range(2):
                        product(1, "B", s + h, r, (3 + h,), (ahi, alo), 0, True, True)

                def gather(n):
                    pe.wait_ge(pick_ok, n + 1)
                    for k in range(KD):
                        for t in range(TT):
                            m = mm(ps[:, 5 + k // 4, k % 4 * P:(k % 4 + 1) * P], w1t[:, t, k * P:(k + 1) * P],
                                   pick[:, t, :], start=t == 0, stop=t == 1)
                    m.then_inc(gather_mm, 1)

                pe.wait_ge(route_ok, 1)
                items = pe.value_load(eid[0:1, 15:16], min_val=NE, max_val=ITEMS)
                gather(0)
                with pe.Fori(0, items) as j:
                    n0, d0 = j * E_CHUNKS, j * E_SUMS + F_SUMS
                    pe.wait_ge(gt_lo, j + 1)
                    e_gate(0, n0, n0)
                    pe.wait_ge(d_out, d0)
                    for t in range(TT):
                        m = turn(ps[:, 7, t * P:(t + 1) * P], pickg[:, t, :])
                    m.then_inc(spread_t, 1)
                    e_up(2, n0, n0)
                    with pe.Fori(0, E_CHUNKS - 1) as i:
                        e_gate(4, n0 + i + 1, n0 + i)
                        e_turn(n0 + i, d0)
                        e_up(6, n0 + i + 1, n0 + i)
                        e_down(8, n0 + i, d0 + i * 2, n0 + i)
                    e_turn(n0 + (E_CHUNKS - 1), d0)
                    gather(j + 1)
                    e_down(E_SLOTS - 2, n0 + (E_CHUNKS - 1), d0 + 2 * (E_CHUNKS - 1), n0)
                    pe.wait_ge(d_out, d0 + 2 * E_CHUNKS)
                    pe.wait_ge(spread_sb, j + 1)
                    for n, bank in enumerate((7, 3, 4, 2)):
                        mm(ps[:, bank, :], spread[:, n // 2 * P:(n // 2 + 1) * P],
                           yacc[:, n % 2 * C:(n % 2 + 1) * C]).then_inc(scat_mm, 1)

        @block.scalar
        def _(act):
            def turned_hi(turn_no, done, dcount, scale):
                for b in range(4):
                    act.wait_ge(done, dcount + b + 1)
                    for kk in range(2):
                        k = 2 * b + kk
                        m = nc.scalar.activation(hhi[:, k, :], ps[:, 4 + b, kk * S:(kk + 1) * S], ACT.Copy,
                                                 scale=scale(k)) if scale else \
                            nc.scalar.activation(hhi[:, k, :], ps[:, 4 + b, kk * S:(kk + 1) * S], ACT.Copy)
                    m.then_inc(ht_hi, 1)

            act.wait_ge(consts_in, 32)
            for layer in range(DEPTH):
                L = layer + 1
                turned_hi(3 * layer, ht_turned, 8 * layer, lambda k: par("norm1", layer * KD + k))
                for s in range(4):
                    hi_of(act, layer, "A", s)
                act.wait_ge(conv_y, L)
                nc.scalar.activation(w4b[:, :, :], w4b[:, :, :], ACT.Silu).then_inc(conv_act, 1)
                for s in range(4, 6):
                    hi_of(act, layer, "A", s)
                act.wait_ge(row_abs, L)
                nc.scalar.activation(rowt[:, 2, :], rowt[:, 3, :], ACT.Exp, scale=-1.0).then_inc(row_exp, 1)
                act.wait_ge(row_exp, L)
                nc.scalar.activation(rowt[:, 3, :], rowt[:, 2, :], ACT.Ln, bias=ones[0:MH, 0:1]).then_inc(row_ln, 1)
                with act.Fori(0, N_LOOP // 2 - 1) as i:
                    for s in range(6, 10):
                        hi_of(act, layer, "A", s, i)

                def silu_rg():
                    act.wait_ge(z_out, layer * Q_G + Z_DQ // C)
                    nc.scalar.activation(z[:, :, Z_RG:Z_DQ], z[:, :, Z_RG:Z_DQ], ACT.Silu).then_inc(rg_act, 1)

                def da_squares():
                    act.wait_ge(z_out, layer * Q_G + Z_DV // C)
                    act.wait_ge(rows_ok, L)
                    nc.scalar.activation(w2[:, :], z[:, 0, Z_DQ:Z_DV], ACT.Square)
                    nc.scalar.activation(w1[:, 0:BLK * 4], z[:, 1, Z_DQ:Z_DV], ACT.Square).then_inc(dsq, 1)

                def col_exp_():
                    act.wait_ge(col_sb, L)
                    nc.scalar.activation(emcol, emcol, ACT.Exp).then_inc(col_exp, 1)

                def ret_turned():
                    act.wait_ge(rqk_t, L)
                    act.wait_ge(dsum, L)
                    for b in range(4):
                        m = nc.scalar.activation(qk[:, 2 * b:2 * b + 2, :],
                                                 ps[:, 4 + b, :].rearrange("p (c s) -> p c s", c=2), ACT.Copy)
                    m.then_inc(rqk_sb, 1)

                def ret_squares():
                    act.wait_ge(rpv_mm, L)
                    for t in range(TT):
                        m = nc.scalar.activation(big2[:, t, :], ps[:, 4 + t, :], ACT.Square)
                    m.then_inc(rpv_sq, 1)

                def da_turned(g):
                    act.wait_ge(dqk_t, layer * NG + g + 1)
                    for b, w in enumerate(("qn", "kn")):
                        m = nc.scalar.activation(qk[:, 2 * b:2 * b + 2, :],
                                                 ps[:, 4 + b, :].rearrange("p (c s) -> p c s", c=2), ACT.Copy,
                                                 scale=par(w, layer))
                    m.then_inc(dqk_sb, 1)

                def da_exp(g):
                    act.wait_ge(dsc_sb, layer * NG + g + 1)
                    for h in range(GH):
                        for t, o in enumerate((slice(0, P), slice(P, BLK))):
                            m = nc.scalar.activation(blk2[:, h, o], blk2[:, h, o], ACT.Exp, bias=dneg[:, g, t, h:h + 1],
                                                     accum_out=dl[:, g, t, h:h + 1])
                    m.then_inc(dexp, 1)

                def da_turned_p(g):
                    act.wait_ge(dp_t, layer * NG + g + 1)
                    for h in range(GH):
                        m = nc.scalar.activation(blkz[:, h // 2, h % 2, :], ps[:, 4 + h, 0:BLK], ACT.Copy)
                    m.then_inc(dp_sb, 1)

                def ml_decay():
                    act.wait_ge(mdw_in, L)
                    for h in range(MH):
                        for t, o in enumerate((slice(0, S), slice(S, BLK))):
                            m = nc.scalar.activation(blkm[:, h // 2, h % 2, o], blkm[:, h // 2, h % 2, o], ACT.Exp,
                                                     bias=ccol[:, t, h:h + 1])
                    m.then_inc(mdw, 1)

                def gate_out(q, func=ACT.Copy):
                    wait_used(act, layer, "A", 3 + 2 * q)
                    _, c, n = chunk(q)
                    for t in range(TT):
                        m = nc.scalar.activation(z[:, t, c:c + n], ps[:, pair(q) + t, 0:n], func)
                    m.then_inc(g_out, 1)

                def gate_sigmoids():
                    act.wait_ge(g_out, layer * N_G + N_G - 2)
                    v = z[:, :, Z_G:Z_G + (N_G - 2) * C]
                    nc.scalar.activation(v, v, ACT.Sigmoid).then_inc(sig_ok, 1)

                def da_logs():
                    act.wait_ge(dexp, L * NG)
                    nc.scalar.activation(dco[:, :, :, :], dl[:, :, :, :], ACT.Ln).then_inc(dln, 1)

                def da_weights():
                    act.wait_ge(dlse, L)
                    nc.scalar.activation(dco[:, :, :, :], dco[:, :, :, :], ACT.Exp).then_inc(dwt, 1)

                def ml_squares():
                    act.wait_ge(mh_sb, L)
                    nc.scalar.activation(w1[:, 0:TT * 512], big2[:, :, :].rearrange("p t n -> p (t n)"),
                                         ACT.Square).then_inc(msq, 1)

                def sigmoid_mo():
                    act.wait_ge(z_out, L * Q_G)
                    nc.scalar.activation(z[:, :, Z_MO:Z_G], z[:, :, Z_MO:Z_G], ACT.Sigmoid).then_inc(mo_act, 1)

                silu_rg()
                da_squares()
                behind = {
                    (Q_HALF, 0): (col_exp_,), (Q_HALF, 1): (ret_turned,),
                    (Q_MV, 1): (ret_squares,),
                    (Q_MO, 0): (lambda: da_turned(0),), (Q_MO, 1): (sigmoid_mo, lambda: da_exp(0),),
                    (Q_G, 0): (lambda: da_turned_p(0),), (Q_G, 1): (lambda: da_turned(1), lambda: gate_out(Q_G)),
                    (Q_G + 1, 0): (lambda: da_exp(1),), (Q_G + 1, 1): (lambda: da_turned_p(1), lambda: gate_out(Q_G + 1)),
                    (Q_G + 2, 0): (lambda: da_turned(2),), (Q_G + 2, 1): (lambda: da_exp(2), lambda: gate_out(Q_G + 2)),
                    (Q_G + 3, 0): (lambda: da_turned_p(2),), (Q_G + 3, 1): (ml_decay, da_logs, lambda: gate_out(Q_G + 3)),
                    (Q_G + 4, 0): (da_weights,),
                    (Q_G + 4, 1): (lambda: gate_out(Q_G + 4, ACT.Sigmoid), gate_sigmoids),
                    (Q_G + 5, 1): (lambda: gate_out(Q_G + 5, ACT.Sigmoid),),
                }
                hi_of(act, layer, "A", 2 + 2 * Q_HALF)
                for q in range(Q_HALF, N_Q):
                    for h in range(2):
                        hi_of(act, layer, "A", 3 + 2 * q + h)
                        for step in behind.get((q, h), ()):
                            step()
                ml_squares()

                def out_hi(n, bank, dst, k0, scale):
                    act.wait_ge(ot_t, layer * 5 + n + 1)
                    for kk in range(2):
                        src = ps[:, bank, kk * S:(kk + 1) * S]
                        m = nc.scalar.activation(dst[:, k0 + kk, :], src, ACT.Copy, scale=scale(kk)) if scale else \
                            nc.scalar.activation(dst[:, k0 + kk, :], src, ACT.Copy)
                    m.then_inc(ot_hi, 1)
                out_hi(0, 4, hhi, 0, lambda k: par("retn", layer * 4 + k))
                out_hi(1, 5, hhi, 2, lambda k: par("retn", layer * 4 + 2 + k))
                out_hi(2, 6, hhi, 4, None)
                out_hi(3, 7, ahi, 0, lambda k: par("mln", layer * 4 + k))
                out_hi(4, 4, ahi, 2, lambda k: par("mln", layer * 4 + 2 + k))
                for s in range(S_BR + 1, S_BR + 7):
                    hi_of(act, layer, "A", s)
                turned_hi(3 * layer + 1, yt_turned, 4 * layer, None)
                for s in range(S_BR + 7, S_BR + 9):
                    hi_of(act, layer, "A", s)
                if layer == 0:
                    for s in range(2):
                        hi_of(act, 0, "B", s)
                turned_hi(3 * layer + 2, ht_turned, 8 * layer + 4, lambda k: par("norm2", layer * KD + k))

                if layer == 0:
                    def f_silu(s, t_n, r=0, n=C):
                        wait_used(act, 0, "B", s, r)
                        if t_n is not None:
                            act.wait_ge(a_ok, t_n)
                        for t in range(TT):
                            nc.scalar.activation(sil_sb[:, t, 0:n], ps[:, t, 0:n], ACT.Silu).then_inc(silu, 1)

                    def f_hi(t_n, n=4):
                        for t in range(TT):
                            act.wait_ge(a_t, t_n + t + 1)
                            nc.scalar.activation(ahi[:, 0:n, t * P:(t + 1) * P],
                                                 ps[:, 4 + t, 0:n * P].rearrange("p (k c) -> p k c", k=n),
                                                 ACT.Copy).then_inc(a_hi, 1)

                    for s in (2, 3):
                        hi_of(act, 0, "B", s)
                    f_silu(1, None)
                    for s in (4, 5):
                        hi_of(act, 0, "B", s)
                    hi_of(act, 0, "B", 6)
                    f_silu(5, 2)
                    f_hi(0)
                    for s in (7, 8, 9):
                        hi_of(act, 0, "B", s)
                    with act.Fori(0, F_CHUNKS - 2) as i:
                        for s in (10, 11, 12):
                            hi_of(act, 0, "B", s, i)
                        f_silu(11, i * 2 + 4, i)
                        f_hi(i * 2 + 2)
                        for s in (13, 14, 15):
                            hi_of(act, 0, "B", s, i)
                    s0 = F_SLOTS - 8
                    for s in range(3):
                        hi_of(act, 0, "B", s0 + s)
                    f_silu(s0 + 1, 2 * F_CHUNKS, n=HALF)
                    f_hi(2 * F_CHUNKS - 2)
                    for s in range(3, 8):
                        hi_of(act, 0, "B", s0 + s)
                    f_hi(2 * F_CHUNKS, n=HALF // P)
                    continue

                act.wait_ge(lg_d, 1)
                nc.scalar.activation(v12[:, :, 2:3], v12[:, :, 2:3], ACT.Exp).then_inc(lg_e, 1)

                def gathered_hi(n):
                    act.wait_ge(gather_mm, n + 1)
                    for k in range(KD):
                        m = nc.scalar.activation(hhi[:, k, 0:CAP], ps[:, 5 + k // 4, k % 4 * P:(k % 4 + 1) * P], ACT.Copy,
                                                 scale=par("norm2", KD + k))
                    m.then_inc(gt_hi, 1)

                def e_silu(s, n, r):
                    wait_used(act, 1, "B", s, r)
                    act.wait_ge(a_ok, n + F_TILES)
                    nc.scalar.activation(sil_sb[:, 0, :], ps[:, 0, :], ACT.Silu).then_inc(silu, 1)

                def e_hi(n):
                    act.wait_ge(a_t, n + (F_TILES + 1))
                    nc.scalar.activation(ahi[:, :, 0:CAP], ps[:, 2, :].rearrange("p (k c) -> p k c", k=4),
                                         ACT.Copy).then_inc(a_hi, 1)

                act.wait_ge(route_ok, 1)
                items = act.value_load(eid[0:1, 15:16], min_val=NE, max_val=ITEMS)
                with act.Fori(0, items) as j:
                    n0 = j * E_CHUNKS
                    for s in (0, 1):
                        hi_of(act, 1, "B", s, n0)
                    gathered_hi(j)
                    for s in (2, 3):
                        hi_of(act, 1, "B", s, n0)
                    e_silu(1, n0, n0)
                    act.wait_ge(spread_t, j + 1)
                    nc.scalar.activation(spread[:, :], ps[:, 7, 0:S], ACT.Copy).then_inc(spread_sb, 1)
                    with act.Fori(0, E_CHUNKS - 1) as i:
                        for s in (4, 5, 6):
                            hi_of(act, 1, "B", s, n0 + i)
                        e_silu(5, n0 + i + 1, n0 + i)
                        e_hi(n0 + i)
                        for s in (7, 8, 9):
                            hi_of(act, 1, "B", s, n0 + i)
                    for s in (E_SLOTS - 2, E_SLOTS - 1):
                        hi_of(act, 1, "B", s, n0)
                    e_hi(n0 + (E_CHUNKS - 1))

        @block.vector
        def _(dve):
            V = nc.vector
            chained = [0]

            def link(ins):
                chained[0] += 1
                ins.then_inc(dve_chain, 1)
                dve.wait_ge(dve_chain, chained[0])

            def inverse_root(out, total, n):
                width = 1
                for d in out.shape[1:]:
                    width *= d
                v, w = root[:, 0:width], root[:, 64:64 + width]
                if len(out.shape) == 3:
                    v, w = (u.rearrange("p (t n) -> p t n", t=out.shape[1]) for u in (v, w))
                link(V.tensor_scalar(v, total, 1.0 / n, EPS, ALU.mult, ALU.add))
                link(V.tensor_scalar(out.bitcast(I32), v.bitcast(I32), 1, None, ALU.logical_shift_right))
                link(V.tensor_scalar(out.bitcast(I32), out.bitcast(I32), -1.0, float(0x5F3759DF), ALU.mult, ALU.add))
                for _ in range(4):
                    link(V.scalar_tensor_tensor(out=w, in0=out, scalar=-0.5, in1=out, op0=ALU.mult, op1=ALU.mult))
                    link(V.tensor_tensor(w, w, v, ALU.mult))
                    link(V.scalar_tensor_tensor(out=out, in0=w, scalar=1.5, in1=out, op0=ALU.add, op1=ALU.mult))

            def normalise():
                for t in range(TT):
                    link(V.tensor_tensor_reduce(out=w1t[:, t, :], in0=x[:, t, :], in1=x[:, t, :], scale=1.0, scalar=0.0,
                                                op0=ALU.mult, op1=ALU.add, accum_out=ss2[:, t:t + 1]))
                inverse_root(rstd2, ss2, D)
                for t in range(TT):
                    V.tensor_scalar(w1t[:, t, :], x[:, t, :], rstd2[:, t:t + 1], None, ALU.mult).then_inc(tok_ready, 1)

            def minus_hi(out, src, scale, hi):
                if scale is None:
                    return V.tensor_tensor(out, src, hi.bitcast(F32), ALU.subtract)
                return V.scalar_tensor_tensor(out=out, in0=src, scalar=scale, in1=hi.bitcast(F32),
                                              op0=ALU.mult, op1=ALU.subtract)

            def turned_lo(n, scale):
                for b in range(4):
                    dve.wait_ge(ht_hi, 4 * n + b + 1)
                    for kk in range(2):
                        k = 2 * b + kk
                        m = minus_hi(hlo[:, k, :], ps[:, 4 + b, kk * S:(kk + 1) * S], scale and scale(k), hhi[:, k, :])
                    m.then_inc(ht_lo, 1)

            def wide(v, n):
                return v.unsqueeze(len(v.shape)).to_broadcast(list(v.shape) + [n])

            link(V.memset(w4a[:, :, :], 0.0))
            dve.wait_ge(x_in, 16)
            dve.wait_ge(consts_in, 32)
            for layer in range(DEPTH):
                L = layer + 1
                normalise()
                turned_lo(3 * layer, lambda k: par("norm1", layer * KD + k))

                wait_used(dve, layer, "A", 1)
                V.tensor_copy(w4a[:, :, TAPS - 1:], ps[:, 0:4, 0:S]).then_inc(conv_pad, 1)
                dve.wait_ge(conv_pad, L)
                for j in range(TAPS):
                    for c in range(4):
                        tap = par("conv", (layer * 4 + c) * TAPS + j)
                        if j == 0:
                            m = V.tensor_scalar(w4b[:, c, :], w4a[:, c, 0:S], tap, None, ALU.mult)
                        else:
                            m = V.scalar_tensor_tensor(out=w4b[:, c, :], in0=w4a[:, c, j:j + S], scalar=tap,
                                                       in1=w4b[:, c, :], op0=ALU.mult, op1=ALU.add)
                    if j < TAPS - 1:
                        link(m)
                m.then_inc(conv_y, 1)
                dve.wait_ge(z8_mm, L)
                V.tensor_copy(z8, ps[:, 4, 0:16].rearrange("p (t n) -> p t n", t=TT)).then_inc(z8_sb, 1)

                def z_copy(q, r=0):
                    wait_used(dve, layer, "A", 3 + 2 * q, r)
                    _, c, n = chunk(q)
                    dst = z[:, :, c:c + n] if isinstance(r, int) else z[:, :, bass.ds(r * (2 * C) + c, n)]
                    V.tensor_copy(dst, ps[:, pair(q):pair(q) + 2, 0:n]).then_inc(z_out, 1)
                z_copy(0)

                dve.wait_ge(row_t, L)
                R = lambda n: rowt[:, n, :]
                V.tensor_scalar(R(0), ps[0:MH, 5, 0:S], par("ib", layer)[0:MH], None, ALU.add)
                link(V.tensor_scalar(R(1), ps[0:MH, 5, S:2 * S], par("fb", layer)[0:MH], None, ALU.add))
                V.scalar_tensor_tensor(out=R(3), in0=R(1), scalar=-1.0, in1=R(1), op0=ALU.mult, op1=ALU.max).then_inc(row_abs, 1)
                dve.wait_ge(row_exp, L)
                link(V.tensor_scalar(R(4), R(2), 1.0, None, ALU.add))
                link(V.tensor_scalar(R(5), R(4), 1.0, None, ALU.subtract))
                link(V.tensor_tensor(R(5), R(2), R(5), ALU.subtract))
                link(V.reciprocal(R(4), R(4)))
                link(V.tensor_tensor(R(5), R(5), R(4), ALU.mult))
                dve.wait_ge(row_ln, L)
                link(V.tensor_tensor(R(3), R(3), R(5), ALU.add))
                V.scalar_tensor_tensor(out=R(1), in0=R(1), scalar=0.0, in1=R(3), op0=ALU.min, op1=ALU.subtract)
                link(V.memset(R(5), 1.0))
                link(V.tensor_tensor_scan(R(4), R(5), R(1), 0.0, ALU.mult, ALU.add))
                link(V.tensor_tensor(rows[:, 0, :], R(0), R(4), ALU.subtract))
                link(V.tensor_tensor_scan(R(2), rows[:, 0, :], rows[:, 0, :], 0.0, ALU.max, ALU.max))
                V.tensor_scalar(rows[:, 1, :], R(2), -1.0, None, ALU.mult)
                V.scalar_tensor_tensor(out=rows[:, 2, :], in0=R(4), scalar=-1.0, in1=R(2), op0=ALU.mult,
                                       op1=ALU.subtract).then_inc(rows_ok, 1)
                z_copy(1)
                with dve.Fori(0, N_LOOP // 2 - 1) as i:
                    for q in (2, 3):
                        z_copy(q, i)

                dve.wait_ge(dsq, L)
                V.tensor_reduce(dss[:, 0, :], w2[:, :].rearrange("p (h d) -> p h d", d=DH), AX, ALU.add)
                V.tensor_reduce(dss[:, 1, :], w1[:, 0:BLK * 4].rearrange("p (h d) -> p h d", d=DH), AX,
                                ALU.add).then_inc(dsum, 1)
                dve.wait_ge(dsum, L)
                inverse_root(drs, dss, DH)
                for t in range(TT):
                    v = z[:, t, 0:Z_RV].rearrange("p (h f d) -> p h f d", f=2, d=64)
                    x1, x2 = v[:, :, 0, :], v[:, :, 1, :]
                    cos, sin = (rot[:, t, f, :].unsqueeze(1).to_broadcast([P, 8, 64]) for f in range(2))
                    A, B, Cc = (w2[:, n * 512:(n + 1) * 512].rearrange("p (h d) -> p h d", d=64) for n in range(3))
                    V.tensor_tensor(A, x1, cos, ALU.mult)
                    V.tensor_tensor(Cc, x1, sin, ALU.mult)
                    link(V.tensor_tensor(B, x2, sin, ALU.mult))
                    link(V.tensor_tensor(x1, A, B, ALU.subtract))
                    link(V.tensor_tensor(A, x2, cos, ALU.mult))
                    m = V.tensor_tensor(x2, Cc, A, ALU.add)
                    if t == 0:
                        link(m)
                m.then_inc(rotated, 1)
                dve.wait_ge(col_t, L)
                V.tensor_copy(st[:, 20:36], ps[:, 7, 0:16]).then_inc(col_sb, 1)
                for t in range(TT):
                    v = z[:, t, Z_DQ:Z_DV].rearrange("p (h d) -> p h d", d=DH)
                    m = V.tensor_tensor(v, v, wide(drs[:, t, :], DH), ALU.mult)
                m.then_inc(dn_ok, 1)
                z_copy(Q_HALF)

                dve.wait_ge(rsc_mm, L)
                V.tensor_tensor(blk2, ps[:, 4:8, 0:BLK], decay, ALU.mult).then_inc(rsc_sb, 1)
                z_copy(Q_MV)
                dve.wait_ge(rpv_sq, L)
                link(V.tensor_reduce(rss, big2.rearrange("p t (h d) -> p (t h) d", d=RDV), AX, ALU.add))
                inverse_root(rrs, rss, RDV)
                link(V.tensor_tensor(big2.rearrange("p t (h d) -> p t h d", d=RDV),
                                     ps[:, 4:6, :].rearrange("p t (h d) -> p t h d", d=RDV),
                                     wide(rrs.rearrange("p (t h) -> p t h", t=TT), RDV), ALU.mult))
                dve.wait_ge(rg_act, L)
                V.tensor_tensor(z[:, :, Z_RG:Z_DQ], big2, z[:, :, Z_RG:Z_DQ], ALU.mult).then_inc(ro_out, 1)

                def da_masked(g):
                    dve.wait_ge(dsc_mm, layer * NG + g + 1)
                    link(V.scalar_tensor_tensor(out=blk2, in0=ps[:, 4:8, 0:BLK], scalar=DH ** -0.5,
                                                in1=damask[:, g, :].unsqueeze(1).to_broadcast([P, GH, BLK]),
                                                op0=ALU.mult, op1=ALU.add))
                    V.tensor_reduce(dneg[:, g, 0, :], blk2[:, :, 0:P], AX, ALU.max)
                    link(V.tensor_reduce(dneg[:, g, 1, :], blk2[:, :, P:BLK], AX, ALU.max))
                    V.tensor_scalar(dneg[:, g, :, :], dneg[:, g, :, :], -1.0, None, ALU.mult).then_inc(dsc_sb, 1)

                def da_keep(g):
                    dve.wait_ge(dpv_mm, layer * NG + g + 1)
                    V.tensor_copy(z[:, :, Z_DQ + g * GH * DH:Z_DQ + (g + 1) * GH * DH],
                                  ps[:, 6:8, 0:GH * DH]).then_inc(dpv_sb, 1)

                z_copy(Q_MO)
                da_masked(0)
                da_keep(0)
                da_masked(1)
                da_keep(1)
                da_masked(2)
                da_keep(2)
                dve.wait_ge(msel_mm, L)
                sp_ = ps[:, 4:6, :].rearrange("p a (b s) -> p a b s", b=2)
                m_ = lambda o: mlmask[:, o].unsqueeze(1).unsqueeze(1)
                for a_ in range(2):
                    V.tensor_tensor(blkm[:, a_, :, 0:S], sp_[:, a_], mlmask[:, 0:S].unsqueeze(1).to_broadcast([P, 2, S]),
                                    ALU.add)
                    m = V.tensor_tensor(blkm[:, a_, :, S:BLK], sp_[:, a_, :, P:S],
                                        mlmask[:, S:BLK].unsqueeze(1).to_broadcast([P, 2, P]), ALU.add)
                m.then_inc(mdw_in, 1)
                dve.wait_ge(dln, L)
                G = lambda v, g: v[:, g, :, :].rearrange("p t h -> p (t h)")
                over = dtmp.unsqueeze(1).to_broadcast([P, NG, 8])
                flat = lambda v: v.rearrange("p g t h -> p g (t h)")
                link(V.tensor_tensor(flat(dco), flat(dco), flat(dneg), ALU.subtract))
                link(V.tensor_tensor(dtmp, G(dco, 0), G(dco, 1), ALU.max))
                link(V.tensor_tensor(dtmp, dtmp, G(dco, 2), ALU.max))
                V.tensor_tensor(flat(dco), flat(dco), over, ALU.subtract).then_inc(dlse, 1)
                dve.wait_ge(dwt, L)
                link(V.tensor_tensor(dtmp, G(dco, 0), G(dco, 1), ALU.add))
                link(V.tensor_tensor(dtmp, dtmp, G(dco, 2), ALU.add))
                link(V.tensor_tensor(flat(dl), flat(dl), over, ALU.mult))
                link(V.reciprocal(flat(dl), flat(dl)))
                link(V.tensor_tensor(flat(dco), flat(dco), flat(dl), ALU.mult))
                og = [z[:, :, Z_DQ + g * GH * DH:Z_DQ + (g + 1) * GH * DH].rearrange("p t (h d) -> p t h d", d=DH)
                      for g in range(NG)]
                for g in range(NG):
                    m = V.tensor_tensor(og[g], og[g], wide(dco[:, g, :, :], DH), ALU.mult)
                link(m)
                link(V.tensor_tensor(og[0], og[0], og[1], ALU.add))
                V.tensor_tensor(og[0], og[0], og[2], ALU.add).then_inc(do_out, 1)
                dve.wait_ge(msc_mm, L)
                dve.wait_ge(mdw, L)
                for a_ in range(2):
                    m = V.scalar_tensor_tensor(out=blkm[:, a_], in0=ps[:, 4 + 2 * a_:6 + 2 * a_, 0:BLK], scalar=MDK ** -0.5,
                                               in1=blkm[:, a_], op0=ALU.mult, op1=ALU.mult)
                m.then_inc(msc_sb, 1)
                dve.wait_ge(mpv_mm, L)
                dve.wait_ge(col_exp, L)
                link(V.tensor_copy(mden, ps[:, 6, 0:8]))
                link(V.scalar_tensor_tensor(out=mden, in0=mden, scalar=-1.0, in1=mden, op0=ALU.mult, op1=ALU.max))
                link(V.tensor_tensor(mden, mden, emcol, ALU.max))
                link(V.reciprocal(mden, mden))
                V.tensor_tensor(big2.rearrange("p t (h d) -> p t h d", d=MDV),
                                ps[:, 4:6, :].rearrange("p t (h d) -> p t h d", d=MDV),
                                wide(mden.rearrange("p (t h) -> p t h", t=TT), MDV), ALU.mult).then_inc(mh_sb, 1)
                dve.wait_ge(msq, L)
                link(V.tensor_reduce(mss, w1[:, 0:TT * 512].rearrange("p (n d) -> p n d", d=MDV), AX, ALU.add))
                inverse_root(mrs, mss, MDV)
                big2h = big2.rearrange("p t (h d) -> p (t h) d", d=MDV)
                link(V.tensor_tensor(big2h, big2h, wide(mrs, MDV), ALU.mult))
                dve.wait_ge(mo_act, L)
                V.tensor_tensor(z[:, :, Z_MO:Z_G], big2, z[:, :, Z_MO:Z_G], ALU.mult).then_inc(mo_out, 1)

                def out_lo(n, bank, hi, lo, k0, scale):
                    dve.wait_ge(ot_hi, layer * 5 + n + 1)
                    for kk in range(2):
                        m = minus_hi(lo[:, k0 + kk, :], ps[:, bank, kk * S:(kk + 1) * S], scale and scale(kk),
                                     hi[:, k0 + kk, :])
                    m.then_inc(ot_lo, 1)
                out_lo(0, 4, hhi, hlo, 0, lambda k: par("retn", layer * 4 + k))
                out_lo(1, 5, hhi, hlo, 2, lambda k: par("retn", layer * 4 + 2 + k))
                out_lo(2, 6, hhi, hlo, 4, None)
                out_lo(3, 7, ahi, alo, 0, lambda k: par("mln", layer * 4 + k))
                out_lo(4, 4, ahi, alo, 2, lambda k: par("mln", layer * 4 + 2 + k))
                dve.wait_ge(g_out, L * N_G)
                dve.wait_ge(sig_ok, L)
                for n in range(6):
                    if n == 2:
                        dve.wait_ge(br_half, L)
                    else:
                        wait_used(dve, layer, "A", S_BR + (0, 1, 0, 2, 3, 4)[n])
                    v = z[:, :, Z_G + n * C:Z_G + (n + 1) * C]
                    V.tensor_tensor(v, v, ps[:, 2 * (n % 2):2 * (n % 2) + 2, :], ALU.mult).then_inc(br_out, 1)
                dve.wait_ge(br_out, 6 * L)
                part_ = lambda n, t: z[:, t, Z_G + n * D:Z_G + (n + 1) * D]
                for t in range(TT):
                    m = V.tensor_tensor(part_(0, t), part_(0, t), part_(1, t), ALU.add)
                link(m)
                for t in range(TT):
                    V.tensor_tensor(part_(0, t), part_(0, t), part_(2, t), ALU.add).then_inc(tok_ready, 1)
                turned_lo(3 * layer + 1, None)
                for half in range(2):
                    wait_used(dve, layer, "A", S_BR + 6 + 2 * half)
                    v = x[:, :, half * C:(half + 1) * C]
                    m = V.tensor_tensor(v, v, ps[:, 2 * half:2 * half + 2, :], ALU.add)
                link(m)
                normalise()
                turned_lo(3 * layer + 2, lambda k: par("norm2", layer * KD + k))

                if layer == 0:
                    def lo_(s, r=0):
                        lo_of(dve, 0, "B", s, r)

                    def f_mult(s, i, r=0, n=C):
                        wait_used(dve, 0, "B", s, r)
                        dve.wait_ge(silu, i * 2 + 2)
                        if s > 3:
                            dve.wait_ge(a_t, i * 2)
                        for t in range(TT):
                            V.tensor_tensor(act_sb[:, t, 0:n], sil_sb[:, t, 0:n], ps[:, 2 + t, 0:n],
                                            ALU.mult).then_inc(a_ok, 1)

                    def f_lo(i, n=4):
                        for t in range(TT):
                            dve.wait_ge(a_hi, i * 2 + t + 1)
                            minus_hi(alo[:, 0:n, t * P:(t + 1) * P],
                                     ps[:, 4 + t, 0:n * P].rearrange("p (k c) -> p k c", k=n), None,
                                     ahi[:, 0:n, t * P:(t + 1) * P]).then_inc(a_lo, 1)

                    def f_sum(s, half, r=0):
                        wait_used(dve, 0, "B", s, r)
                        for t in range(TT):
                            v = x[:, t, half * C:(half + 1) * C]
                            V.tensor_tensor(v, v, ps[:, 6 - 2 * half + t, :], ALU.add).then_inc(d_out, 1)

                    def f_round(s, i, r=0, before=True, n=C):
                        lo_(s, r)
                        if before:
                            f_sum(s - 1, 1, r)
                        lo_(s + 2, r)
                        f_lo(i - 1)
                        lo_(s + 3, r)
                        lo_(s + 5, r)
                        f_mult(s + 3, i, r, n)
                        f_sum(s + 4, 0, r)

                    for s in (0, 1, 3):
                        lo_(s)
                    f_mult(3, 0)
                    f_round(4, 1, before=False)
                    with dve.Fori(0, F_CHUNKS - 2) as i:
                        f_round(10, i + 2, i)
                    s0 = F_SLOTS - 8
                    f_round(s0, F_CHUNKS, n=HALF)
                    lo_(s0 + 6)
                    f_sum(s0 + 5, 1)
                    f_lo(F_CHUNKS, HALF // P)
                    f_sum(s0 + 6, 0)
                    f_sum(s0 + 7, 1)
                    dve.wait_ge(d_out, F_SUMS)
                    continue

                dve.wait_ge(lg_mm, 1)
                link(V.tensor_tensor(lg, ps[:, 0, 0:16].rearrange("p (t n) -> p t n", t=TT),
                                     par("rb", 0, NE).unsqueeze(1).to_broadcast([P, TT, NE]), ALU.add))

                def first_max(src, v, m, cum):
                    link(V.tensor_reduce(v, src, AX, ALU.max))
                    link(V.tensor_tensor(m, src, v.to_broadcast([P, TT, NE]), ALU.is_equal))
                    for t in range(TT):
                        c = V.tensor_tensor_scan(cum[:, t, :], ones[:, 0:NE], m[:, t, :], 0.0, ALU.mult, ALU.add)
                    link(c)
                    link(V.scalar_tensor_tensor(out=m, in0=cum, scalar=1.0, in1=m, op0=ALU.is_equal, op1=ALU.mult))

                first_max(lg, v12[:, :, 0:1], m1, rt)
                link(V.scalar_tensor_tensor(out=rtmp, in0=m1, scalar=-1e30, in1=lg, op0=ALU.mult, op1=ALU.add))
                first_max(rtmp, v12[:, :, 1:2], m2, rt)
                V.tensor_tensor(v12[:, :, 2:3], v12[:, :, 1:2], v12[:, :, 0:1], ALU.subtract).then_inc(lg_d, 1)
                V.tensor_tensor(rt, m1, m2, ALU.add).then_inc(sel_ok, 1)
                V.memset(posx[:, :, :], -1000.0)
                link(V.memset(gatex[:, :, :], 0.0))
                dve.wait_ge(lg_e, 1)
                link(V.tensor_scalar(v12[:, :, 3:4], v12[:, :, 2:3], 1.0, None, ALU.add))
                link(V.reciprocal(v12[:, :, 3:4], v12[:, :, 3:4]))
                link(V.tensor_tensor(v12[:, :, 2:3], v12[:, :, 2:3], v12[:, :, 3:4], ALU.mult))
                V.tensor_tensor(m1, m1, v12[:, :, 3:4].to_broadcast([P, TT, NE]), ALU.mult)
                link(V.tensor_tensor(m2, m2, v12[:, :, 2:3].to_broadcast([P, TT, NE]), ALU.mult))
                link(V.tensor_tensor(gatex[:, :, 0:NE], m1, m2, ALU.add))
                dve.wait_ge(cnt_mm, 1)
                dve.wait_ge(sel_ok, 1)
                link(V.scalar_tensor_tensor(out=posx[:, :, 0:NE], in0=ps[:, 1, 0:16].rearrange("p (t n) -> p t n", t=TT),
                                            scalar=1000.0, in1=rt, op0=ALU.add, op1=ALU.mult))
                link(V.tensor_scalar(posx[:, :, 0:NE], posx[:, :, 0:NE], 1000.0, None, ALU.subtract))
                link(V.tensor_scalar(big, ps[:, 1, 16:24], float(CAP), None, ALU.is_gt))
                link(V.tensor_tensor_scan(rank, ones[:, 0:NE], big, 0.0, ALU.mult, ALU.add))
                link(V.memset(eidf, 0.0))
                V.tensor_copy(eidf[:, 0:NE], iota[:, 0:NE])
                link(V.tensor_scalar(eidf[:, 15:16], rank[:, NE - 1:NE], float(NE), None, ALU.add))
                for n in range(EXTRA):
                    link(V.scalar_tensor_tensor(out=selx, in0=rank, scalar=float(n + 1), in1=big,
                                                op0=ALU.is_equal, op1=ALU.mult))

                    def pick_sum(src, dst):
                        link(V.tensor_tensor_reduce(out=cnt, in0=selx, in1=src, scale=1.0, scalar=0.0, op0=ALU.mult,
                                                    op1=ALU.add, accum_out=dst))
                    pick_sum(iota[:, 0:NE], eidf[:, NE + n:NE + n + 1])
                    for t in range(TT):
                        pick_sum(posx[:, t, 0:NE], posx[:, t, NE + n:NE + n + 1])
                        pick_sum(gatex[:, t, 0:NE], gatex[:, t, NE + n:NE + n + 1])
                link(V.tensor_scalar(posx[:, :, NE:NE + EXTRA], posx[:, :, NE:NE + EXTRA], float(CAP), None, ALU.subtract))
                V.memset(yacc, 0.0).then_inc(y_zero, 1)
                V.tensor_copy(eid[:, :], eidf[0:1, :]).then_inc(route_ok, 1)

                def picks(n):
                    for t in range(TT):
                        p_ = posx[:, t, bass.ds(n, 1)]
                        V.tensor_scalar(pickg[:, t, :], iota, p_, gatex[:, t, bass.ds(n, 1)], ALU.is_equal, ALU.mult)
                        m = V.tensor_scalar(pick[:, t, :], iota, p_, None, ALU.is_equal)
                    m.then_inc(pick_ok, 1)

                def e_mult(s, n, r):
                    wait_used(dve, 1, "B", s, r)
                    dve.wait_ge(silu, n + (F_TILES + 1))
                    dve.wait_ge(a_t, n + F_TILES)
                    V.tensor_tensor(act_sb[:, 0, :], sil_sb[:, 0, :], ps[:, 1, :], ALU.mult).then_inc(a_ok, 1)

                def e_lo(n):
                    dve.wait_ge(a_hi, n + (F_TILES + 1))
                    minus_hi(alo[:, :, 0:CAP], ps[:, 2, :].rearrange("p (k c) -> p k c", k=4), None,
                             ahi[:, :, 0:CAP]).then_inc(a_lo, 1)

                def e_sum(s, half, r):
                    wait_used(dve, 1, "B", s, r)
                    v = yacc[:, half * C:(half + 1) * C]
                    V.tensor_tensor(v, v, ps[:, 3 + half, :], ALU.add).then_inc(d_out, 1)

                def e_round(s, n, r, before=True):
                    lo_of(dve, 1, "B", s, r)
                    if before:
                        e_sum(s - 1, 1, r)
                    lo_of(dve, 1, "B", s + 2, r)
                    e_lo(n - 1)
                    lo_of(dve, 1, "B", s + 3, r)
                    lo_of(dve, 1, "B", s + 5, r)
                    e_mult(s + 3, n, r)
                    e_sum(s + 4, 0, r)

                picks(0)
                dve.wait_ge(route_ok, 1)
                items = dve.value_load(eid[0:1, 15:16], min_val=NE, max_val=ITEMS)
                with dve.Fori(0, items) as j:
                    n0, d0 = j * E_CHUNKS, j * E_SUMS + F_SUMS
                    lo_of(dve, 1, "B", 0, n0)
                    lo_of(dve, 1, "B", 1, n0)
                    dve.wait_ge(gt_hi, j + 1)
                    for k in range(KD):
                        m = minus_hi(hlo[:, k, 0:CAP], ps[:, 5 + k // 4, k % 4 * P:(k % 4 + 1) * P],
                                     par("norm2", KD + k), hhi[:, k, 0:CAP])
                    m.then_inc(gt_lo, 1)
                    lo_of(dve, 1, "B", 3, n0)
                    e_mult(3, n0, n0)
                    dve.wait_ge(spread_t, j + 1)
                    picks(j + 1)
                    dve.wait_ge(y_zero, j + 1)
                    e_round(4, n0 + 1, n0, before=False)
                    with dve.Fori(0, E_CHUNKS - 2) as i:
                        e_round(10, n0 + i + 2, n0 + i)
                    lo_of(dve, 1, "B", E_SLOTS - 2, n0)
                    e_sum(E_SLOTS - 3, 1, n0)
                    e_lo(n0 + (E_CHUNKS - 1))
                    e_sum(E_SLOTS - 2, 0, n0)
                    e_sum(E_SLOTS - 1, 1, n0)
                    for n, bank in enumerate((7, 3, 4, 2)):
                        dve.wait_ge(scat_mm, j * 4 + n + 1)
                        v = x[:, n // 2, n % 2 * C:(n % 2 + 1) * C]
                        V.tensor_tensor(v, v, ps[:, bank, :], ALU.add).then_inc(d_out, 1)
                    V.memset(yacc, 0.0).then_inc(y_zero, 1)
                dve.wait_ge(y_zero, items + 1)
                V.memset(cnt, 0.0).then_inc(x_end, 1)


def _constants():
    f = np.float32
    c = np.zeros((P, N_CONST), f)

    def put(name, v):
        lo, hi = CONST[name]
        c[:v.shape[0], lo:hi] = v.reshape(v.shape[0], -1)
    put("ident", np.eye(P, dtype=f))
    half = RDV // 2
    inv = np.power(f(10000.0), -np.arange(half, dtype=f) / f(half)).astype(f)
    ang = (np.arange(S, dtype=f)[:, None] * inv[None, :]).astype(f).astype(np.float64)
    rot = np.stack([np.cos(ang), np.sin(ang)], 1).astype(f)
    put("rot", rot.reshape(TT, P, 2, half).transpose(1, 0, 2, 3))
    i = np.arange(S)
    rel = i[None, :] - i[:, None]
    log_gamma = np.log1p(-np.exp2(-5.0 - np.arange(RH)))
    decay = np.where(rel >= 0, np.exp(log_gamma[:, None, None] * np.maximum(rel, 0)), 0.0) * RDV ** -0.5
    put("decay", np.concatenate([decay[:, :P, :], decay[:, P:, P:]], 2).transpose(1, 0, 2).astype(f))
    ok = np.stack([(rel.T >= 0) & (rel.T % d == 0) & (rel.T <= w) for w, d in GROUPS])
    mask = np.where(ok, 0.0, -1e30).astype(f)
    put("damask", np.concatenate([mask[:, :P, :P], mask[:, P:, :]], 2).transpose(1, 0, 2))
    ml = np.where(rel >= 0, 0.0, -1e30).astype(f)
    put("mlmask", np.concatenate([ml[:P, :], ml[P:, P:]], 1))
    put("tri", np.triu(np.ones((P, P), f), 1))
    put("ones", np.ones((P, P), f))
    put("iota", np.broadcast_to(np.arange(P, dtype=f), (P, P)))
    put("sel", np.repeat(np.eye(MH, dtype=f), P, 1))
    return c


def _small(w):
    s = np.zeros((P, N_SMALL), np.float32)

    def put(name, v):
        lo, hi = SMALL[name]
        s[:v.shape[0], lo:hi] = v.reshape(v.shape[0], -1)
    tiles = lambda v: v.reshape(DEPTH, -1, P).transpose(2, 0, 1)
    for name, v in (("norm1", "norm1_w"), ("norm2", "norm2_w"), ("retn", "ret_norm_w"), ("mln", "ml_norm_w")):
        put(name, tiles(w[v]))
    for name, v in (("qn", "da_q_norm_w"), ("kn", "da_k_norm_w")):
        put(name, np.concatenate([w[v], w[v]], 1).T)
    put("conv", w["ml_conv_w"].reshape(DEPTH, TAPS, 4, P).transpose(3, 0, 2, 1))
    put("ib", w["ml_i_bias"].T)
    put("fb", w["ml_f_bias"].T)
    put("rb", np.broadcast_to(w["moe_b_router"], (P, NE)))
    put("gates", w["w_in"][:, :, IN_GATES:IN_G].reshape(DEPTH, KD, P, 8).transpose(2, 0, 1, 3))
    put("router", w["moe_w_router"][0].reshape(KD, P, NE).transpose(1, 0, 2))
    return s


_WHOLE = ["x", "w_in", "w_br_ret", "w_br_da", "w_br_ml", "w_out", "ffn_w_gate", "ffn_w_up", "ffn_w_down",
          "moe_w_gate", "moe_w_up", "moe_w_down"]


def kernel(**inputs):
    from concourse import bacc
    from concourse.bass_utils import run_bass_kernel_spmd

    w = {name: np.ascontiguousarray(v) for name, v in inputs.items()}
    arrays = {name: w[name] for name in _WHOLE}
    arrays["const"], arrays["small"] = _constants(), _small(w)
    nc = bacc.Bacc("TRN2", target_bir_lowering=False, num_devices=1)
    a = {name: nc.dram_tensor(f"in_{name}_dram", v.shape, mybir.dt.from_np(v.dtype), kind="ExternalInput").ap()
         for name, v in arrays.items()}
    a["out"] = nc.dram_tensor("out_dram", w["x"].shape, F32, kind="ExternalOutput").ap()
    build(nc, a)
    r = run_bass_kernel_spmd(nc, [{f"in_{name}_dram": v for name, v in arrays.items()}], core_ids=[0])
    return r.results[0]["out_dram"]
```

```python
from contextlib import ExitStack

import numpy as np
import concourse.bass as bass
from concourse import mybir

F32 = mybir.dt.float32
F32R = mybir.dt.float32r
I32 = mybir.dt.int32
ALU = mybir.AluOpType
ACT = mybir.ActivationFunctionType
AX = mybir.AxisListType.X

P = 128
D = 1024
KD = D // P
S = 256
TT = S // P
DEPTH = 2
EPS = 1e-6
RH, RDV = 4, 128
GROUPS = ((128, 1), (512, 4), (2048, 16))
NG = len(GROUPS)
GH, DH = 4, 64
NH = NG * GH
MH, MDK, MDV = 4, 64, 128
TAPS = 4
FF = 2816
NE, FE = 8, 3584
C = 512
SLOT = 4 * C
KH = KD // 2
BLK = 3 * P

IN_DV_END = 2048 + 3 * NH * DH
IN_QK = IN_DV_END
IN_MV = IN_QK + 2 * MH * MDK
IN_GATES = IN_MV + 2 * MH * MDV
IN_G = IN_GATES + 2 * MH
P_IN = IN_G + 3 * D
Z_RV, Z_RG, Z_DQ = 1024, 1536, 2048
Z_DK = Z_DQ + NH * DH
Z_DV = Z_DK + NH * DH
Z_MV = IN_DV_END
Z_MO = Z_MV + MH * MDV
Z_G = Z_MO + MH * MDV
ZW = Z_G + 3 * D

RING_A, RING_B, RING_L = 2, 6, 3
ROUND = 6
N_LOOP = 8
N_G = 6
A_SLOTS = 2 + 2 * N_LOOP + 6 + 2 * N_G + 2 + 1 + 2 + 4
F_CHUNKS = FF // C
F_SLOTS = 6 * (F_CHUNKS + 1)
E_CHUNKS = FE // C
DVE_SHARE = 0.69
E_SLOTS = 6 * E_CHUNKS
F_TILES = TT * (F_CHUNKS + 1)
F_SUMS = 2 * F_TILES
E_SUMS = 2 * E_CHUNKS + 2 * TT
EXTRA = TT * S // P - 1
ITEMS = NE + EXTRA
CAP = P

CONST = {}
SMALL = {}


def _place(table, parts):
    at = 0
    for name, width in parts:
        table[name] = (at, at + width)
        at += width
    return at


N_CONST = _place(CONST, [("ident", P), ("rot", 2 * TT * 64), ("decay", RH * BLK), ("damask", NG * BLK),
                         ("mlmask", BLK), ("tri", P), ("ones", P), ("iota", P), ("sel", MH * P)])
N_SMALL = _place(SMALL, [("norm1", DEPTH * KD), ("norm2", DEPTH * KD), ("retn", DEPTH * 4), ("mln", DEPTH * 4),
                         ("qn", DEPTH), ("kn", DEPTH), ("conv", DEPTH * 4 * TAPS), ("ib", DEPTH), ("fb", DEPTH),
                         ("rb", NE), ("gates", DEPTH * KD * 8), ("router", KD * NE)])


def build(nc, a):
    with ExitStack() as ctx:
        def sb(name, shape, dt=F32):
            return ctx.enter_context(nc.sbuf_tensor("sb_" + name, shape, dt))

        def sem(name):
            return ctx.enter_context(nc.semaphore(name))

        const = sb("const", [P, N_CONST])
        small = sb("small", [P, N_SMALL])
        x = sb("x", [P, TT, D])
        ringa = sb("ringa", [P, RING_A, SLOT])
        z = sb("z", [P, TT, ZW])
        whi = sb("whi", [P, RING_L, SLOT], F32R)
        wlo = sb("wlo", [P, RING_L, SLOT], F32R)
        hhi = sb("hhi", [P, KD, S], F32R)
        hlo = sb("hlo", [P, KD, S], F32R)
        ahi = sb("ahi", [P, 4, S], F32R)
        alo = sb("alo", [P, 4, S], F32R)
        w1 = sb("w1", [P, TT * D])
        w2 = sb("w2", [P, GH * BLK])
        w4a = sb("w4a", [P, 4, S + TAPS - 1])
        w4b = sb("w4b", [P, 4, S])
        rows = sb("rows", [MH, 3, S])
        st = sb("st", [P, 448])
        root = sb("root", [P, 128])
        eid = sb("eid", [1, 16], I32)
        ps = ctx.enter_context(nc.psum_tensor("ps", [P, 8, 512], F32))

        def con(name):
            return const[:, CONST[name][0]:CONST[name][1]]

        def par(name, at, n=1):
            return small[:, SMALL[name][0] + at:SMALL[name][0] + at + n]

        zf = z[:, :, :].rearrange("p t n -> p (t n)")
        ident, tri, ones, iota = con("ident"), con("tri"), con("ones"), con("iota")
        rot = con("rot").rearrange("p (t f d) -> p t f d", t=TT, f=2)
        decay = con("decay").rearrange("p (h n) -> p h n", h=RH)
        damask = con("damask").rearrange("p (g n) -> p g n", g=NG)
        mlmask = con("mlmask")

        def stat(at, n):
            return st[:, at:at + n]
        ss2, rstd2 = stat(0, 2), stat(2, 2)
        z8 = stat(4, 16).rearrange("p (t n) -> p t n", t=TT)
        ccol = stat(20, 8).rearrange("p (t h) -> p t h", t=TT)
        emcol = stat(28, 8)
        rss, rrs = stat(36, 8), stat(44, 8)
        mss, mrs, mden = stat(52, 8), stat(60, 8), stat(68, 8)
        dss = stat(76, 48).rearrange("p (t n) -> p t n", t=TT)
        drs = stat(124, 48).rearrange("p (t n) -> p t n", t=TT)
        dneg = stat(172, 24).rearrange("p (g t h) -> p g t h", g=NG, t=TT)
        dl = stat(196, 24).rearrange("p (g t h) -> p g t h", g=NG, t=TT)
        dco = stat(220, 24).rearrange("p (g t h) -> p g t h", g=NG, t=TT)
        dtmp = stat(244, 8)
        lg = stat(252, 16).rearrange("p (t n) -> p t n", t=TT)
        m1 = stat(268, 16).rearrange("p (t n) -> p t n", t=TT)
        m2 = stat(284, 16).rearrange("p (t n) -> p t n", t=TT)
        rt = stat(300, 16).rearrange("p (t n) -> p t n", t=TT)
        v12 = stat(316, 8).rearrange("p (t n) -> p t n", t=TT)
        posx = stat(324, 24).rearrange("p (t n) -> p t n", t=TT)
        gatex = stat(348, 24).rearrange("p (t n) -> p t n", t=TT)
        cnt, big, rank = stat(372, 8), stat(380, 8), stat(388, 8)
        eidf = stat(396, 16)
        selx = stat(412, 8)
        rtmp = stat(420, 16).rearrange("p (t n) -> p t n", t=TT)

        blk2 = w2[:, :].rearrange("p (h n) -> p h n", h=4)
        blkz = z[:, :, 0:2 * BLK].rearrange("p t (h n) -> p t h n", h=2)
        blkm = z[:, :, 2 * BLK:4 * BLK].rearrange("p t (h n) -> p t h n", h=2)
        qk = w1[:, :].rearrange("p (c s) -> p c s", s=S)
        w1t = w1[:, :].rearrange("p (t n) -> p t n", t=TT)
        big1 = w1[:, 0:TT * 512].rearrange("p (t n) -> p t n", t=TT)
        big2 = w1[:, TT * 512:].rearrange("p (t n) -> p t n", t=TT)
        rowt = w2[0:MH, :].rearrange("p (r s) -> p r s", s=S)
        ringb = zf[:, 0:RING_B * SLOT].rearrange("p (r n) -> p r n", r=RING_B)
        spare = zf[:, RING_B * SLOT:]
        act_sb = spare[:, 0:TT * C].rearrange("p (t n) -> p t n", t=TT)
        y_sb = z[:, :, Z_G:Z_G + D]
        sil_sb = spare[:, TT * C:2 * TT * C].rearrange("p (t n) -> p t n", t=TT)
        yacc = spare[:, 2 * TT * C:2 * TT * C + D]
        pick = spare[:, 3072:3072 + TT * CAP].rearrange("p (t n) -> p t n", t=TT)
        pickg = spare[:, 3328:3328 + TT * CAP].rearrange("p (t n) -> p t n", t=TT)
        spread = spare[:, 3584:3584 + S]

        raw_a = [sem(f"raw_a{i}") for i in range(RING_A)]
        raw_b = [sem(f"raw_b{i}") for i in range(RING_B)]
        hi_done = sem("hi_done")
        lo_pool = sem("lo_pool")
        lo_dve = sem("lo_dve")
        used = sem("used")
        ident_in, consts_in, x_in, out_done = sem("ident_in"), sem("consts_in"), sem("x_in"), sem("out_done")
        dve_chain, act_chain = sem("dve_chain"), sem("act_chain")
        tok_ready = sem("tok_ready")
        ht_turned, ht_hi, ht_lo = sem("ht_turned"), sem("ht_hi"), sem("ht_lo")
        yt_turned = sem("yt_turned")
        conv_pad, conv_y, conv_act = (sem(n) for n in ("conv_pad", "conv_y", "conv_act"))
        z8_mm, z8_sb, row_t, row_abs, row_exp, row_ln, rows_ok = (
            sem(n) for n in ("z8_mm", "z8_sb", "row_t", "row_abs", "row_exp", "row_ln", "rows_ok"))
        col_t, col_sb, col_exp = sem("col_t"), sem("col_sb"), sem("col_exp")
        z_out, g_out = sem("z_out"), sem("g_out")
        rg_act, mo_act, rotated = sem("rg_act"), sem("mo_act"), sem("rotated")
        rqk_t, rqk_sb, rsc_mm, rsc_sb, rpv_mm, rpv_sq, ro_out = (
            sem(n) for n in ("rqk_t", "rqk_sb", "rsc_mm", "rsc_sb", "rpv_mm", "rpv_sq", "ro_out"))
        dsq, dsum, dn_ok = sem("dsq"), sem("dsum"), sem("dn_ok")
        dqk_t, dqk_sb, dsc_mm, dsc_sb, dexp, dp_t, dp_sb, dpv_mm, dpv_sb = (
            sem(n) for n in ("dqk_t", "dqk_sb", "dsc_mm", "dsc_sb", "dexp", "dp_t", "dp_sb", "dpv_mm", "dpv_sb"))
        dln, dlse, dwt, do_out = sem("dln"), sem("dlse"), sem("dwt"), sem("do_out")
        msel_mm, mdw_in, mdw, msc_mm, msc_sb, mpv_mm, mh_sb, msq, mo_out = (
            sem(n) for n in ("msel_mm", "mdw_in", "mdw", "msc_mm", "msc_sb", "mpv_mm", "mh_sb", "msq", "mo_out"))
        ot_t, ot_hi, ot_lo, br_half, br_out = (sem(n) for n in ("ot_t", "ot_hi", "ot_lo", "br_half", "br_out"))
        sig_ok, x_end = sem("sig_ok"), sem("x_end")
        silu, a_ok, a_t, a_hi, a_lo, d_out = (sem(n) for n in ("silu", "a_ok", "a_t", "a_hi", "a_lo", "d_out"))
        lg_mm, lg_e, lg_d, sel_ok, cnt_mm, route_ok = (
            sem(n) for n in ("lg_mm", "lg_e", "lg_d", "sel_ok", "cnt_mm", "route_ok"))
        pick_ok, gather_mm, gt_hi, gt_lo, spread_t, spread_sb, scat_mm, y_zero = (
            sem(n) for n in ("pick_ok", "gather_mm", "gt_hi", "gt_lo", "spread_t", "spread_sb", "scat_mm", "y_zero"))

        def number(layer, phase, s, r=0):
            at = layer * (A_SLOTS + F_SLOTS) + (A_SLOTS if phase == "B" else 0) + s
            return r * ROUND + at

        def ordinal(layer, phase, s):
            return layer * (A_SLOTS if phase == "A" else F_SLOTS) + s

        def lane(layer, phase, s):
            return number(layer, phase, s) % RING_L

        def ring(phase):
            return (RING_A, raw_a, ringa[:, :, :]) if phase == "A" else (RING_B, raw_b, ringb)

        def raw_slot(layer, phase, s):
            n, _, tile = ring(phase)
            return tile[:, ordinal(layer, phase, s) % n, :]

        def wait_lo(eng, layer, phase, s, r=0):
            eng.wait_ge(lo_pool, number(layer, phase, s, r) + 1)
            if phase == "B":
                eng.wait_ge(lo_dve, r * ROUND + (ordinal(layer, phase, s) + 1))

        def wait_split(eng, layer, phase, s, r=0):
            size = ring(phase)[0]
            if number(layer, phase, s) < size:
                return
            if phase == "B" and ordinal(layer, phase, s) >= size:
                eng.wait_ge(used, number(layer, phase, s - size, r) + 1)
            elif phase == "A":
                eng.wait_ge(lo_pool, number(layer, phase, s - size, r) + 1)

        def hi_of(act, layer, phase, s, r=0):
            size, sems, _ = ring(phase)
            o = ordinal(layer, phase, s)
            act.wait_ge(sems[o % size], (r * (ROUND // size) + (o // size + 1)) * 16)
            if number(layer, phase, s) >= RING_L:
                act.wait_ge(used, number(layer, phase, s, r) + 1 - RING_L)
            n = width(layer, phase, s)
            nc.scalar.activation(whi[:, lane(layer, phase, s), 0:n], raw_slot(layer, phase, s)[:, 0:n],
                                 ACT.Copy).then_inc(hi_done, 1)

        def lo_of(eng, layer, phase, s, r=0):
            eng.wait_ge(hi_done, number(layer, phase, s, r) + 1)
            k, n = lane(layer, phase, s), width(layer, phase, s)
            cut = int(n * DVE_SHARE) // 4 * 4 if phase == "B" else 0
            c = slice(0, cut) if eng is nc.vector else slice(cut, n)
            eng.tensor_tensor(wlo[:, k, c], raw_slot(layer, phase, s)[:, c], whi[:, k, c].bitcast(F32),
                              ALU.subtract).then_inc(lo_dve if eng is nc.vector else lo_pool, 1)

        def wait_used(eng, layer, phase, s, r=0):
            eng.wait_ge(used, number(layer, phase, s, r) + 1)

        Q_HALF, Q_MV, Q_MO, Q_G = N_LOOP, N_LOOP + 1, N_LOOP + 2, N_LOOP + 3
        N_Q = Q_G + N_G
        S_BR = 2 + 2 * N_Q

        def chunk(q):
            if q < N_LOOP:
                return q * C, q * C, C
            if q == Q_HALF:
                return N_LOOP * C, N_LOOP * C, IN_DV_END - N_LOOP * C
            if q <= Q_MO:
                return IN_MV + (q - Q_MV) * C, Z_MV + (q - Q_MV) * C, C
            return IN_G + (q - Q_G) * C, Z_G + (q - Q_G) * C, C

        HALF = FF - F_CHUNKS * C

        def width(layer, phase, s):
            if phase == "A" and 2 <= s < S_BR:
                return KH * chunk((s - 2) // 2)[2]
            if phase == "B" and layer == 0 and s >= F_SLOTS - 8:
                return KH * HALF if s < F_SLOTS - 4 else (SLOT if s < F_SLOTS - 2 else HALF // P * C)
            return SLOT

        block = ctx.enter_context(nc.Block())

        @block.sync
        def _(sp):
            def load(layer, phase, s, src, r=0, k=KH):
                wait_split(sp, layer, phase, s, r)
                size, sems, _ = ring(phase)
                dst = raw_slot(layer, phase, s)[:, 0:width(layer, phase, s)].rearrange("p (k n) -> p k n", k=k)
                sp.dma_start(dst, src).then_inc(sems[ordinal(layer, phase, s) % size], 16)

            def part(w, k0, kn, c0, n):
                return w[k0 * P:(k0 + kn) * P, c0:c0 + n].rearrange("(k p) n -> p k n", p=P)

            def run(w, k0, kn, c0, n):
                return w[k0 * P:(k0 + kn) * P, bass.ds(c0, n)].rearrange("(k p) n -> p k n", p=P)

            sp.dma_start(x[:, :, :], a["x"].rearrange("b (t p) d -> p (b t) d", p=P)).then_inc(x_in, 16)
            sp.dma_start(const[:, 0:P], a["const"][:, 0:P]).then_inc(ident_in, 16)
            sp.dma_start(small[:, :], a["small"]).then_inc(ident_in, 16)

            for layer in range(DEPTH):
                w_in = a["w_in"][layer]
                for h in range(2):
                    load(layer, "A", h, part(w_in, KH * h, KH, IN_QK, C))
                if layer == 0:
                    sp.dma_start(const[:, P:], a["const"][:, P:]).then_inc(consts_in, 16)
                for s in range(4):
                    load(layer, "A", 2 + s, part(w_in, KH * (s % 2), KH, s // 2 * C, C))
                with sp.Fori(0, (N_LOOP - 2) // 3) as i:
                    for s in range(ROUND):
                        load(layer, "A", 6 + s, run(w_in, KH * (s % 2), KH, i * (3 * C) + (2 + s // 2) * C, C), r=i)
                for q in range(N_LOOP, N_Q):
                    c0, _, n = chunk(q)
                    for h in range(2):
                        load(layer, "A", 2 + 2 * q + h, part(w_in, KH * h, KH, c0, n))
                for h in range(2):
                    load(layer, "A", S_BR + h, part(a["w_br_ret"][layer], 0, 4, h * C, C))
                load(layer, "A", S_BR + 2, part(a["w_br_da"][layer], 0, 2, 0, D), k=2)
                for h in range(2):
                    load(layer, "A", S_BR + 3 + h, part(a["w_br_ml"][layer], 0, 4, h * C, C))
                for s in range(4):
                    load(layer, "A", S_BR + 5 + s, part(a["w_out"][layer], KH * (s % 2), KH, s // 2 * C, C))

                sp.wait_ge(yt_turned, 4 * (layer + 1))
                if layer == 0:
                    gu, wd = (a["ffn_w_gate"][0], a["ffn_w_up"][0]), a["ffn_w_down"][0]
                    for s in range(4):
                        load(0, "B", s, part(gu[s // 2], KH * (s % 2), KH, 0, C))
                    for s in range(4):
                        load(0, "B", 4 + s, part(gu[s // 2], KH * (s % 2), KH, C, C))
                    for h in range(2):
                        load(0, "B", 8 + h, part(wd, 0, 4, h * C, C))
                    with sp.Fori(0, F_CHUNKS - 2) as i:
                        for s in range(4):
                            load(0, "B", 10 + s, run(gu[s // 2], KH * (s % 2), KH, i * C + 2 * C, C), r=i)
                        for h in range(2):
                            load(0, "B", 14 + h, wd[bass.ds(i * C + C, C), h * C:(h + 1) * C]
                                 .rearrange("(k p) n -> p k n", p=P), r=i)
                    s0 = F_SLOTS - 8
                    for s in range(4):
                        load(0, "B", s0 + s, part(gu[s // 2], KH * (s % 2), KH, F_CHUNKS * C, HALF))
                    for h in range(2):
                        load(0, "B", s0 + 4 + h, part(wd, 4 * (F_CHUNKS - 1), 4, h * C, C))
                    for h in range(2):
                        load(0, "B", s0 + 6 + h, part(wd, 4 * F_CHUNKS, HALF // P, h * C, C), k=HALF // P)
                else:
                    gu = [a[n][0].rearrange("e d f -> (e d) f") for n in ("moe_w_gate", "moe_w_up")]
                    wd = a["moe_w_down"][0].rearrange("e f d -> (e f) d")

                    def load_round(e, j):
                        def from_gu(s, c0):
                            return gu[s // 2][bass.ds(e * D + KH * (s % 2) * P, KH * P), c0].rearrange(
                                "(k p) n -> p k n", p=P)

                        def from_d(h, f0):
                            return wd[bass.ds(f0, C), h * C:(h + 1) * C].rearrange("(k p) n -> p k n", p=P)

                        for s in range(4):
                            load(1, "B", s, from_gu(s, slice(0, C)), r=j * E_CHUNKS)
                        with sp.Fori(0, E_CHUNKS - 1) as i:
                            for s in range(4):
                                load(1, "B", 4 + s, from_gu(s, bass.ds(i * C + C, C)), r=i + j * E_CHUNKS)
                            for h in range(2):
                                load(1, "B", 8 + h, from_d(h, i * C + e * FE), r=i + j * E_CHUNKS)
                        for h in range(2):
                            load(1, "B", E_SLOTS - 2 + h, from_d(h, e * FE + (E_CHUNKS - 1) * C), r=j * E_CHUNKS)

                    load_round(0, 0)
                    sp.wait_ge(route_ok, 1)
                    items = sp.value_load(eid[0:1, 15:16], min_val=NE, max_val=ITEMS)
                    with sp.Fori(1, items) as j:
                        load_round(sp.value_load(eid[0:1, bass.ds(j, 1)], min_val=0, max_val=NE - 1), j)
            sp.wait_ge(x_end, 1)
            sp.dma_start(a["out"].rearrange("b (t p) d -> p (b t) d", p=P), x[:, :, :]).then_inc(out_done, 16)
            sp.wait_ge(out_done, 16)

        @block.gpsimd
        def _(pool):
            for layer in range(DEPTH):
                for s in range(6):
                    lo_of(pool, layer, "A", s)
                with pool.Fori(0, (N_LOOP - 2) // 3) as i:
                    for s in range(ROUND):
                        lo_of(pool, layer, "A", 6 + s, i)
                for s in range(2 + 2 * N_LOOP, A_SLOTS):
                    lo_of(pool, layer, "A", s)
                if layer == 0:
                    with pool.Fori(0, F_CHUNKS - 1) as i:
                        for s in range(ROUND):
                            lo_of(pool, 0, "B", s, i)
                    for s in range(ROUND * (F_CHUNKS - 1), F_SLOTS):
                        lo_of(pool, 0, "B", s)
                else:
                    with pool.Fori(0, E_CHUNKS) as i:
                        for s in range(ROUND):
                            lo_of(pool, 1, "B", s, i)
                    pool.wait_ge(route_ok, 1)
                    items = pool.value_load(eid[0:1, 15:16], min_val=NE, max_val=ITEMS)
                    with pool.Fori(E_CHUNKS, items * E_CHUNKS) as i:
                        for s in range(ROUND):
                            lo_of(pool, 1, "B", s, i)

        def pair(q):
            return 2 * (q % 3) if q < N_LOOP else 2 * (q % 2)

        @block.tensor
        def _(pe):
            def mm3(out, lh, ll, rh, rl, start, stop):
                nc.tensor.matmul(out, lh, rh, start=start, stop=False)
                nc.tensor.matmul(out, ll, rh, start=False, stop=False)
                return nc.tensor.matmul(out, lh, rl, start=False, stop=stop)

            def mm(out, l, r, start=True, stop=True):
                return nc.tensor.matmul(out, l, r, start=start, stop=stop)

            def turn(out, src):
                n = src.shape[0]
                return nc.tensor.transpose(out, src, ident[0:n, 0:n])

            def product(layer, phase, s, r, banks, lhs, rows0, first, last, n=C, k=KH):
                wait_lo(pe, layer, phase, s, r)
                ln = lane(layer, phase, s)
                hi = whi[:, ln, 0:k * n].rearrange("p (k n) -> p k n", k=k)
                lo = wlo[:, ln, 0:k * n].rearrange("p (k n) -> p k n", k=k)
                lh, ll = lhs
                for t, b in enumerate(banks):
                    for kk in range(k):
                        m = mm3(ps[:, b, 0:n], lh[:, rows0 + kk, t * P:(t + 1) * P],
                                      ll[:, rows0 + kk, t * P:(t + 1) * P], hi[:, kk, :], lo[:, kk, :],
                                      first and kk == 0, last and kk == k - 1)
                m.then_inc(used, 1)

            def turn_tokens(src, done):
                for b in range(4):
                    for kk in range(2):
                        for t in range(TT):
                            m = turn(ps[:, 4 + b, kk * S + t * P:kk * S + (t + 1) * P],
                                     src[:, t, (2 * b + kk) * P:(2 * b + kk + 1) * P])
                    m.then_inc(done, 1)

            pe.wait_ge(ident_in, 32)
            for layer in range(DEPTH):
                L = layer + 1

                pe.wait_ge(tok_ready, 2 * (3 * layer + 1))
                if layer > 0:
                    pe.wait_ge(d_out, 4 * (F_CHUNKS + 1))
                turn_tokens(w1t, ht_turned)
                pe.wait_ge(ht_lo, 4 * (3 * layer + 1))

                for s in range(2):
                    wait_lo(pe, layer, "A", s)
                    hi, lo = (w[:, lane(layer, "A", s), :].rearrange("p (k n) -> p k n", n=C) for w in (whi, wlo))
                    for c in range(4):
                        for kk in range(KH):
                            m = mm3(ps[:, c, 0:S], hi[:, kk, c * P:(c + 1) * P], lo[:, kk, c * P:(c + 1) * P],
                                    hhi[:, KH * s + kk, :], hlo[:, KH * s + kk, :],
                                    s == 0 and kk == 0, s == 1 and kk == KH - 1)
                    m.then_inc(used, 1)
                for t in range(TT):
                    for k in range(KD):
                        for part_, h in enumerate((hhi, hlo)):
                            m = mm(ps[:, 6, t * 8:t * 8 + 8], h[:, k, t * P:(t + 1) * P].bitcast(F32),
                                   par("gates", (layer * KD + k) * 8, 8),
                                   start=k == 0 and part_ == 0, stop=k == KD - 1 and part_ == 1)
                m.then_inc(z8_mm, 1)

                def z_chunk(q, h, r=0):
                    if h == 0:
                        if q < 2:
                            pe.wait_ge(conv_pad, L)
                        elif q <= Q_G + 1:
                            pe.wait_ge(z_out, r * 3 + (layer * Q_G + q - 1))
                        else:
                            pe.wait_ge(g_out, layer * N_G + q - 1 - Q_G)
                    b, n = pair(q), chunk(q)[2]
                    product(layer, "A", 2 + 2 * q + h, r, (b, b + 1), (hhi, hlo), KH * h, h == 0, h == 1, n)

                z_chunk(0, 0)
                z_chunk(0, 1)
                pe.wait_ge(z8_sb, L)
                for g in range(2):
                    for t in range(TT):
                        m = turn(ps[0:MH, 7, g * S + t * P:g * S + (t + 1) * P], z8[:, t, g * MH:(g + 1) * MH])
                m.then_inc(row_t, 1)
                z_chunk(1, 0)
                z_chunk(1, 1)
                with pe.Fori(0, (N_LOOP - 2) // 3) as i:
                    for q in (2, 3, 4):
                        z_chunk(q, 0, i)
                        z_chunk(q, 1, i)

                def ml_columns():
                    if layer == 0:
                        pe.wait_ge(consts_in, 16)
                    pe.wait_ge(rows_ok, L)
                    for g, row in enumerate((0, 2)):
                        for t in range(TT):
                            m = turn(ps[:, 7, g * 8 + t * 4:g * 8 + t * 4 + 4], rows[:, row, t * P:(t + 1) * P])
                    m.then_inc(col_t, 1)

                def ret_turn():
                    pe.wait_ge(rotated, L)
                    pe.wait_ge(col_sb, L)
                    for c in range(8):
                        for t in range(TT):
                            m = turn(ps[:, 4 + c // 2, c % 2 * S + t * P:c % 2 * S + (t + 1) * P],
                                     z[:, t, c * P:(c + 1) * P])
                    m.then_inc(rqk_t, 1)

                def ret_scores():
                    pe.wait_ge(rqk_sb, L)
                    for h in range(RH):
                        mm(ps[:, 4 + h, 0:S], qk[:, RH + h, 0:P], qk[:, h, :])
                        m = mm(ps[:, 4 + h, S:BLK], qk[:, RH + h, P:S], qk[:, h, P:S])
                    m.then_inc(rsc_mm, 1)

                def weighted(bank0, src, vcol, width, m_of=None):
                    for h in range(4):
                        o = slice(h * width, (h + 1) * width)
                        v = [z[:, t, vcol + h * width:vcol + (h + 1) * width] for t in range(TT)]
                        mm(ps[:, bank0, o], src(h)[:, 0:P], v[0])
                        mm(ps[:, bank0 + 1, o], src(h)[:, P:S], v[0], stop=False)
                        m = mm(ps[:, bank0 + 1, o], src(h)[:, S:BLK], v[1], start=False)
                    return m

                def ret_out():
                    pe.wait_ge(rsc_sb, L)
                    weighted(4, lambda h: blk2[:, h, :], Z_RV, RDV).then_inc(rpv_mm, 1)

                def da_turn(g):
                    if g == 0:
                        pe.wait_ge(dn_ok, L)
                        pe.wait_ge(ro_out, L)
                    else:
                        pe.wait_ge(dp_sb, layer * NG + g)
                    for b, col in enumerate((Z_DQ, Z_DK)):
                        for c in range(2):
                            for t in range(TT):
                                m = turn(ps[:, 4 + b, c * S + t * P:c * S + (t + 1) * P],
                                         z[:, t, col + (2 * g + c) * P:col + (2 * g + c + 1) * P])
                    m.then_inc(dqk_t, 1)

                def da_scores(g):
                    pe.wait_ge(dqk_sb, layer * NG + g + 1)
                    if g > 0:
                        pe.wait_ge(dpv_sb, layer * NG + g)
                    for h in range(GH):
                        r = slice(h % 2 * DH, (h % 2 + 1) * DH)
                        q, k = qk[r, h // 2, :], qk[r, 2 + h // 2, :]
                        mm(ps[:, 4 + h, 0:P], q[:, 0:P], k[:, 0:P])
                        m = mm(ps[:, 4 + h, P:BLK], q[:, P:S], k)
                    m.then_inc(dsc_mm, 1)

                def da_turn_p(g):
                    pe.wait_ge(dexp, layer * NG + g + 1)
                    for h in range(GH):
                        for j in range(3):
                            m = turn(ps[:, 4 + h, j * P:(j + 1) * P], blk2[:, h, j * P:(j + 1) * P])
                    m.then_inc(dp_t, 1)

                def da_out(g):
                    pe.wait_ge(dp_sb, layer * NG + g + 1)
                    weighted(6, lambda h: blkz[:, h // 2, h % 2, :], Z_DV + g * GH * DH, DH).then_inc(dpv_mm, 1)

                def ml_spread():
                    for h in range(MH):
                        m = mm(ps[:, 4 + h // 2, h % 2 * S:(h % 2 + 1) * S], con("sel")[0:MH, h * P:(h + 1) * P],
                               rows[:, 1, :])
                    m.then_inc(msel_mm, 1)

                def ml_scores():
                    pe.wait_ge(conv_act, L)
                    pe.wait_ge(mdw_in, L)
                    pe.wait_ge(dpv_sb, L * NG)
                    for h in range(MH):
                        r = slice(h % 2 * MDK, (h % 2 + 1) * MDK)
                        q, k = w4b[r, h // 2, :], w4b[r, 2 + h // 2, :]
                        mm(ps[:, 4 + h, 0:S], k[:, 0:P], q)
                        m = mm(ps[:, 4 + h, S:BLK], k[:, P:S], q[:, P:S])
                    m.then_inc(msc_mm, 1)

                def ml_out():
                    pe.wait_ge(msc_sb, L)
                    s = lambda h: blkm[:, h // 2, h % 2, :]
                    weighted(4, s, Z_MV, MDV)
                    one = ones[:, 0:1]
                    for h in range(MH):
                        mm(ps[:, 6, h:h + 1], s(h)[:, 0:P], one)
                        mm(ps[:, 6, MH + h:MH + h + 1], s(h)[:, P:S], one, stop=False)
                        m = mm(ps[:, 6, MH + h:MH + h + 1], s(h)[:, S:BLK], one, start=False)
                    m.then_inc(mpv_mm, 1)

                behind = {
                    (Q_HALF, 0): (ml_columns,), (Q_HALF, 1): (ret_turn,),
                    (Q_MV, 0): (ret_scores,), (Q_MV, 1): (ret_out,),
                    (Q_MO, 0): (lambda: da_turn(0),), (Q_MO, 1): (lambda: da_scores(0),),
                    (Q_G, 0): (lambda: da_turn_p(0),), (Q_G, 1): (lambda: da_turn(1), lambda: da_out(0)),
                    (Q_G + 1, 0): (lambda: da_scores(1),), (Q_G + 1, 1): (lambda: da_turn_p(1),),
                    (Q_G + 2, 0): (lambda: da_turn(2), lambda: da_out(1)), (Q_G + 2, 1): (lambda: da_scores(2),),
                    (Q_G + 3, 0): (lambda: da_turn_p(2),), (Q_G + 3, 1): (lambda: da_out(2), ml_spread),
                    (Q_G + 4, 0): (ml_scores,), (Q_G + 4, 1): (ml_out,),
                }
                for q in range(Q_HALF, N_Q):
                    for h in range(2):
                        z_chunk(q, h)
                        for step in behind.get((q, h), ()):
                            step()

                def turn_out(n, bank, col):
                    for kk in range(2):
                        for t in range(TT):
                            m = turn(ps[:, bank, kk * S + t * P:kk * S + (t + 1) * P],
                                     z[:, t, col + kk * P:col + (kk + 1) * P])
                    m.then_inc(ot_t, 1)
                pe.wait_ge(mo_out, L)
                pe.wait_ge(do_out, L)
                turn_out(0, 4, Z_RG)
                turn_out(1, 5, Z_RG + 2 * P)
                turn_out(2, 6, Z_DQ)
                turn_out(3, 7, Z_MO)
                pe.wait_ge(ot_lo, layer * 5 + 1)
                turn_out(4, 4, Z_MO + 2 * P)

                def branch(slot, bank, lhs):
                    product(layer, "A", S_BR + slot, 0, (bank, bank + 1), lhs, 0, True, True)
                pe.wait_ge(g_out, L * N_G)
                pe.wait_ge(ot_lo, layer * 5 + 2)
                branch(0, 0, (hhi, hlo))
                branch(1, 2, (hhi, hlo))
                pe.wait_ge(ot_lo, layer * 5 + 3)
                wait_lo(pe, layer, "A", S_BR + 2)
                ln = lane(layer, "A", S_BR + 2)
                hi, lo = (w[:, ln, :].rearrange("p (k n) -> p k n", k=2) for w in (whi, wlo))
                for half in range(2):
                    pe.wait_ge(br_out, layer * 6 + 1 + half)
                    for t in range(TT):
                        for kk in range(2):
                            m = mm3(ps[:, 2 * half + t, :], hhi[:, 4 + kk, t * P:(t + 1) * P],
                                    hlo[:, 4 + kk, t * P:(t + 1) * P], hi[:, kk, half * C:(half + 1) * C],
                                    lo[:, kk, half * C:(half + 1) * C], kk == 0, kk == 1)
                    m.then_inc(used if half else br_half, 1)
                pe.wait_ge(ot_lo, layer * 5 + 5)
                for half in range(2):
                    pe.wait_ge(br_out, layer * 6 + 3 + half)
                    branch(3 + half, 2 * half, (ahi, alo))

                pe.wait_ge(tok_ready, 2 * (3 * layer + 2))
                turn_tokens(y_sb, yt_turned)
                pe.wait_ge(ht_lo, 4 * (3 * layer + 2))
                for half in range(2):
                    pe.wait_ge(br_out, layer * 6 + 5 + half)
                    for kh in range(2):
                        product(layer, "A", S_BR + 5 + 2 * half + kh, 0, (2 * half, 2 * half + 1), (hhi, hlo),
                                KH * kh, kh == 0, kh == 1)

                pe.wait_ge(tok_ready, 2 * (3 * layer + 3))
                turn_tokens(w1t, ht_turned)
                pe.wait_ge(ht_lo, 4 * (3 * layer + 3))
                if layer == 0:
                    def f_gate(s, i, r=0, n=C):
                        if s > 0:
                            pe.wait_ge(silu, i * 2)
                        for h in range(2):
                            product(0, "B", s + h, r, (0, 1), (hhi, hlo), KH * h, h == 0, h == 1, n)

                    def f_up(s, i, r=0, n=C):
                        if s > 2:
                            pe.wait_ge(a_ok, i * 2)
                        for h in range(2):
                            product(0, "B", s + h, r, (2, 3), (hhi, hlo), KH * h, h == 0, h == 1, n)

                    def f_turn(i, n=4, first=False):
                        pe.wait_ge(a_ok, i * 2 + 2)
                        if not first:
                            pe.wait_ge(d_out, i * 4)
                        for t in range(TT):
                            for k in range(n):
                                m = turn(ps[:, 4 + t, k * P:(k + 1) * P], act_sb[:, t, k * P:(k + 1) * P])
                            m.then_inc(a_t, 1)

                    def f_down(s, i, r=0, k=4):
                        pe.wait_ge(a_lo, i * 2 + 2)
                        for h in range(2):
                            product(0, "B", s + h, r, (6 - 2 * h, 7 - 2 * h), (ahi, alo), 0, True, True, k=k)

                    f_gate(0, 0)
                    f_up(2, 0)
                    f_gate(4, 1)
                    f_turn(0, first=True)
                    f_up(6, 1)
                    f_down(8, 0)
                    with pe.Fori(0, F_CHUNKS - 2) as i:
                        f_gate(10, i + 2, i)
                        f_turn(i + 1)
                        f_up(12, i + 2, i)
                        f_down(14, i + 1, i)
                    s = F_SLOTS - 8
                    f_gate(s, F_CHUNKS, n=HALF)
                    f_turn(F_CHUNKS - 1)
                    f_up(s + 2, F_CHUNKS, n=HALF)
                    f_down(s + 4, F_CHUNKS - 1)
                    f_turn(F_CHUNKS, n=HALF // P)
                    f_down(s + 6, F_CHUNKS, k=HALF // P)
                    continue

                for t in range(TT):
                    for k in range(KD):
                        for part_, h in enumerate((hhi, hlo)):
                            m = mm(ps[:, 0, t * NE:(t + 1) * NE], h[:, k, t * P:(t + 1) * P].bitcast(F32),
                                   par("router", k * NE, NE), start=k == 0 and part_ == 0, stop=k == KD - 1 and part_ == 1)
                m.then_inc(lg_mm, 1)
                pe.wait_ge(sel_ok, 1)
                mm(ps[:, 1, 0:NE], tri, rt[:, 0, :])
                mm(ps[:, 1, NE:2 * NE], tri, rt[:, 1, :], stop=False)
                mm(ps[:, 1, NE:2 * NE], ones, rt[:, 0, :], start=False)
                mm(ps[:, 1, 2 * NE:3 * NE], ones, rt[:, 0, :], stop=False)
                mm(ps[:, 1, 2 * NE:3 * NE], ones, rt[:, 1, :], start=False).then_inc(cnt_mm, 1)

                def e_gate(s, n, r):
                    pe.wait_ge(silu, n + F_TILES)
                    for h in range(2):
                        product(1, "B", s + h, r, (0,), (hhi, hlo), KH * h, h == 0, h == 1)

                def e_up(s, n, r):
                    pe.wait_ge(a_ok, n + F_TILES)
                    for h in range(2):
                        product(1, "B", s + h, r, (1,), (hhi, hlo), KH * h, h == 0, h == 1)

                def e_turn(n, d):
                    pe.wait_ge(a_ok, n + (F_TILES + 1))
                    pe.wait_ge(a_lo, n + F_TILES)
                    pe.wait_ge(d_out, d)
                    for k in range(4):
                        m = turn(ps[:, 2, k * P:(k + 1) * P], act_sb[:, 0, k * P:(k + 1) * P])
                    m.then_inc(a_t, 1)

                def e_down(s, n, d, r):
                    pe.wait_ge(a_lo, n + (F_TILES + 1))
                    pe.wait_ge(d_out, d)
                    for h in range(2):
                        product(1, "B", s + h, r, (3 + h,), (ahi, alo), 0, True, True)

                def gather(n):
                    pe.wait_ge(pick_ok, n + 1)
                    for k in range(KD):
                        for t in range(TT):
                            m = mm(ps[:, 5 + k // 4, k % 4 * P:(k % 4 + 1) * P], w1t[:, t, k * P:(k + 1) * P],
                                   pick[:, t, :], start=t == 0, stop=t == 1)
                    m.then_inc(gather_mm, 1)

                def scatter(n):
                    pe.wait_ge(d_out, n * E_SUMS + F_SUMS)
                    pe.wait_ge(spread_sb, n + 1)
                    for k, bank in enumerate((7, 3, 4, 2)):
                        mm(ps[:, bank, :], spread[:, k // 2 * P:(k // 2 + 1) * P],
                           yacc[:, k % 2 * C:(k % 2 + 1) * C]).then_inc(scat_mm, 1)

                gather(0)
                pe.wait_ge(route_ok, 1)
                items = pe.value_load(eid[0:1, 15:16], min_val=NE, max_val=ITEMS)
                with pe.Fori(0, items) as j:
                    n0, d0 = j * E_CHUNKS, j * E_SUMS + (F_SUMS + 2 * TT)
                    pe.wait_ge(gt_lo, j + 1)
                    e_gate(0, n0, n0)
                    scatter(j)
                    e_up(2, n0, n0)
                    pe.wait_ge(d_out, d0)
                    for t in range(TT):
                        m = turn(ps[:, 7, t * P:(t + 1) * P], pickg[:, t, :])
                    m.then_inc(spread_t, 1)
                    with pe.Fori(0, E_CHUNKS - 1) as i:
                        e_gate(4, n0 + i + 1, n0 + i)
                        e_turn(n0 + i, d0)
                        e_up(6, n0 + i + 1, n0 + i)
                        e_down(8, n0 + i, d0 + i * 2, n0 + i)
                    e_turn(n0 + (E_CHUNKS - 1), d0)
                    gather(j + 1)
                    e_down(E_SLOTS - 2, n0 + (E_CHUNKS - 1), d0 + 2 * (E_CHUNKS - 1), n0)
                scatter(items)

        @block.scalar
        def _(act):
            def turned_hi(turn_no, done, dcount, scale):
                for b in range(4):
                    act.wait_ge(done, dcount + b + 1)
                    for kk in range(2):
                        k = 2 * b + kk
                        m = nc.scalar.activation(hhi[:, k, :], ps[:, 4 + b, kk * S:(kk + 1) * S], ACT.Copy,
                                                 scale=scale(k)) if scale else \
                            nc.scalar.activation(hhi[:, k, :], ps[:, 4 + b, kk * S:(kk + 1) * S], ACT.Copy)
                    m.then_inc(ht_hi, 1)

            act.wait_ge(ident_in, 32)
            for layer in range(DEPTH):
                L = layer + 1
                for s in range(2):
                    hi_of(act, layer, "A", s)
                turned_hi(3 * layer, ht_turned, 8 * layer, lambda k: par("norm1", layer * KD + k))
                for s in range(2, 5):
                    hi_of(act, layer, "A", s)
                act.wait_ge(conv_y, L)
                nc.scalar.activation(w4b[:, :, :], w4b[:, :, :], ACT.Silu).then_inc(conv_act, 1)
                hi_of(act, layer, "A", 5)
                if layer == 0:
                    act.wait_ge(consts_in, 16)
                act.wait_ge(row_abs, L)
                nc.scalar.activation(rowt[:, 2, :], rowt[:, 3, :], ACT.Exp, scale=-1.0).then_inc(row_exp, 1)
                act.wait_ge(row_exp, L)
                nc.scalar.activation(rowt[:, 3, :], rowt[:, 2, :], ACT.Ln, bias=ones[0:MH, 0:1]).then_inc(row_ln, 1)
                with act.Fori(0, (N_LOOP - 2) // 3) as i:
                    for s in range(6, 6 + ROUND):
                        hi_of(act, layer, "A", s, i)

                def silu_rg():
                    act.wait_ge(z_out, layer * Q_G + Z_DQ // C)
                    nc.scalar.activation(z[:, :, Z_RG:Z_DQ], z[:, :, Z_RG:Z_DQ], ACT.Silu).then_inc(rg_act, 1)

                def da_squares():
                    act.wait_ge(z_out, layer * Q_G + Z_DV // C)
                    act.wait_ge(rows_ok, L)
                    nc.scalar.activation(w2[:, :], z[:, 0, Z_DQ:Z_DV], ACT.Square)
                    nc.scalar.activation(w1[:, 0:BLK * 4], z[:, 1, Z_DQ:Z_DV], ACT.Square).then_inc(dsq, 1)

                def col_exp_():
                    act.wait_ge(col_sb, L)
                    nc.scalar.activation(emcol, emcol, ACT.Exp).then_inc(col_exp, 1)

                def ret_turned():
                    act.wait_ge(rqk_t, L)
                    act.wait_ge(dsum, L)
                    for b in range(4):
                        m = nc.scalar.activation(qk[:, 2 * b:2 * b + 2, :],
                                                 ps[:, 4 + b, :].rearrange("p (c s) -> p c s", c=2), ACT.Copy)
                    m.then_inc(rqk_sb, 1)

                def ret_squares():
                    act.wait_ge(rpv_mm, L)
                    for t in range(TT):
                        m = nc.scalar.activation(big2[:, t, :], ps[:, 4 + t, :], ACT.Square)
                    m.then_inc(rpv_sq, 1)

                def da_turned(g):
                    act.wait_ge(dqk_t, layer * NG + g + 1)
                    for b, w in enumerate(("qn", "kn")):
                        m = nc.scalar.activation(qk[:, 2 * b:2 * b + 2, :],
                                                 ps[:, 4 + b, :].rearrange("p (c s) -> p c s", c=2), ACT.Copy,
                                                 scale=par(w, layer))
                    m.then_inc(dqk_sb, 1)

                def da_exp(g):
                    act.wait_ge(dsc_sb, layer * NG + g + 1)
                    for h in range(GH):
                        for t, o in enumerate((slice(0, P), slice(P, BLK))):
                            m = nc.scalar.activation(blk2[:, h, o], blk2[:, h, o], ACT.Exp, bias=dneg[:, g, t, h:h + 1],
                                                     accum_out=dl[:, g, t, h:h + 1])
                    m.then_inc(dexp, 1)

                def da_turned_p(g):
                    act.wait_ge(dp_t, layer * NG + g + 1)
                    for h in range(GH):
                        m = nc.scalar.activation(blkz[:, h // 2, h % 2, :], ps[:, 4 + h, 0:BLK], ACT.Copy)
                    m.then_inc(dp_sb, 1)

                def ml_decay():
                    act.wait_ge(mdw_in, L)
                    for h in range(MH):
                        for t, o in enumerate((slice(0, S), slice(S, BLK))):
                            m = nc.scalar.activation(blkm[:, h // 2, h % 2, o], blkm[:, h // 2, h % 2, o], ACT.Exp,
                                                     bias=ccol[:, t, h:h + 1])
                    m.then_inc(mdw, 1)

                def gate_out(q, func=ACT.Copy):
                    wait_used(act, layer, "A", 3 + 2 * q)
                    _, c, n = chunk(q)
                    for t in range(TT):
                        m = nc.scalar.activation(z[:, t, c:c + n], ps[:, pair(q) + t, 0:n], func)
                    m.then_inc(g_out, 1)

                def gate_sigmoids():
                    act.wait_ge(g_out, layer * N_G + N_G - 2)
                    v = z[:, :, Z_G:Z_G + (N_G - 2) * C]
                    nc.scalar.activation(v, v, ACT.Sigmoid).then_inc(sig_ok, 1)

                def da_logs():
                    act.wait_ge(dexp, L * NG)
                    nc.scalar.activation(dco[:, :, :, :], dl[:, :, :, :], ACT.Ln).then_inc(dln, 1)

                def da_weights():
                    act.wait_ge(dlse, L)
                    nc.scalar.activation(dco[:, :, :, :], dco[:, :, :, :], ACT.Exp).then_inc(dwt, 1)

                def ml_squares():
                    act.wait_ge(mh_sb, L)
                    nc.scalar.activation(w1[:, 0:TT * 512], big2[:, :, :].rearrange("p t n -> p (t n)"),
                                         ACT.Square).then_inc(msq, 1)

                def sigmoid_mo():
                    act.wait_ge(z_out, L * Q_G)
                    nc.scalar.activation(z[:, :, Z_MO:Z_G], z[:, :, Z_MO:Z_G], ACT.Sigmoid).then_inc(mo_act, 1)

                silu_rg()
                da_squares()
                behind = {
                    (Q_HALF, 0): (col_exp_,), (Q_HALF, 1): (ret_turned,),
                    (Q_MV, 1): (ret_squares,),
                    (Q_MO, 0): (lambda: da_turned(0),), (Q_MO, 1): (sigmoid_mo, lambda: da_exp(0),),
                    (Q_G, 0): (lambda: da_turned_p(0),), (Q_G, 1): (lambda: da_turned(1), lambda: gate_out(Q_G)),
                    (Q_G + 1, 0): (lambda: da_exp(1),), (Q_G + 1, 1): (lambda: da_turned_p(1), lambda: gate_out(Q_G + 1)),
                    (Q_G + 2, 0): (lambda: da_turned(2),), (Q_G + 2, 1): (lambda: da_exp(2), lambda: gate_out(Q_G + 2)),
                    (Q_G + 3, 0): (lambda: da_turned_p(2),), (Q_G + 3, 1): (ml_decay, da_logs, lambda: gate_out(Q_G + 3)),
                    (Q_G + 4, 0): (da_weights,),
                    (Q_G + 4, 1): (lambda: gate_out(Q_G + 4, ACT.Sigmoid), gate_sigmoids),
                    (Q_G + 5, 1): (lambda: gate_out(Q_G + 5, ACT.Sigmoid),),
                }
                for h in range(2):
                    hi_of(act, layer, "A", 2 + 2 * Q_HALF + h)
                for q in range(Q_HALF, N_Q):
                    for h in range(2):
                        hi_of(act, layer, "A", 4 + 2 * q + h)
                        for step in behind.get((q, h), ()):
                            step()
                ml_squares()

                def out_hi(n, bank, dst, k0, scale):
                    act.wait_ge(ot_t, layer * 5 + n + 1)
                    for kk in range(2):
                        src = ps[:, bank, kk * S:(kk + 1) * S]
                        m = nc.scalar.activation(dst[:, k0 + kk, :], src, ACT.Copy, scale=scale(kk)) if scale else \
                            nc.scalar.activation(dst[:, k0 + kk, :], src, ACT.Copy)
                    m.then_inc(ot_hi, 1)
                out_hi(0, 4, hhi, 0, lambda k: par("retn", layer * 4 + k))
                out_hi(1, 5, hhi, 2, lambda k: par("retn", layer * 4 + 2 + k))
                out_hi(2, 6, hhi, 4, None)
                out_hi(3, 7, ahi, 0, lambda k: par("mln", layer * 4 + k))
                out_hi(4, 4, ahi, 2, lambda k: par("mln", layer * 4 + 2 + k))
                for s in range(S_BR + 2, S_BR + 8):
                    hi_of(act, layer, "A", s)
                turned_hi(3 * layer + 1, yt_turned, 4 * layer, None)
                hi_of(act, layer, "A", S_BR + 8)
                for s in range(3):
                    hi_of(act, layer, "B", s)
                turned_hi(3 * layer + 2, ht_turned, 8 * layer + 4, lambda k: par("norm2", layer * KD + k))

                if layer == 0:
                    def f_silu(s, i, r=0, n=C):
                        wait_used(act, 0, "B", s, r)
                        if s > 1:
                            act.wait_ge(a_ok, i * 2)
                        for t in range(TT):
                            nc.scalar.activation(sil_sb[:, t, 0:n], ps[:, t, 0:n], ACT.Silu).then_inc(silu, 1)

                    def f_hi(i, n=4):
                        for t in range(TT):
                            act.wait_ge(a_t, i * 2 + t + 1)
                            nc.scalar.activation(ahi[:, 0:n, t * P:(t + 1) * P],
                                                 ps[:, 4 + t, 0:n * P].rearrange("p (k c) -> p k c", k=n),
                                                 ACT.Copy).then_inc(a_hi, 1)

                    def f_round(s, i, r=0, n=C):
                        for k in range(4):
                            hi_of(act, 0, "B", s + k, r)
                        f_hi(i - 1)
                        hi_of(act, 0, "B", s + 4, r)
                        f_silu(s + 1, i, r, n)
                        hi_of(act, 0, "B", s + 5, r)

                    f_silu(1, 0)
                    hi_of(act, 0, "B", 3)
                    f_round(4, 1)
                    with act.Fori(0, F_CHUNKS - 2) as i:
                        f_round(10, i + 2, i)
                    f_round(F_SLOTS - 8, F_CHUNKS, n=HALF)
                    for s in (2, 1):
                        hi_of(act, 0, "B", F_SLOTS - s)
                    f_hi(F_CHUNKS, n=HALF // P)
                    continue

                act.wait_ge(lg_d, 1)
                nc.scalar.activation(v12[:, :, 2:3], v12[:, :, 2:3], ACT.Exp).then_inc(lg_e, 1)

                def gathered_hi(n):
                    act.wait_ge(gather_mm, n + 1)
                    for k in range(KD):
                        m = nc.scalar.activation(hhi[:, k, 0:CAP], ps[:, 5 + k // 4, k % 4 * P:(k % 4 + 1) * P], ACT.Copy,
                                                 scale=par("norm2", KD + k))
                    m.then_inc(gt_hi, 1)

                def e_silu(s, n, r):
                    wait_used(act, 1, "B", s, r)
                    act.wait_ge(a_ok, n + F_TILES)
                    nc.scalar.activation(sil_sb[:, 0, :], ps[:, 0, :], ACT.Silu).then_inc(silu, 1)

                def e_hi(n):
                    act.wait_ge(a_t, n + (F_TILES + 1))
                    nc.scalar.activation(ahi[:, :, 0:CAP], ps[:, 2, :].rearrange("p (k c) -> p k c", k=4),
                                         ACT.Copy).then_inc(a_hi, 1)

                def e_rest(j):
                    n0 = j * E_CHUNKS
                    e_silu(1, n0, n0)
                    hi_of(act, 1, "B", 3, n0)
                    for k in range(2):
                        hi_of(act, 1, "B", 4 + k, n0)
                    act.wait_ge(spread_t, j + 1)
                    nc.scalar.activation(spread[:, :], ps[:, 7, 0:S], ACT.Copy).then_inc(spread_sb, 1)

                    def e_round(s, n, r, ahead):
                        for k in range(ahead, 4):
                            hi_of(act, 1, "B", s + k, r)
                        e_hi(n - 1)
                        hi_of(act, 1, "B", s + 4, r)
                        e_silu(s + 1, n, r)
                        hi_of(act, 1, "B", s + 5, r)
                    e_round(4, n0 + 1, n0, 2)
                    with act.Fori(0, E_CHUNKS - 2) as i:
                        e_round(10, i + n0 + 2, i + n0, 0)
                    for s in (2, 1):
                        hi_of(act, 1, "B", E_SLOTS - s, n0)
                    e_hi(n0 + (E_CHUNKS - 1))

                gathered_hi(0)
                act.wait_ge(route_ok, 1)
                last = act.value_load(eid[0:1, 14:15], min_val=NE - 1, max_val=ITEMS - 1)
                with act.Fori(0, last) as j:
                    e_rest(j)
                    n1 = j * E_CHUNKS + E_CHUNKS
                    wait_used(act, 1, "B", E_SLOTS - 5, j * E_CHUNKS)
                    gathered_hi(j + 1)
                    for s in range(3):
                        hi_of(act, 1, "B", s, n1)
                e_rest(last)

        @block.vector
        def _(dve):
            V = nc.vector
            chained = [0]

            def link(ins):
                chained[0] += 1
                ins.then_inc(dve_chain, 1)
                dve.wait_ge(dve_chain, chained[0])

            def inverse_root(out, total, n):
                width = 1
                for d in out.shape[1:]:
                    width *= d
                v, w = root[:, 0:width], root[:, 64:64 + width]
                if len(out.shape) == 3:
                    v, w = (u.rearrange("p (t n) -> p t n", t=out.shape[1]) for u in (v, w))
                link(V.tensor_scalar(v, total, 1.0 / n, EPS, ALU.mult, ALU.add))
                link(V.tensor_scalar(out.bitcast(I32), v.bitcast(I32), 1, None, ALU.logical_shift_right))
                link(V.tensor_scalar(out.bitcast(I32), out.bitcast(I32), -1.0, float(0x5F3759DF), ALU.mult, ALU.add))
                for _ in range(4):
                    link(V.scalar_tensor_tensor(out=w, in0=out, scalar=-0.5, in1=out, op0=ALU.mult, op1=ALU.mult))
                    link(V.tensor_tensor(w, w, v, ALU.mult))
                    link(V.scalar_tensor_tensor(out=out, in0=w, scalar=1.5, in1=out, op0=ALU.add, op1=ALU.mult))

            def normalise():
                for t in range(TT):
                    link(V.tensor_tensor_reduce(out=w1t[:, t, :], in0=x[:, t, :], in1=x[:, t, :], scale=1.0, scalar=0.0,
                                                op0=ALU.mult, op1=ALU.add, accum_out=ss2[:, t:t + 1]))
                inverse_root(rstd2, ss2, D)
                for t in range(TT):
                    V.tensor_scalar(w1t[:, t, :], x[:, t, :], rstd2[:, t:t + 1], None, ALU.mult).then_inc(tok_ready, 1)

            def minus_hi(out, src, scale, hi):
                if scale is None:
                    return V.tensor_tensor(out, src, hi.bitcast(F32), ALU.subtract)
                return V.scalar_tensor_tensor(out=out, in0=src, scalar=scale, in1=hi.bitcast(F32),
                                              op0=ALU.mult, op1=ALU.subtract)

            def turned_lo(n, scale):
                for b in range(4):
                    dve.wait_ge(ht_hi, 4 * n + b + 1)
                    for kk in range(2):
                        k = 2 * b + kk
                        m = minus_hi(hlo[:, k, :], ps[:, 4 + b, kk * S:(kk + 1) * S], scale and scale(k), hhi[:, k, :])
                    m.then_inc(ht_lo, 1)

            def wide(v, n):
                return v.unsqueeze(len(v.shape)).to_broadcast(list(v.shape) + [n])

            link(V.memset(w4a[:, :, :], 0.0))
            dve.wait_ge(x_in, 16)
            dve.wait_ge(ident_in, 32)
            for layer in range(DEPTH):
                L = layer + 1
                normalise()
                turned_lo(3 * layer, lambda k: par("norm1", layer * KD + k))

                wait_used(dve, layer, "A", 1)
                V.tensor_copy(w4a[:, :, TAPS - 1:], ps[:, 0:4, 0:S]).then_inc(conv_pad, 1)
                dve.wait_ge(conv_pad, L)
                for j in range(TAPS):
                    for c in range(4):
                        tap = par("conv", (layer * 4 + c) * TAPS + j)
                        if j == 0:
                            m = V.tensor_scalar(w4b[:, c, :], w4a[:, c, 0:S], tap, None, ALU.mult)
                        else:
                            m = V.scalar_tensor_tensor(out=w4b[:, c, :], in0=w4a[:, c, j:j + S], scalar=tap,
                                                       in1=w4b[:, c, :], op0=ALU.mult, op1=ALU.add)
                    if j < TAPS - 1:
                        link(m)
                m.then_inc(conv_y, 1)
                dve.wait_ge(z8_mm, L)
                V.tensor_copy(z8, ps[:, 6, 0:16].rearrange("p (t n) -> p t n", t=TT)).then_inc(z8_sb, 1)

                def z_copy(q, r=0):
                    wait_used(dve, layer, "A", 3 + 2 * q, r)
                    _, c, n = chunk(q)
                    dst = z[:, :, c:c + n] if isinstance(r, int) else z[:, :, bass.ds(r * (3 * C) + c, n)]
                    V.tensor_copy(dst, ps[:, pair(q):pair(q) + 2, 0:n]).then_inc(z_out, 1)
                z_copy(0)

                if layer == 0:
                    dve.wait_ge(consts_in, 16)
                dve.wait_ge(row_t, L)
                R = lambda n: rowt[:, n, :]
                V.tensor_scalar(R(0), ps[0:MH, 7, 0:S], par("ib", layer)[0:MH], None, ALU.add)
                link(V.tensor_scalar(R(1), ps[0:MH, 7, S:2 * S], par("fb", layer)[0:MH], None, ALU.add))
                V.scalar_tensor_tensor(out=R(3), in0=R(1), scalar=-1.0, in1=R(1), op0=ALU.mult, op1=ALU.max).then_inc(row_abs, 1)
                dve.wait_ge(row_exp, L)
                link(V.tensor_scalar(R(4), R(2), 1.0, None, ALU.add))
                link(V.tensor_scalar(R(5), R(4), 1.0, None, ALU.subtract))
                link(V.tensor_tensor(R(5), R(2), R(5), ALU.subtract))
                link(V.reciprocal(R(4), R(4)))
                link(V.tensor_tensor(R(5), R(5), R(4), ALU.mult))
                dve.wait_ge(row_ln, L)
                link(V.tensor_tensor(R(3), R(3), R(5), ALU.add))
                V.scalar_tensor_tensor(out=R(1), in0=R(1), scalar=0.0, in1=R(3), op0=ALU.min, op1=ALU.subtract)
                link(V.memset(R(5), 1.0))
                link(V.tensor_tensor_scan(R(4), R(5), R(1), 0.0, ALU.mult, ALU.add))
                link(V.tensor_tensor(rows[:, 0, :], R(0), R(4), ALU.subtract))
                link(V.tensor_tensor_scan(R(2), rows[:, 0, :], rows[:, 0, :], 0.0, ALU.max, ALU.max))
                V.tensor_scalar(rows[:, 1, :], R(2), -1.0, None, ALU.mult)
                V.scalar_tensor_tensor(out=rows[:, 2, :], in0=R(4), scalar=-1.0, in1=R(2), op0=ALU.mult,
                                       op1=ALU.subtract).then_inc(rows_ok, 1)
                z_copy(1)
                with dve.Fori(0, (N_LOOP - 2) // 3) as i:
                    for q in (2, 3, 4):
                        z_copy(q, i)

                dve.wait_ge(dsq, L)
                V.tensor_reduce(dss[:, 0, :], w2[:, :].rearrange("p (h d) -> p h d", d=DH), AX, ALU.add)
                V.tensor_reduce(dss[:, 1, :], w1[:, 0:BLK * 4].rearrange("p (h d) -> p h d", d=DH), AX,
                                ALU.add).then_inc(dsum, 1)
                dve.wait_ge(dsum, L)
                inverse_root(drs, dss, DH)
                for t in range(TT):
                    v = z[:, t, 0:Z_RV].rearrange("p (h f d) -> p h f d", f=2, d=64)
                    x1, x2 = v[:, :, 0, :], v[:, :, 1, :]
                    cos, sin = (rot[:, t, f, :].unsqueeze(1).to_broadcast([P, 8, 64]) for f in range(2))
                    A, B, Cc = (w2[:, n * 512:(n + 1) * 512].rearrange("p (h d) -> p h d", d=64) for n in range(3))
                    V.tensor_tensor(A, x1, cos, ALU.mult)
                    V.tensor_tensor(Cc, x1, sin, ALU.mult)
                    link(V.tensor_tensor(B, x2, sin, ALU.mult))
                    link(V.tensor_tensor(x1, A, B, ALU.subtract))
                    link(V.tensor_tensor(A, x2, cos, ALU.mult))
                    m = V.tensor_tensor(x2, Cc, A, ALU.add)
                    if t == 0:
                        link(m)
                m.then_inc(rotated, 1)
                dve.wait_ge(col_t, L)
                V.tensor_copy(st[:, 20:36], ps[:, 7, 0:16]).then_inc(col_sb, 1)
                for t in range(TT):
                    v = z[:, t, Z_DQ:Z_DV].rearrange("p (h d) -> p h d", d=DH)
                    m = V.tensor_tensor(v, v, wide(drs[:, t, :], DH), ALU.mult)
                m.then_inc(dn_ok, 1)
                z_copy(Q_HALF)

                dve.wait_ge(rsc_mm, L)
                V.tensor_tensor(blk2, ps[:, 4:8, 0:BLK], decay, ALU.mult).then_inc(rsc_sb, 1)
                z_copy(Q_MV)
                dve.wait_ge(rpv_sq, L)
                link(V.tensor_reduce(rss, big2.rearrange("p t (h d) -> p (t h) d", d=RDV), AX, ALU.add))
                inverse_root(rrs, rss, RDV)
                link(V.tensor_tensor(big2.rearrange("p t (h d) -> p t h d", d=RDV),
                                     ps[:, 4:6, :].rearrange("p t (h d) -> p t h d", d=RDV),
                                     wide(rrs.rearrange("p (t h) -> p t h", t=TT), RDV), ALU.mult))
                dve.wait_ge(rg_act, L)
                V.tensor_tensor(z[:, :, Z_RG:Z_DQ], big2, z[:, :, Z_RG:Z_DQ], ALU.mult).then_inc(ro_out, 1)

                def da_masked(g):
                    dve.wait_ge(dsc_mm, layer * NG + g + 1)
                    link(V.scalar_tensor_tensor(out=blk2, in0=ps[:, 4:8, 0:BLK], scalar=DH ** -0.5,
                                                in1=damask[:, g, :].unsqueeze(1).to_broadcast([P, GH, BLK]),
                                                op0=ALU.mult, op1=ALU.add))
                    V.tensor_reduce(dneg[:, g, 0, :], blk2[:, :, 0:P], AX, ALU.max)
                    link(V.tensor_reduce(dneg[:, g, 1, :], blk2[:, :, P:BLK], AX, ALU.max))
                    V.tensor_scalar(dneg[:, g, :, :], dneg[:, g, :, :], -1.0, None, ALU.mult).then_inc(dsc_sb, 1)

                def da_keep(g):
                    dve.wait_ge(dpv_mm, layer * NG + g + 1)
                    V.tensor_copy(z[:, :, Z_DQ + g * GH * DH:Z_DQ + (g + 1) * GH * DH],
                                  ps[:, 6:8, 0:GH * DH]).then_inc(dpv_sb, 1)

                z_copy(Q_MO)
                da_masked(0)
                da_keep(0)
                da_masked(1)
                da_keep(1)
                da_masked(2)
                da_keep(2)
                dve.wait_ge(msel_mm, L)
                sp_ = ps[:, 4:6, :].rearrange("p a (b s) -> p a b s", b=2)
                m_ = lambda o: mlmask[:, o].unsqueeze(1).unsqueeze(1)
                for a_ in range(2):
                    V.tensor_tensor(blkm[:, a_, :, 0:S], sp_[:, a_], mlmask[:, 0:S].unsqueeze(1).to_broadcast([P, 2, S]),
                                    ALU.add)
                    m = V.tensor_tensor(blkm[:, a_, :, S:BLK], sp_[:, a_, :, P:S],
                                        mlmask[:, S:BLK].unsqueeze(1).to_broadcast([P, 2, P]), ALU.add)
                m.then_inc(mdw_in, 1)
                dve.wait_ge(dln, L)
                G = lambda v, g: v[:, g, :, :].rearrange("p t h -> p (t h)")
                over = dtmp.unsqueeze(1).to_broadcast([P, NG, 8])
                flat = lambda v: v.rearrange("p g t h -> p g (t h)")
                link(V.tensor_tensor(flat(dco), flat(dco), flat(dneg), ALU.subtract))
                link(V.tensor_tensor(dtmp, G(dco, 0), G(dco, 1), ALU.max))
                link(V.tensor_tensor(dtmp, dtmp, G(dco, 2), ALU.max))
                V.tensor_tensor(flat(dco), flat(dco), over, ALU.subtract).then_inc(dlse, 1)
                dve.wait_ge(dwt, L)
                link(V.tensor_tensor(dtmp, G(dco, 0), G(dco, 1), ALU.add))
                link(V.tensor_tensor(dtmp, dtmp, G(dco, 2), ALU.add))
                link(V.tensor_tensor(flat(dl), flat(dl), over, ALU.mult))
                link(V.reciprocal(flat(dl), flat(dl)))
                link(V.tensor_tensor(flat(dco), flat(dco), flat(dl), ALU.mult))
                og = [z[:, :, Z_DQ + g * GH * DH:Z_DQ + (g + 1) * GH * DH].rearrange("p t (h d) -> p t h d", d=DH)
                      for g in range(NG)]
                for g in range(NG):
                    m = V.tensor_tensor(og[g], og[g], wide(dco[:, g, :, :], DH), ALU.mult)
                link(m)
                link(V.tensor_tensor(og[0], og[0], og[1], ALU.add))
                V.tensor_tensor(og[0], og[0], og[2], ALU.add).then_inc(do_out, 1)
                dve.wait_ge(msc_mm, L)
                dve.wait_ge(mdw, L)
                for a_ in range(2):
                    m = V.scalar_tensor_tensor(out=blkm[:, a_], in0=ps[:, 4 + 2 * a_:6 + 2 * a_, 0:BLK], scalar=MDK ** -0.5,
                                               in1=blkm[:, a_], op0=ALU.mult, op1=ALU.mult)
                m.then_inc(msc_sb, 1)
                dve.wait_ge(mpv_mm, L)
                dve.wait_ge(col_exp, L)
                link(V.tensor_copy(mden, ps[:, 6, 0:8]))
                link(V.scalar_tensor_tensor(out=mden, in0=mden, scalar=-1.0, in1=mden, op0=ALU.mult, op1=ALU.max))
                link(V.tensor_tensor(mden, mden, emcol, ALU.max))
                link(V.reciprocal(mden, mden))
                V.tensor_tensor(big2.rearrange("p t (h d) -> p t h d", d=MDV),
                                ps[:, 4:6, :].rearrange("p t (h d) -> p t h d", d=MDV),
                                wide(mden.rearrange("p (t h) -> p t h", t=TT), MDV), ALU.mult).then_inc(mh_sb, 1)
                dve.wait_ge(msq, L)
                link(V.tensor_reduce(mss, w1[:, 0:TT * 512].rearrange("p (n d) -> p n d", d=MDV), AX, ALU.add))
                inverse_root(mrs, mss, MDV)
                big2h = big2.rearrange("p t (h d) -> p (t h) d", d=MDV)
                link(V.tensor_tensor(big2h, big2h, wide(mrs, MDV), ALU.mult))
                dve.wait_ge(mo_act, L)
                V.tensor_tensor(z[:, :, Z_MO:Z_G], big2, z[:, :, Z_MO:Z_G], ALU.mult).then_inc(mo_out, 1)

                def out_lo(n, bank, hi, lo, k0, scale):
                    dve.wait_ge(ot_hi, layer * 5 + n + 1)
                    for kk in range(2):
                        m = minus_hi(lo[:, k0 + kk, :], ps[:, bank, kk * S:(kk + 1) * S], scale and scale(kk),
                                     hi[:, k0 + kk, :])
                    m.then_inc(ot_lo, 1)
                out_lo(0, 4, hhi, hlo, 0, lambda k: par("retn", layer * 4 + k))
                out_lo(1, 5, hhi, hlo, 2, lambda k: par("retn", layer * 4 + 2 + k))
                out_lo(2, 6, hhi, hlo, 4, None)
                out_lo(3, 7, ahi, alo, 0, lambda k: par("mln", layer * 4 + k))
                out_lo(4, 4, ahi, alo, 2, lambda k: par("mln", layer * 4 + 2 + k))
                dve.wait_ge(g_out, L * N_G)
                dve.wait_ge(sig_ok, L)
                for n in range(6):
                    if n == 2:
                        dve.wait_ge(br_half, L)
                    else:
                        wait_used(dve, layer, "A", S_BR + (0, 1, 0, 2, 3, 4)[n])
                    v = z[:, :, Z_G + n * C:Z_G + (n + 1) * C]
                    V.tensor_tensor(v, v, ps[:, 2 * (n % 2):2 * (n % 2) + 2, :], ALU.mult).then_inc(br_out, 1)
                dve.wait_ge(br_out, 6 * L)
                part_ = lambda n, t: z[:, t, Z_G + n * D:Z_G + (n + 1) * D]
                for t in range(TT):
                    m = V.tensor_tensor(part_(0, t), part_(0, t), part_(1, t), ALU.add)
                link(m)
                for t in range(TT):
                    V.tensor_tensor(part_(0, t), part_(0, t), part_(2, t), ALU.add).then_inc(tok_ready, 1)
                turned_lo(3 * layer + 1, None)
                for half in range(2):
                    wait_used(dve, layer, "A", S_BR + 6 + 2 * half)
                    v = x[:, :, half * C:(half + 1) * C]
                    m = V.tensor_tensor(v, v, ps[:, 2 * half:2 * half + 2, :], ALU.add)
                link(m)
                normalise()
                turned_lo(3 * layer + 2, lambda k: par("norm2", layer * KD + k))

                if layer == 0:
                    def lo_(s, r=0):
                        lo_of(dve, 0, "B", s, r)

                    def f_mult(s, i, r=0, n=C):
                        wait_used(dve, 0, "B", s, r)
                        dve.wait_ge(silu, i * 2 + 2)
                        if s > 3:
                            dve.wait_ge(a_t, i * 2)
                        for t in range(TT):
                            V.tensor_tensor(act_sb[:, t, 0:n], sil_sb[:, t, 0:n], ps[:, 2 + t, 0:n],
                                            ALU.mult).then_inc(a_ok, 1)

                    def f_lo(i, n=4):
                        for t in range(TT):
                            dve.wait_ge(a_hi, i * 2 + t + 1)
                            minus_hi(alo[:, 0:n, t * P:(t + 1) * P],
                                     ps[:, 4 + t, 0:n * P].rearrange("p (k c) -> p k c", k=n), None,
                                     ahi[:, 0:n, t * P:(t + 1) * P]).then_inc(a_lo, 1)

                    def f_sum(s, half, r=0):
                        wait_used(dve, 0, "B", s, r)
                        for t in range(TT):
                            v = x[:, t, half * C:(half + 1) * C]
                            V.tensor_tensor(v, v, ps[:, 6 - 2 * half + t, :], ALU.add).then_inc(d_out, 1)

                    def f_round(s, i, r=0, before=True):
                        lo_(s, r)
                        f_mult(s - 3 if before else s - 1, i - 1, r)
                        lo_(s + 1, r)
                        if before:
                            f_sum(s - 2, 0, r)
                        lo_(s + 2, r)
                        if before:
                            f_sum(s - 1, 1, r)
                        lo_(s + 3, r)
                        f_lo(i - 1)
                        lo_(s + 4, r)
                        lo_(s + 5, r)

                    for s in range(4):
                        lo_(s)
                    f_round(4, 1, before=False)
                    with dve.Fori(0, F_CHUNKS - 2) as i:
                        f_round(10, i + 2, i)
                    s0 = F_SLOTS - 8
                    f_round(s0, F_CHUNKS)
                    lo_(s0 + 6)
                    f_mult(s0 + 3, F_CHUNKS, n=HALF)
                    lo_(s0 + 7)
                    f_sum(s0 + 4, 0)
                    f_sum(s0 + 5, 1)
                    f_lo(F_CHUNKS, HALF // P)
                    f_sum(s0 + 6, 0)
                    f_sum(s0 + 7, 1)
                    dve.wait_ge(d_out, F_SUMS)
                    continue

                dve.wait_ge(lg_mm, 1)
                link(V.tensor_tensor(lg, ps[:, 0, 0:16].rearrange("p (t n) -> p t n", t=TT),
                                     par("rb", 0, NE).unsqueeze(1).to_broadcast([P, TT, NE]), ALU.add))

                def first_max(src, v, m, cum):
                    link(V.tensor_reduce(v, src, AX, ALU.max))
                    link(V.tensor_tensor(m, src, v.to_broadcast([P, TT, NE]), ALU.is_equal))
                    for t in range(TT):
                        c = V.tensor_tensor_scan(cum[:, t, :], ones[:, 0:NE], m[:, t, :], 0.0, ALU.mult, ALU.add)
                    link(c)
                    link(V.scalar_tensor_tensor(out=m, in0=cum, scalar=1.0, in1=m, op0=ALU.is_equal, op1=ALU.mult))

                first_max(lg, v12[:, :, 0:1], m1, rt)
                link(V.scalar_tensor_tensor(out=rtmp, in0=m1, scalar=-1e30, in1=lg, op0=ALU.mult, op1=ALU.add))
                first_max(rtmp, v12[:, :, 1:2], m2, rt)
                V.tensor_tensor(v12[:, :, 2:3], v12[:, :, 1:2], v12[:, :, 0:1], ALU.subtract).then_inc(lg_d, 1)
                V.tensor_tensor(rt, m1, m2, ALU.add).then_inc(sel_ok, 1)
                V.memset(posx[:, :, :], -1000.0)
                link(V.memset(gatex[:, :, :], 0.0))
                dve.wait_ge(lg_e, 1)
                link(V.tensor_scalar(v12[:, :, 3:4], v12[:, :, 2:3], 1.0, None, ALU.add))
                link(V.reciprocal(v12[:, :, 3:4], v12[:, :, 3:4]))
                link(V.tensor_tensor(v12[:, :, 2:3], v12[:, :, 2:3], v12[:, :, 3:4], ALU.mult))
                V.tensor_tensor(m1, m1, v12[:, :, 3:4].to_broadcast([P, TT, NE]), ALU.mult)
                link(V.tensor_tensor(m2, m2, v12[:, :, 2:3].to_broadcast([P, TT, NE]), ALU.mult))
                link(V.tensor_tensor(gatex[:, :, 0:NE], m1, m2, ALU.add))
                dve.wait_ge(cnt_mm, 1)
                dve.wait_ge(sel_ok, 1)
                link(V.scalar_tensor_tensor(out=posx[:, :, 0:NE], in0=ps[:, 1, 0:16].rearrange("p (t n) -> p t n", t=TT),
                                            scalar=1000.0, in1=rt, op0=ALU.add, op1=ALU.mult))
                link(V.tensor_scalar(posx[:, :, 0:NE], posx[:, :, 0:NE], 1000.0, None, ALU.subtract))
                link(V.tensor_scalar(big, ps[:, 1, 16:24], float(CAP), None, ALU.is_gt))
                link(V.tensor_tensor_scan(rank, ones[:, 0:NE], big, 0.0, ALU.mult, ALU.add))
                link(V.memset(eidf, 0.0))
                V.tensor_copy(eidf[:, 0:NE], iota[:, 0:NE])
                V.tensor_scalar(eidf[:, 14:15], rank[:, NE - 1:NE], float(NE - 1), None, ALU.add)
                link(V.tensor_scalar(eidf[:, 15:16], rank[:, NE - 1:NE], float(NE), None, ALU.add))
                for n in range(EXTRA):
                    link(V.scalar_tensor_tensor(out=selx, in0=rank, scalar=float(n + 1), in1=big,
                                                op0=ALU.is_equal, op1=ALU.mult))

                    def pick_sum(src, dst):
                        link(V.tensor_tensor_reduce(out=cnt, in0=selx, in1=src, scale=1.0, scalar=0.0, op0=ALU.mult,
                                                    op1=ALU.add, accum_out=dst))
                    pick_sum(iota[:, 0:NE], eidf[:, NE + n:NE + n + 1])
                    for t in range(TT):
                        pick_sum(posx[:, t, 0:NE], posx[:, t, NE + n:NE + n + 1])
                        pick_sum(gatex[:, t, 0:NE], gatex[:, t, NE + n:NE + n + 1])
                link(V.tensor_scalar(posx[:, :, NE:NE + EXTRA], posx[:, :, NE:NE + EXTRA], float(CAP), None, ALU.subtract))
                V.memset(yacc, 0.0).then_inc(y_zero, 1)
                V.memset(spread, 0.0).then_inc(spread_sb, 1)
                V.tensor_copy(eid[:, :], eidf[0:1, :]).then_inc(route_ok, 1)

                def picks(n):
                    for t in range(TT):
                        p_ = posx[:, t, bass.ds(n, 1)]
                        V.tensor_scalar(pickg[:, t, :], iota, p_, gatex[:, t, bass.ds(n, 1)], ALU.is_equal, ALU.mult)
                        m = V.tensor_scalar(pick[:, t, :], iota, p_, None, ALU.is_equal)
                    m.then_inc(pick_ok, 1)

                def e_mult(s, n, r):
                    wait_used(dve, 1, "B", s, r)
                    dve.wait_ge(silu, n + (F_TILES + 1))
                    dve.wait_ge(a_t, n + F_TILES)
                    V.tensor_tensor(act_sb[:, 0, :], sil_sb[:, 0, :], ps[:, 1, :], ALU.mult).then_inc(a_ok, 1)

                def e_lo(n):
                    dve.wait_ge(a_hi, n + (F_TILES + 1))
                    minus_hi(alo[:, :, 0:CAP], ps[:, 2, :].rearrange("p (k c) -> p k c", k=4), None,
                             ahi[:, :, 0:CAP]).then_inc(a_lo, 1)

                def e_sum(s, half, r):
                    wait_used(dve, 1, "B", s, r)
                    v = yacc[:, half * C:(half + 1) * C]
                    V.tensor_tensor(v, v, ps[:, 3 + half, :], ALU.add).then_inc(d_out, 1)

                def e_lo_tokens(j):
                    dve.wait_ge(gt_hi, j + 1)
                    for k in range(KD):
                        m = minus_hi(hlo[:, k, 0:CAP], ps[:, 5 + k // 4, k % 4 * P:(k % 4 + 1) * P],
                                     par("norm2", KD + k), hhi[:, k, 0:CAP])
                    m.then_inc(gt_lo, 1)

                def scattered(n):
                    for k, bank in enumerate((7, 3, 4, 2)):
                        dve.wait_ge(scat_mm, n * 4 + k + 1)
                        v = x[:, k // 2, k % 2 * C:(k % 2 + 1) * C]
                        V.tensor_tensor(v, v, ps[:, bank, :], ALU.add).then_inc(d_out, 1)
                    V.memset(yacc, 0.0).then_inc(y_zero, 1)

                def lo_(s, r):
                    lo_of(dve, 1, "B", s, r)

                def e_round(s, n, r, before=True):
                    lo_(s, r)
                    e_mult(s - 3 if before else s - 1, n - 1, r)
                    lo_(s + 1, r)
                    if before:
                        e_sum(s - 2, 0, r)
                    lo_(s + 2, r)
                    if before:
                        e_sum(s - 1, 1, r)
                    lo_(s + 3, r)
                    e_lo(n - 1)
                    lo_(s + 4, r)
                    lo_(s + 5, r)

                def e_rest(j):
                    n0 = j * E_CHUNKS
                    for s in (2, 3):
                        lo_(s, n0)
                    scattered(j)
                    dve.wait_ge(y_zero, j + 2)
                    e_round(4, n0 + 1, n0, before=False)
                    dve.wait_ge(spread_t, j + 1)
                    picks(j + 1)
                    with dve.Fori(0, E_CHUNKS - 2) as i:
                        e_round(10, i + n0 + 2, i + n0)
                    lo_(E_SLOTS - 2, n0)
                    e_mult(E_SLOTS - 5, n0 + (E_CHUNKS - 1), n0)
                    lo_(E_SLOTS - 1, n0)
                    e_sum(E_SLOTS - 4, 0, n0)
                    e_sum(E_SLOTS - 3, 1, n0)
                    e_lo(n0 + (E_CHUNKS - 1))

                picks(0)
                for s in range(2):
                    lo_(s, 0)
                e_lo_tokens(0)
                dve.wait_ge(route_ok, 1)
                last = dve.value_load(eid[0:1, 14:15], min_val=NE - 1, max_val=ITEMS - 1)
                with dve.Fori(0, last) as j:
                    e_rest(j)
                    n0, n1 = j * E_CHUNKS, j * E_CHUNKS + E_CHUNKS
                    lo_(0, n1)
                    e_lo_tokens(j + 1)
                    e_sum(E_SLOTS - 2, 0, n0)
                    lo_(1, n1)
                    e_sum(E_SLOTS - 1, 1, n0)
                e_rest(last)
                e_sum(E_SLOTS - 2, 0, last * E_CHUNKS)
                e_sum(E_SLOTS - 1, 1, last * E_CHUNKS)
                scattered(last + 1)
                dve.wait_ge(y_zero, last + 3)
                V.memset(cnt, 0.0).then_inc(x_end, 1)


def _constants():
    f = np.float32
    c = np.zeros((P, N_CONST), f)

    def put(name, v):
        lo, hi = CONST[name]
        c[:v.shape[0], lo:hi] = v.reshape(v.shape[0], -1)
    put("ident", np.eye(P, dtype=f))
    half = RDV // 2
    inv = np.power(f(10000.0), -np.arange(half, dtype=f) / f(half)).astype(f)
    ang = (np.arange(S, dtype=f)[:, None] * inv[None, :]).astype(f).astype(np.float64)
    rot = np.stack([np.cos(ang), np.sin(ang)], 1).astype(f)
    put("rot", rot.reshape(TT, P, 2, half).transpose(1, 0, 2, 3))
    i = np.arange(S)
    rel = i[None, :] - i[:, None]
    log_gamma = np.log1p(-np.exp2(-5.0 - np.arange(RH)))
    decay = np.where(rel >= 0, np.exp(log_gamma[:, None, None] * np.maximum(rel, 0)), 0.0) * RDV ** -0.5
    put("decay", np.concatenate([decay[:, :P, :], decay[:, P:, P:]], 2).transpose(1, 0, 2).astype(f))
    ok = np.stack([(rel.T >= 0) & (rel.T % d == 0) & (rel.T <= w) for w, d in GROUPS])
    mask = np.where(ok, 0.0, -1e30).astype(f)
    put("damask", np.concatenate([mask[:, :P, :P], mask[:, P:, :]], 2).transpose(1, 0, 2))
    ml = np.where(rel >= 0, 0.0, -1e30).astype(f)
    put("mlmask", np.concatenate([ml[:P, :], ml[P:, P:]], 1))
    put("tri", np.triu(np.ones((P, P), f), 1))
    put("ones", np.ones((P, P), f))
    put("iota", np.broadcast_to(np.arange(P, dtype=f), (P, P)))
    put("sel", np.repeat(np.eye(MH, dtype=f), P, 1))
    return c


def _small(w):
    s = np.zeros((P, N_SMALL), np.float32)

    def put(name, v):
        lo, hi = SMALL[name]
        s[:v.shape[0], lo:hi] = v.reshape(v.shape[0], -1)
    tiles = lambda v: v.reshape(DEPTH, -1, P).transpose(2, 0, 1)
    for name, v in (("norm1", "norm1_w"), ("norm2", "norm2_w"), ("retn", "ret_norm_w"), ("mln", "ml_norm_w")):
        put(name, tiles(w[v]))
    for name, v in (("qn", "da_q_norm_w"), ("kn", "da_k_norm_w")):
        put(name, np.concatenate([w[v], w[v]], 1).T)
    put("conv", w["ml_conv_w"].reshape(DEPTH, TAPS, 4, P).transpose(3, 0, 2, 1))
    put("ib", w["ml_i_bias"].T)
    put("fb", w["ml_f_bias"].T)
    put("rb", np.broadcast_to(w["moe_b_router"], (P, NE)))
    put("gates", w["w_in"][:, :, IN_GATES:IN_G].reshape(DEPTH, KD, P, 8).transpose(2, 0, 1, 3))
    put("router", w["moe_w_router"][0].reshape(KD, P, NE).transpose(1, 0, 2))
    return s


_WHOLE = ["x", "w_in", "w_br_ret", "w_br_da", "w_br_ml", "w_out", "ffn_w_gate", "ffn_w_up", "ffn_w_down",
          "moe_w_gate", "moe_w_up", "moe_w_down"]


def kernel(**inputs):
    from concourse import bacc
    from concourse.bass_utils import run_bass_kernel_spmd

    w = {name: np.ascontiguousarray(v) for name, v in inputs.items()}
    arrays = {name: w[name] for name in _WHOLE}
    arrays["const"], arrays["small"] = _constants(), _small(w)
    nc = bacc.Bacc("TRN2", target_bir_lowering=False, num_devices=1)
    a = {name: nc.dram_tensor(f"in_{name}_dram", v.shape, mybir.dt.from_np(v.dtype), kind="ExternalInput").ap()
         for name, v in arrays.items()}
    a["out"] = nc.dram_tensor("out_dram", w["x"].shape, F32, kind="ExternalOutput").ap()
    build(nc, a)
    r = run_bass_kernel_spmd(nc, [{f"in_{name}_dram": v for name, v in arrays.items()}], core_ids=[0])
    return r.results[0]["out_dram"]
```

```python
from contextlib import ExitStack

import numpy as np
import concourse.bass as bass
from concourse import mybir

F32 = mybir.dt.float32
F32R = mybir.dt.float32r
I32 = mybir.dt.int32
ALU = mybir.AluOpType
ACT = mybir.ActivationFunctionType
AX = mybir.AxisListType.X

P = 128
D = 1024
KD = D // P
S = 256
TT = S // P
DEPTH = 2
EPS = 1e-6
RH, RDV = 4, 128
GROUPS = ((128, 1), (512, 4), (2048, 16))
NG = len(GROUPS)
GH, DH = 4, 64
NH = NG * GH
MH, MDK, MDV = 4, 64, 128
TAPS = 4
FF = 2816
NE, FE = 8, 3584
C = 512
SLOT = 4 * C
KH = KD // 2
BLK = 3 * P

IN_DV_END = 2048 + 3 * NH * DH
IN_QK = IN_DV_END
IN_MV = IN_QK + 2 * MH * MDK
IN_GATES = IN_MV + 2 * MH * MDV
IN_G = IN_GATES + 2 * MH
P_IN = IN_G + 3 * D
Z_RV, Z_RG, Z_DQ = 1024, 1536, 2048
Z_DK = Z_DQ + NH * DH
Z_DV = Z_DK + NH * DH
Z_MV = IN_DV_END
Z_MO = Z_MV + MH * MDV
Z_G = Z_MO + MH * MDV
ZW = Z_G + 3 * D

RING_A, RING_B, RING_L = 2, 6, 3
ROUND = 6
N_LOOP = 8
N_G = 6
A_SLOTS = 2 + 2 * N_LOOP + 6 + 2 * N_G + 2 + 1 + 2 + 4
F_CHUNKS = FF // C
F_SLOTS = 6 * (F_CHUNKS + 1)
E_CHUNKS = FE // C
SHARED_A = (2, 18)
DVE_SHARE = 0.53
E_SLOTS = 6 * E_CHUNKS
F_TILES = TT * (F_CHUNKS + 1)
F_SUMS = 2 * F_TILES
E_SUMS = 2 * E_CHUNKS + 2 * TT
ROT_STEPS = 4
EXTRA = TT * S // P - 1
ITEMS = NE + EXTRA
CAP = P

CONST = {}
SMALL = {}


def _place(table, parts):
    at = 0
    for name, width in parts:
        table[name] = (at, at + width)
        at += width
    return at


N_CONST = _place(CONST, [("ident", P), ("rot", 2 * TT * 64), ("decay", RH * BLK), ("damask", NG * BLK),
                         ("mlmask", BLK), ("tri", P), ("ones", P), ("iota", P), ("sel", MH * P)])
N_SMALL = _place(SMALL, [("norm1", DEPTH * KD), ("norm2", DEPTH * KD), ("retn", DEPTH * 4), ("mln", DEPTH * 4),
                         ("qn", DEPTH), ("kn", DEPTH), ("conv", DEPTH * 4 * TAPS), ("ib", DEPTH), ("fb", DEPTH),
                         ("rb", NE), ("gates", DEPTH * KD * 8), ("router", KD * NE)])


def build(nc, a):
    with ExitStack() as ctx:
        def sb(name, shape, dt=F32):
            return ctx.enter_context(nc.sbuf_tensor("sb_" + name, shape, dt))

        def sem(name):
            return ctx.enter_context(nc.semaphore(name))

        const = sb("const", [P, N_CONST])
        small = sb("small", [P, N_SMALL])
        x = sb("x", [P, TT, D])
        ringa = sb("ringa", [P, RING_A, SLOT])
        z = sb("z", [P, TT, ZW])
        whi = sb("whi", [P, RING_L, SLOT], F32R)
        wlo = sb("wlo", [P, RING_L, SLOT], F32R)
        hhi = sb("hhi", [P, KD, S], F32R)
        hlo = sb("hlo", [P, KD, S], F32R)
        ahi = sb("ahi", [P, 4, S], F32R)
        alo = sb("alo", [P, 4, S], F32R)
        w1 = sb("w1", [P, TT * D])
        w2 = sb("w2", [P, GH * BLK])
        w4a = sb("w4a", [P, 4, S + TAPS - 1])
        w4b = sb("w4b", [P, 4, S])
        rows = sb("rows", [MH, 3, S])
        st = sb("st", [P, 448])
        root = sb("root", [P, 128])
        eid = sb("eid", [1, 16], I32)
        ps = ctx.enter_context(nc.psum_tensor("ps", [P, 8, 512], F32))

        def con(name):
            return const[:, CONST[name][0]:CONST[name][1]]

        def par(name, at, n=1):
            return small[:, SMALL[name][0] + at:SMALL[name][0] + at + n]

        zf = z[:, :, :].rearrange("p t n -> p (t n)")
        ident, tri, ones, iota = con("ident"), con("tri"), con("ones"), con("iota")
        rot = con("rot").rearrange("p (t f d) -> p t f d", t=TT, f=2)
        decay = con("decay").rearrange("p (h n) -> p h n", h=RH)
        damask = con("damask").rearrange("p (g n) -> p g n", g=NG)
        mlmask = con("mlmask")

        def stat(at, n):
            return st[:, at:at + n]
        ss2, rstd2 = stat(0, 2), stat(2, 2)
        z8 = stat(4, 16).rearrange("p (t n) -> p t n", t=TT)
        ccol = stat(20, 8).rearrange("p (t h) -> p t h", t=TT)
        emcol = stat(28, 8)
        rss, rrs = stat(36, 8), stat(44, 8)
        mss, mrs, mden = stat(52, 8), stat(60, 8), stat(68, 8)
        dss = stat(76, 48).rearrange("p (t n) -> p t n", t=TT)
        drs = stat(124, 48).rearrange("p (t n) -> p t n", t=TT)
        dneg = stat(172, 24).rearrange("p (g t h) -> p g t h", g=NG, t=TT)
        dl = stat(196, 24).rearrange("p (g t h) -> p g t h", g=NG, t=TT)
        dco = stat(220, 24).rearrange("p (g t h) -> p g t h", g=NG, t=TT)
        dtmp = stat(244, 8)
        lg = stat(252, 16).rearrange("p (t n) -> p t n", t=TT)
        m1 = stat(268, 16).rearrange("p (t n) -> p t n", t=TT)
        m2 = stat(284, 16).rearrange("p (t n) -> p t n", t=TT)
        rt = stat(300, 16).rearrange("p (t n) -> p t n", t=TT)
        v12 = stat(316, 8).rearrange("p (t n) -> p t n", t=TT)
        posx = stat(324, 24).rearrange("p (t n) -> p t n", t=TT)
        gatex = stat(348, 24).rearrange("p (t n) -> p t n", t=TT)
        cnt, big, rank = stat(372, 8), stat(380, 8), stat(388, 8)
        eidf = stat(396, 16)
        selx = stat(412, 8)
        rtmp = stat(420, 16).rearrange("p (t n) -> p t n", t=TT)

        ssh = stat(436, 2 * TT).rearrange("p (h t) -> p h t", h=2)

        blk2 = w2[:, :].rearrange("p (h n) -> p h n", h=4)
        blkz = z[:, :, 0:2 * BLK].rearrange("p t (h n) -> p t h n", h=2)
        blkm = z[:, :, 2 * BLK:4 * BLK].rearrange("p t (h n) -> p t h n", h=2)
        qk = w1[:, :].rearrange("p (c s) -> p c s", s=S)
        w1t = w1[:, :].rearrange("p (t n) -> p t n", t=TT)
        big1 = w1[:, 0:TT * 512].rearrange("p (t n) -> p t n", t=TT)
        big2 = w1[:, TT * 512:].rearrange("p (t n) -> p t n", t=TT)
        rowt = w2[0:MH, :].rearrange("p (r s) -> p r s", s=S)
        ringb = zf[:, 0:RING_B * SLOT].rearrange("p (r n) -> p r n", r=RING_B)
        spare = zf[:, RING_B * SLOT:]
        y_sb = z[:, :, Z_G:Z_G + D]
        act_sb = spare[:, 0:TT * C].rearrange("p (t n) -> p t n", t=TT)
        sil_sb = spare[:, TT * C:2 * TT * C].rearrange("p (t n) -> p t n", t=TT)
        yacc = spare[:, 2 * TT * C:2 * TT * C + D]
        at = 2 * TT * C + D
        pick, pickg = (spare[:, at + n * TT * CAP:at + (n + 1) * TT * CAP].rearrange("p (t n) -> p t n", t=TT)
                       for n in range(2))
        spread = spare[:, at + 2 * TT * CAP:at + 2 * TT * CAP + S]

        nhi, nlo = (v[:, 0, 0:KD * NE] for v in (ahi, alo))

        raw_a = [sem(f"raw_a{i}") for i in range(RING_A)]
        raw_b = [sem(f"raw_b{i}") for i in range(RING_B)]
        hi_done = sem("hi_done")
        lo_dve = sem("lo_dve")
        split = sem("split")
        narrow_hi, narrow_lo = sem("narrow_hi"), sem("narrow_lo")
        used = sem("used")
        ident_in, consts_in, x_in, out_done = sem("ident_in"), sem("consts_in"), sem("x_in"), sem("out_done")
        dve_chain = sem("dve_chain")
        tok_ready = sem("tok_ready")
        rstd_ok = sem("rstd_ok")
        ht_turned, ht_hi, ht_lo = sem("ht_turned"), sem("ht_hi"), sem("ht_lo")
        yt_turned = sem("yt_turned")
        conv_pad, conv_y, conv_act = (sem(n) for n in ("conv_pad", "conv_y", "conv_act"))
        z8_mm, z8_sb, row_t, row_abs, row_exp, row_ln, rows_ok = (
            sem(n) for n in ("z8_mm", "z8_sb", "row_t", "row_abs", "row_exp", "row_ln", "rows_ok"))
        col_t, col_sb, col_exp = sem("col_t"), sem("col_sb"), sem("col_exp")
        z_out, g_out = sem("z_out"), sem("g_out")
        rg_act, mo_act = sem("rg_act"), sem("mo_act")
        rot_step = sem("rot_step")
        rqk_t, rqk_sb, rsc_mm, rsc_sb, rpv_mm, rpv_sq, ro_out = (
            sem(n) for n in ("rqk_t", "rqk_sb", "rsc_mm", "rsc_sb", "rpv_mm", "rpv_sq", "ro_out"))
        dsq, dsum, dn_ok = sem("dsq"), sem("dsum"), sem("dn_ok")
        dqk_t, dqk_sb, dsc_mm, dsc_sb, dexp, dp_t, dp_sb, dpv_mm, dpv_sb = (
            sem(n) for n in ("dqk_t", "dqk_sb", "dsc_mm", "dsc_sb", "dexp", "dp_t", "dp_sb", "dpv_mm", "dpv_sb"))
        dln, dlse, dwt, do_out = sem("dln"), sem("dlse"), sem("dwt"), sem("do_out")
        msel_mm, mdw_in, mdw, msc_mm, msc_sb, mpv_mm, mh_sb, msq, mo_out = (
            sem(n) for n in ("msel_mm", "mdw_in", "mdw", "msc_mm", "msc_sb", "mpv_mm", "mh_sb", "msq", "mo_out"))
        ot_t, ot_hi, ot_lo, br_half, br_out = (sem(n) for n in ("ot_t", "ot_hi", "ot_lo", "br_half", "br_out"))
        sig_ok, x_end = sem("sig_ok"), sem("x_end")
        silu, a_ok, a_t, a_hi, a_lo, d_out = (sem(n) for n in ("silu", "a_ok", "a_t", "a_hi", "a_lo", "d_out"))
        lg_mm, lg_e, lg_d, sel_ok, cnt_mm, route_ok = (
            sem(n) for n in ("lg_mm", "lg_e", "lg_d", "sel_ok", "cnt_mm", "route_ok"))
        pick_ok, gather_mm, gt_hi, gt_lo, spread_t, spread_sb, scat_mm, y_zero = (
            sem(n) for n in ("pick_ok", "gather_mm", "gt_hi", "gt_lo", "spread_t", "spread_sb", "scat_mm", "y_zero"))

        def number(layer, phase, s, r=0):
            at = layer * (A_SLOTS + F_SLOTS) + (A_SLOTS if phase == "B" else 0) + s
            return r * ROUND + at

        def ordinal(layer, phase, s):
            return layer * (A_SLOTS if phase == "A" else F_SLOTS) + s

        def lane(layer, phase, s):
            return number(layer, phase, s) % RING_L

        def ring(phase):
            return (RING_A, raw_a, ringa[:, :, :]) if phase == "A" else (RING_B, raw_b, ringb)

        def raw_slot(layer, phase, s):
            n, _, tile = ring(phase)
            return tile[:, ordinal(layer, phase, s) % n, :]

        def shared(phase, s):
            return phase == "B" or SHARED_A[0] <= s < SHARED_A[1]

        def dve_number(layer, phase, s, r=0):
            a = SHARED_A[1] - SHARED_A[0]
            if phase == "A":
                return r * ROUND + (layer * (a + F_SLOTS) + s - SHARED_A[0] + 1)
            return r * ROUND + (layer * (a + F_SLOTS) + a + s + 1)

        def wait_lo(eng, layer, phase, s, r=0):
            eng.wait_ge(split, number(layer, phase, s, r) + 1)

        def wait_split(eng, layer, phase, s, r=0):
            size = ring(phase)[0]
            if s >= size or not isinstance(r, int):
                wait_lo(eng, layer, phase, s - size, r)
            elif layer > 0:
                wait_lo(eng, layer - 1, phase, (A_SLOTS if phase == "A" else F_SLOTS) + s - size)

        def hi_of(act, layer, phase, s, r=0):
            size, sems, _ = ring(phase)
            o = ordinal(layer, phase, s)
            act.wait_ge(sems[o % size], (r * (ROUND // size) + (o // size + 1)) * 16)
            if number(layer, phase, s) >= RING_L:
                act.wait_ge(used, number(layer, phase, s, r) + 1 - RING_L)
            n = width(layer, phase, s)
            nc.scalar.activation(whi[:, lane(layer, phase, s), 0:n], raw_slot(layer, phase, s)[:, 0:n],
                                 ACT.Copy).then_inc(hi_done, 1)

        def lo_of(eng, layer, phase, s, r=0):
            k, n = lane(layer, phase, s), width(layer, phase, s)
            cut = int(n * DVE_SHARE) // 4 * 4 if shared(phase, s) else 0
            last = n - n // 16 if cut else 0

            def subtract(c0, c1):
                return eng.tensor_tensor(wlo[:, k, c0:c1], raw_slot(layer, phase, s)[:, c0:c1],
                                         whi[:, k, c0:c1].bitcast(F32), ALU.subtract)
            eng.wait_ge(hi_done, number(layer, phase, s, r) + 1)
            if eng is nc.vector:
                subtract(0, cut).then_inc(lo_dve, 1)
                return
            if cut:
                subtract(cut, last)
                eng.wait_ge(lo_dve, dve_number(layer, phase, s, r))
            subtract(last, n).then_inc(split, 1)

        def wait_used(eng, layer, phase, s, r=0):
            eng.wait_ge(used, number(layer, phase, s, r) + 1)

        Q_HALF, Q_MV, Q_MO, Q_G = N_LOOP, N_LOOP + 1, N_LOOP + 2, N_LOOP + 3
        N_Q = Q_G + N_G
        S_BR = 2 + 2 * N_Q

        def chunk(q):
            if q < N_LOOP:
                return q * C, q * C, C
            if q == Q_HALF:
                return N_LOOP * C, N_LOOP * C, IN_DV_END - N_LOOP * C
            if q <= Q_MO:
                return IN_MV + (q - Q_MV) * C, Z_MV + (q - Q_MV) * C, C
            return IN_G + (q - Q_G) * C, Z_G + (q - Q_G) * C, C

        HALF = FF - F_CHUNKS * C

        def width(layer, phase, s):
            if phase == "A" and 2 <= s < S_BR:
                return KH * chunk((s - 2) // 2)[2]
            if phase == "B" and layer == 0 and s >= F_SLOTS - 8:
                return KH * HALF if s < F_SLOTS - 4 else (SLOT if s < F_SLOTS - 2 else HALF // P * C)
            return SLOT

        block = ctx.enter_context(nc.Block())

        @block.sync
        def _(sp):
            def load(layer, phase, s, src, r=0, k=KH):
                wait_split(sp, layer, phase, s, r)
                size, sems, _ = ring(phase)
                dst = raw_slot(layer, phase, s)[:, 0:width(layer, phase, s)].rearrange("p (k n) -> p k n", k=k)
                sp.dma_start(dst, src).then_inc(sems[ordinal(layer, phase, s) % size], 16)

            def part(w, k0, kn, c0, n):
                return w[k0 * P:(k0 + kn) * P, c0:c0 + n].rearrange("(k p) n -> p k n", p=P)

            def run(w, k0, kn, c0, n):
                return w[k0 * P:(k0 + kn) * P, bass.ds(c0, n)].rearrange("(k p) n -> p k n", p=P)

            sp.dma_start(x[:, :, :], a["x"].rearrange("b (t p) d -> p (b t) d", p=P)).then_inc(x_in, 16)
            sp.dma_start(const[:, 0:P], a["const"][:, 0:P]).then_inc(ident_in, 16)
            sp.dma_start(small[:, :], a["small"]).then_inc(ident_in, 16)

            for layer in range(DEPTH):
                w_in = a["w_in"][layer]
                for h in range(2):
                    load(layer, "A", h, part(w_in, KH * h, KH, IN_QK, C))
                if layer == 0:
                    sp.dma_start(const[:, P:], a["const"][:, P:]).then_inc(consts_in, 16)
                for s in range(4):
                    load(layer, "A", 2 + s, part(w_in, KH * (s % 2), KH, s // 2 * C, C))
                with sp.Fori(0, (N_LOOP - 2) // 3) as i:
                    for s in range(ROUND):
                        load(layer, "A", 6 + s, run(w_in, KH * (s % 2), KH, i * (3 * C) + (2 + s // 2) * C, C), r=i)
                for q in range(N_LOOP, N_Q):
                    c0, _, n = chunk(q)
                    for h in range(2):
                        load(layer, "A", 2 + 2 * q + h, part(w_in, KH * h, KH, c0, n))
                for h in range(2):
                    load(layer, "A", S_BR + h, part(a["w_br_ret"][layer], 0, 4, h * C, C))
                load(layer, "A", S_BR + 2, part(a["w_br_da"][layer], 0, 2, 0, D), k=2)
                for h in range(2):
                    load(layer, "A", S_BR + 3 + h, part(a["w_br_ml"][layer], 0, 4, h * C, C))
                for s in range(4):
                    load(layer, "A", S_BR + 5 + s, part(a["w_out"][layer], KH * (s % 2), KH, s // 2 * C, C))

                sp.wait_ge(yt_turned, 4 * (layer + 1))
                if layer == 0:
                    gu, wd = (a["ffn_w_gate"][0], a["ffn_w_up"][0]), a["ffn_w_down"][0]
                    for s in range(4):
                        load(0, "B", s, part(gu[s // 2], KH * (s % 2), KH, 0, C))
                    for s in range(4):
                        load(0, "B", 4 + s, part(gu[s // 2], KH * (s % 2), KH, C, C))
                    for h in range(2):
                        load(0, "B", 8 + h, part(wd, 0, 4, h * C, C))
                    with sp.Fori(0, F_CHUNKS - 2) as i:
                        for s in range(4):
                            load(0, "B", 10 + s, run(gu[s // 2], KH * (s % 2), KH, i * C + 2 * C, C), r=i)
                        for h in range(2):
                            load(0, "B", 14 + h, wd[bass.ds(i * C + C, C), h * C:(h + 1) * C]
                                 .rearrange("(k p) n -> p k n", p=P), r=i)
                    s0 = F_SLOTS - 8
                    for s in range(4):
                        load(0, "B", s0 + s, part(gu[s // 2], KH * (s % 2), KH, F_CHUNKS * C, HALF))
                    for h in range(2):
                        load(0, "B", s0 + 4 + h, part(wd, 4 * (F_CHUNKS - 1), 4, h * C, C))
                    for h in range(2):
                        load(0, "B", s0 + 6 + h, part(wd, 4 * F_CHUNKS, HALF // P, h * C, C), k=HALF // P)
                else:
                    gu = [a[n][0].rearrange("e d f -> (e d) f") for n in ("moe_w_gate", "moe_w_up")]
                    wd = a["moe_w_down"][0].rearrange("e f d -> (e f) d")

                    def load_round(e, j):
                        def from_gu(s, c0):
                            return gu[s // 2][bass.ds(e * D + KH * (s % 2) * P, KH * P), c0].rearrange(
                                "(k p) n -> p k n", p=P)

                        def from_d(h, f0):
                            return wd[bass.ds(f0, C), h * C:(h + 1) * C].rearrange("(k p) n -> p k n", p=P)

                        for s in range(4):
                            load(1, "B", s, from_gu(s, slice(0, C)), r=j * E_CHUNKS)
                        with sp.Fori(0, E_CHUNKS - 1) as i:
                            for s in range(4):
                                load(1, "B", 4 + s, from_gu(s, bass.ds(i * C + C, C)), r=i + j * E_CHUNKS)
                            for h in range(2):
                                load(1, "B", 8 + h, from_d(h, i * C + e * FE), r=i + j * E_CHUNKS)
                        for h in range(2):
                            load(1, "B", E_SLOTS - 2 + h, from_d(h, e * FE + (E_CHUNKS - 1) * C), r=j * E_CHUNKS)

                    load_round(0, 0)
                    sp.wait_ge(route_ok, 1)
                    items = sp.value_load(eid[0:1, 15:16], min_val=NE, max_val=ITEMS)
                    with sp.Fori(1, items) as j:
                        load_round(sp.value_load(eid[0:1, bass.ds(j, 1)], min_val=0, max_val=NE - 1), j)
            sp.wait_ge(x_end, 1)
            sp.dma_start(a["out"].rearrange("b (t p) d -> p (b t) d", p=P), x[:, :, :]).then_inc(out_done, 16)
            sp.wait_ge(out_done, 16)

        @block.gpsimd
        def _(pool):
            def split_narrow(n, src):
                pool.tensor_copy(nhi, src).then_inc(narrow_hi, 1)
                pool.wait_ge(narrow_hi, n + 1)
                pool.tensor_tensor(nlo, src, nhi.bitcast(F32), ALU.subtract).then_inc(narrow_lo, 1)

            pool.wait_ge(ident_in, 32)
            for layer in range(DEPTH):
                if layer > 0:
                    wait_used(pool, 0, "B", F_SLOTS - 1)
                split_narrow(layer, par("gates", layer * KD * 8, KD * 8))
                for s in range(6):
                    lo_of(pool, layer, "A", s)
                with pool.Fori(0, (N_LOOP - 2) // 3) as i:
                    for s in range(ROUND):
                        lo_of(pool, layer, "A", 6 + s, i)
                for s in range(2 + 2 * N_LOOP, A_SLOTS):
                    lo_of(pool, layer, "A", s)
                if layer == DEPTH - 1:
                    wait_used(pool, layer, "A", S_BR + 1)
                    split_narrow(DEPTH, par("router", 0, KD * NE))
                if layer == 0:
                    with pool.Fori(0, F_CHUNKS - 1) as i:
                        for s in range(ROUND):
                            lo_of(pool, 0, "B", s, i)
                    for s in range(ROUND * (F_CHUNKS - 1), F_SLOTS):
                        lo_of(pool, 0, "B", s)
                else:
                    with pool.Fori(0, E_CHUNKS) as i:
                        for s in range(ROUND):
                            lo_of(pool, 1, "B", s, i)
                    pool.wait_ge(route_ok, 1)
                    items = pool.value_load(eid[0:1, 15:16], min_val=NE, max_val=ITEMS)
                    with pool.Fori(E_CHUNKS, items * E_CHUNKS) as i:
                        for s in range(ROUND):
                            lo_of(pool, 1, "B", s, i)

        def pair(q):
            return 2 * (q % 3) if q < N_LOOP else 2 * (q % 2)

        @block.tensor
        def _(pe):
            def mm3(out, lh, ll, rh, rl, start, stop):
                nc.tensor.matmul(out, lh, rh, start=start, stop=False)
                nc.tensor.matmul(out, ll, rh, start=False, stop=False)
                return nc.tensor.matmul(out, lh, rl, start=False, stop=stop)

            def mm(out, l, r, start=True, stop=True):
                return nc.tensor.matmul(out, l, r, start=start, stop=stop)

            def turn(out, src):
                n = src.shape[0]
                return nc.tensor.transpose(out, src, ident[0:n, 0:n])

            def product(layer, phase, s, r, banks, lhs, rows0, first, last, n=C, k=KH):
                wait_lo(pe, layer, phase, s, r)
                ln = lane(layer, phase, s)
                hi = whi[:, ln, 0:k * n].rearrange("p (k n) -> p k n", k=k)
                lo = wlo[:, ln, 0:k * n].rearrange("p (k n) -> p k n", k=k)
                lh, ll = lhs
                for t, b in enumerate(banks):
                    for kk in range(k):
                        m = mm3(ps[:, b, 0:n], lh[:, rows0 + kk, t * P:(t + 1) * P],
                                      ll[:, rows0 + kk, t * P:(t + 1) * P], hi[:, kk, :], lo[:, kk, :],
                                      first and kk == 0, last and kk == k - 1)
                m.then_inc(used, 1)

            def turn_tokens(src, done, banks=range(4)):
                for b in banks:
                    for kk in range(2):
                        for t in range(TT):
                            m = turn(ps[:, 4 + b, kk * S + t * P:kk * S + (t + 1) * P],
                                     src[:, t, (2 * b + kk) * P:(2 * b + kk + 1) * P])
                    m.then_inc(done, 1)

            pe.wait_ge(ident_in, 32)
            for layer in range(DEPTH):
                L = layer + 1

                pe.wait_ge(tok_ready, 2 * (3 * layer + 1))
                if layer > 0:
                    pe.wait_ge(d_out, 4 * (F_CHUNKS + 1))
                turn_tokens(w1t, ht_turned)

                for s in range(2):
                    pe.wait_ge(ht_lo, 4 * (3 * layer) + 2 * s + 2)
                    wait_lo(pe, layer, "A", s)
                    hi, lo = (w[:, lane(layer, "A", s), :].rearrange("p (k n) -> p k n", n=C) for w in (whi, wlo))
                    for c in range(4):
                        for kk in range(KH):
                            m = mm3(ps[:, c, 0:S], hi[:, kk, c * P:(c + 1) * P], lo[:, kk, c * P:(c + 1) * P],
                                    hhi[:, KH * s + kk, :], hlo[:, KH * s + kk, :],
                                    s == 0 and kk == 0, s == 1 and kk == KH - 1)
                    m.then_inc(used, 1)
                pe.wait_ge(narrow_lo, layer + 1)
                for t in range(TT):
                    for k in range(KD):
                        m = mm3(ps[:, 6, t * 8:t * 8 + 8], hhi[:, k, t * P:(t + 1) * P], hlo[:, k, t * P:(t + 1) * P],
                                nhi[:, k * 8:k * 8 + 8], nlo[:, k * 8:k * 8 + 8], k == 0, k == KD - 1)
                m.then_inc(z8_mm, 1)

                def z_chunk(q, h, r=0):
                    if h == 0:
                        if q < 2:
                            pe.wait_ge(conv_pad, L)
                        elif q <= Q_G + 1:
                            pe.wait_ge(z_out, r * 3 + (layer * Q_G + q - 1))
                        else:
                            pe.wait_ge(g_out, layer * N_G + q - 1 - Q_G)
                    b, n = pair(q), chunk(q)[2]
                    product(layer, "A", 2 + 2 * q + h, r, (b, b + 1), (hhi, hlo), KH * h, h == 0, h == 1, n)

                z_chunk(0, 0)
                z_chunk(0, 1)
                pe.wait_ge(z8_sb, L)
                for g in range(2):
                    for t in range(TT):
                        m = turn(ps[0:MH, 7, g * S + t * P:g * S + (t + 1) * P], z8[:, t, g * MH:(g + 1) * MH])
                m.then_inc(row_t, 1)
                z_chunk(1, 0)
                z_chunk(1, 1)
                with pe.Fori(0, (N_LOOP - 2) // 3) as i:
                    for q in (2, 3, 4):
                        z_chunk(q, 0, i)
                        z_chunk(q, 1, i)

                def ml_columns():
                    if layer == 0:
                        pe.wait_ge(consts_in, 16)
                    pe.wait_ge(rows_ok, L)
                    for g, row in enumerate((0, 2)):
                        for t in range(TT):
                            m = turn(ps[:, 7, g * 8 + t * 4:g * 8 + t * 4 + 4], rows[:, row, t * P:(t + 1) * P])
                    m.then_inc(col_t, 1)

                def ret_turn():
                    pe.wait_ge(rot_step, L * TT * ROT_STEPS)
                    for c in range(8):
                        if c == 6:
                            pe.wait_ge(col_sb, L)
                        for t in range(TT):
                            m = turn(ps[:, 4 + c // 2, c % 2 * S + t * P:c % 2 * S + (t + 1) * P],
                                     z[:, t, c * P:(c + 1) * P])
                    m.then_inc(rqk_t, 1)

                def ret_scores():
                    pe.wait_ge(rqk_sb, L)
                    for h in range(RH):
                        mm(ps[:, 4 + h, 0:S], qk[:, RH + h, 0:P], qk[:, h, :])
                        m = mm(ps[:, 4 + h, S:BLK], qk[:, RH + h, P:S], qk[:, h, P:S])
                    m.then_inc(rsc_mm, 1)

                def weighted(bank0, src, vcol, width, m_of=None):
                    for h in range(4):
                        o = slice(h * width, (h + 1) * width)
                        v = [z[:, t, vcol + h * width:vcol + (h + 1) * width] for t in range(TT)]
                        mm(ps[:, bank0, o], src(h)[:, 0:P], v[0])
                        mm(ps[:, bank0 + 1, o], src(h)[:, P:S], v[0], stop=False)
                        m = mm(ps[:, bank0 + 1, o], src(h)[:, S:BLK], v[1], start=False)
                    return m

                def ret_out():
                    pe.wait_ge(rsc_sb, L)
                    weighted(4, lambda h: blk2[:, h, :], Z_RV, RDV).then_inc(rpv_mm, 1)

                def da_turn(g):
                    if g == 0:
                        pe.wait_ge(dn_ok, L)
                        pe.wait_ge(ro_out, L)
                    else:
                        pe.wait_ge(dp_sb, layer * NG + g)
                    for b, col in enumerate((Z_DQ, Z_DK)):
                        for c in range(2):
                            for t in range(TT):
                                m = turn(ps[:, 4 + b, c * S + t * P:c * S + (t + 1) * P],
                                         z[:, t, col + (2 * g + c) * P:col + (2 * g + c + 1) * P])
                    m.then_inc(dqk_t, 1)

                def da_scores(g):
                    pe.wait_ge(dqk_sb, layer * NG + g + 1)
                    if g > 0:
                        pe.wait_ge(dpv_sb, layer * NG + g)
                    else:
                        pe.wait_ge(ot_lo, layer * 5 + 2)
                    for h in range(GH):
                        r = slice(h % 2 * DH, (h % 2 + 1) * DH)
                        q, k = qk[r, h // 2, :], qk[r, 2 + h // 2, :]
                        mm(ps[:, 4 + h, 0:P], q[:, 0:P], k[:, 0:P])
                        m = mm(ps[:, 4 + h, P:BLK], q[:, P:S], k)
                    m.then_inc(dsc_mm, 1)

                def da_turn_p(g):
                    for h in range(GH):
                        if h % 2 == 0:
                            pe.wait_ge(dexp, 2 * (layer * NG + g) + h // 2 + 1)
                        for j in range(3):
                            m = turn(ps[:, 4 + h, j * P:(j + 1) * P], blk2[:, h, j * P:(j + 1) * P])
                    m.then_inc(dp_t, 1)

                def da_out(g):
                    pe.wait_ge(dp_sb, layer * NG + g + 1)
                    weighted(6, lambda h: blkz[:, h // 2, h % 2, :], Z_DV + g * GH * DH, DH).then_inc(dpv_mm, 1)

                def ml_spread():
                    for h in range(MH):
                        m = mm(ps[:, 4 + h // 2, h % 2 * S:(h % 2 + 1) * S], con("sel")[0:MH, h * P:(h + 1) * P],
                               rows[:, 1, :])
                    m.then_inc(msel_mm, 1)

                def ml_scores():
                    pe.wait_ge(conv_act, L)
                    pe.wait_ge(mdw_in, L)
                    pe.wait_ge(dpv_sb, L * NG)
                    for h in range(MH):
                        r = slice(h % 2 * MDK, (h % 2 + 1) * MDK)
                        q, k = w4b[r, h // 2, :], w4b[r, 2 + h // 2, :]
                        mm(ps[:, 4 + h, 0:S], k[:, 0:P], q)
                        m = mm(ps[:, 4 + h, S:BLK], k[:, P:S], q[:, P:S])
                    m.then_inc(msc_mm, 1)

                def ml_out():
                    pe.wait_ge(msc_sb, L)
                    s = lambda h: blkm[:, h // 2, h % 2, :]
                    weighted(4, s, Z_MV, MDV)
                    one = ones[:, 0:1]
                    for h in range(MH):
                        mm(ps[:, 6, h:h + 1], s(h)[:, 0:P], one)
                        mm(ps[:, 6, MH + h:MH + h + 1], s(h)[:, P:S], one, stop=False)
                        m = mm(ps[:, 6, MH + h:MH + h + 1], s(h)[:, S:BLK], one, start=False)
                    m.then_inc(mpv_mm, 1)

                def turn_out(n, bank, col):
                    for kk in range(2):
                        for t in range(TT):
                            m = turn(ps[:, bank, kk * S + t * P:kk * S + (t + 1) * P],
                                     z[:, t, col + kk * P:col + (kk + 1) * P])
                    m.then_inc(ot_t, 1)

                def ret_turn_out():
                    turn_out(0, 6, Z_RG)
                    turn_out(1, 7, Z_RG + 2 * P)

                behind = {
                    (Q_HALF, 0): (ml_columns, ret_turn), (Q_HALF, 1): (ret_scores,),
                    (Q_MV, 0): (ret_out,),
                    (Q_MO, 0): (lambda: da_turn(0), ret_turn_out), (Q_MO, 1): (lambda: da_scores(0),),
                    (Q_G, 0): (lambda: da_turn_p(0),), (Q_G, 1): (lambda: da_turn(1), lambda: da_out(0)),
                    (Q_G + 1, 0): (lambda: da_scores(1),), (Q_G + 1, 1): (lambda: da_turn_p(1),),
                    (Q_G + 2, 0): (lambda: da_turn(2), lambda: da_out(1)), (Q_G + 2, 1): (lambda: da_scores(2),),
                    (Q_G + 3, 0): (lambda: da_turn_p(2),), (Q_G + 3, 1): (lambda: da_out(2), ml_spread),
                    (Q_G + 4, 0): (ml_scores,), (Q_G + 4, 1): (ml_out,),
                }
                for q in range(Q_HALF, N_Q):
                    for h in range(2):
                        z_chunk(q, h)
                        for step in behind.get((q, h), ()):
                            step()

                def branch(slot, bank, lhs):
                    product(layer, "A", S_BR + slot, 0, (bank, bank + 1), lhs, 0, True, True)
                pe.wait_ge(do_out, L)
                turn_out(2, 7, Z_DQ)
                pe.wait_ge(g_out, L * N_G - 1)
                branch(0, 2, (ahi, alo))
                pe.wait_ge(mo_out, L)
                turn_out(3, 4, Z_MO)
                turn_out(4, 5, Z_MO + 2 * P)
                pe.wait_ge(g_out, L * N_G)
                branch(1, 0, (ahi, alo))
                pe.wait_ge(ot_lo, layer * 5 + 3)
                wait_lo(pe, layer, "A", S_BR + 2)
                ln = lane(layer, "A", S_BR + 2)
                hi, lo = (w[:, ln, :].rearrange("p (k n) -> p k n", k=2) for w in (whi, wlo))
                for half in range(2):
                    pe.wait_ge(br_out, layer * 6 + 1 + half)
                    for t in range(TT):
                        for kk in range(2):
                            m = mm3(ps[:, 2 * (1 - half) + t, :], hhi[:, 4 + kk, t * P:(t + 1) * P],
                                    hlo[:, 4 + kk, t * P:(t + 1) * P], hi[:, kk, half * C:(half + 1) * C],
                                    lo[:, kk, half * C:(half + 1) * C], kk == 0, kk == 1)
                    m.then_inc(used if half else br_half, 1)
                pe.wait_ge(ot_lo, layer * 5 + 5)
                for half in range(2):
                    pe.wait_ge(br_out, layer * 6 + 3 + half)
                    branch(3 + half, 2 * (1 - half), (hhi, hlo))

                for half in range(2):
                    for kh in range(2):
                        if half == 0:
                            pe.wait_ge(tok_ready, 2 * (3 * layer + 1) + kh + 1)
                            turn_tokens(y_sb, yt_turned, (2 * kh, 2 * kh + 1))
                            pe.wait_ge(ht_lo, 4 * (3 * layer + 1) + 2 * kh + 2)
                        if kh == 0:
                            pe.wait_ge(br_out, layer * 6 + 5 + half)
                        product(layer, "A", S_BR + 5 + 2 * half + kh, 0, (2 * (1 - half), 2 * (1 - half) + 1),
                                (hhi, hlo), KH * kh, kh == 0, kh == 1)

                pe.wait_ge(tok_ready, 2 * (3 * layer + 3))
                turn_tokens(w1t, ht_turned)
                pe.wait_ge(ht_lo, 4 * (3 * layer + 2) + 2)
                if layer == 0:
                    def f_gate(s, i, r=0, n=C):
                        if s > 0:
                            pe.wait_ge(silu, i * 2)
                        for h in range(2):
                            if s == 0 and h == 1:
                                pe.wait_ge(ht_lo, 4 * 3)
                            product(0, "B", s + h, r, (0, 1), (hhi, hlo), KH * h, h == 0, h == 1, n)

                    def f_up(s, i, r=0, n=C):
                        if s > 2:
                            pe.wait_ge(a_ok, i * 2)
                        for h in range(2):
                            product(0, "B", s + h, r, (2, 3), (hhi, hlo), KH * h, h == 0, h == 1, n)

                    def f_turn(i, n=4, first=False):
                        pe.wait_ge(a_ok, i * 2 + 2)
                        if not first:
                            pe.wait_ge(d_out, i * 4)
                        for t in range(TT):
                            for k in range(n):
                                m = turn(ps[:, 4 + t, k * P:(k + 1) * P], act_sb[:, t, k * P:(k + 1) * P])
                            m.then_inc(a_t, 1)

                    def f_down(s, i, r=0, k=4):
                        pe.wait_ge(a_lo, i * 2 + 2)
                        for h in range(2):
                            product(0, "B", s + h, r, (6 - 2 * h, 7 - 2 * h), (ahi, alo), 0, True, True, k=k)

                    f_gate(0, 0)
                    f_up(2, 0)
                    f_gate(4, 1)
                    f_turn(0, first=True)
                    f_up(6, 1)
                    f_down(8, 0)
                    with pe.Fori(0, F_CHUNKS - 2) as i:
                        f_gate(10, i + 2, i)
                        f_turn(i + 1)
                        f_up(12, i + 2, i)
                        f_down(14, i + 1, i)
                    s = F_SLOTS - 8
                    f_gate(s, F_CHUNKS, n=HALF)
                    f_turn(F_CHUNKS - 1)
                    f_up(s + 2, F_CHUNKS, n=HALF)
                    f_down(s + 4, F_CHUNKS - 1)
                    f_turn(F_CHUNKS, n=HALF // P)
                    f_down(s + 6, F_CHUNKS, k=HALF // P)
                    continue

                pe.wait_ge(narrow_lo, DEPTH + 1)
                for t in range(TT):
                    for k in range(KD):
                        if t == 0 and k == KH:
                            pe.wait_ge(ht_lo, 4 * (3 * layer + 3))
                        m = mm3(ps[:, 0, t * NE:(t + 1) * NE], hhi[:, k, t * P:(t + 1) * P],
                                hlo[:, k, t * P:(t + 1) * P], nhi[:, k * NE:(k + 1) * NE], nlo[:, k * NE:(k + 1) * NE],
                                k == 0, k == KD - 1)
                m.then_inc(lg_mm, 1)
                pe.wait_ge(sel_ok, 1)
                mm(ps[:, 1, 0:NE], tri, rt[:, 0, :])
                mm(ps[:, 1, NE:2 * NE], tri, rt[:, 1, :], stop=False)
                mm(ps[:, 1, NE:2 * NE], ones, rt[:, 0, :], start=False)
                mm(ps[:, 1, 2 * NE:3 * NE], ones, rt[:, 0, :], stop=False)
                mm(ps[:, 1, 2 * NE:3 * NE], ones, rt[:, 1, :], start=False).then_inc(cnt_mm, 1)

                def e_gate(s, n, r):
                    pe.wait_ge(silu, n + F_TILES)
                    for h in range(2):
                        product(1, "B", s + h, r, (0,), (hhi, hlo), KH * h, h == 0, h == 1)

                def e_up(s, n, r):
                    pe.wait_ge(a_ok, n + F_TILES)
                    for h in range(2):
                        product(1, "B", s + h, r, (1,), (hhi, hlo), KH * h, h == 0, h == 1)

                def e_turn(n, d):
                    pe.wait_ge(a_ok, n + (F_TILES + 1))
                    pe.wait_ge(a_lo, n + F_TILES)
                    pe.wait_ge(d_out, d)
                    for k in range(4):
                        m = turn(ps[:, 2, k * P:(k + 1) * P], act_sb[:, 0, k * P:(k + 1) * P])
                    m.then_inc(a_t, 1)

                def e_down(s, n, d, r):
                    pe.wait_ge(a_lo, n + (F_TILES + 1))
                    pe.wait_ge(d_out, d)
                    for h in range(2):
                        product(1, "B", s + h, r, (3 + h,), (ahi, alo), 0, True, True)

                def gather(n):
                    pe.wait_ge(pick_ok, n + 1)
                    for k in range(KD):
                        for t in range(TT):
                            m = mm(ps[:, 5 + k // 4, k % 4 * P:(k % 4 + 1) * P], w1t[:, t, k * P:(k + 1) * P],
                                   pick[:, t, :], start=t == 0, stop=t == 1)
                    m.then_inc(gather_mm, 1)

                def scatter(n):
                    pe.wait_ge(d_out, n * E_SUMS + F_SUMS)
                    pe.wait_ge(spread_sb, n + 1)
                    for k, bank in enumerate((7, 3, 4, 2)):
                        mm(ps[:, bank, :], spread[:, k // 2 * P:(k // 2 + 1) * P],
                           yacc[:, k % 2 * C:(k % 2 + 1) * C]).then_inc(scat_mm, 1)

                gather(0)
                pe.wait_ge(route_ok, 1)
                items = pe.value_load(eid[0:1, 15:16], min_val=NE, max_val=ITEMS)
                with pe.Fori(0, items) as j:
                    n0, d0 = j * E_CHUNKS, j * E_SUMS + (F_SUMS + 2 * TT)
                    pe.wait_ge(gt_lo, j + 1)
                    e_gate(0, n0, n0)
                    scatter(j)
                    e_up(2, n0, n0)
                    pe.wait_ge(d_out, d0)
                    for t in range(TT):
                        m = turn(ps[:, 7, t * P:(t + 1) * P], pickg[:, t, :])
                    m.then_inc(spread_t, 1)
                    with pe.Fori(0, E_CHUNKS - 1) as i:
                        e_gate(4, n0 + i + 1, n0 + i)
                        e_turn(n0 + i, d0)
                        e_up(6, n0 + i + 1, n0 + i)
                        e_down(8, n0 + i, d0 + i * 2, n0 + i)
                    e_turn(n0 + (E_CHUNKS - 1), d0)
                    gather(j + 1)
                    e_down(E_SLOTS - 2, n0 + (E_CHUNKS - 1), d0 + 2 * (E_CHUNKS - 1), n0)
                scatter(items)

        @block.scalar
        def _(act):
            def turned_hi(done, dcount, scale, banks=range(4)):
                for b in banks:
                    act.wait_ge(done, dcount + b + 1)
                    for kk in range(2):
                        k = 2 * b + kk
                        m = nc.scalar.activation(hhi[:, k, :], ps[:, 4 + b, kk * S:(kk + 1) * S], ACT.Copy,
                                                 scale=scale(k)) if scale else \
                            nc.scalar.activation(hhi[:, k, :], ps[:, 4 + b, kk * S:(kk + 1) * S], ACT.Copy)
                    m.then_inc(ht_hi, 1)

            def scale_tokens(n):
                act.wait_ge(rstd_ok, n + 1)
                nc.scalar.activation(w1t[:, 1, :], x[:, 1, :], ACT.Copy, scale=rstd2[:, 1:2]).then_inc(tok_ready, 1)

            act.wait_ge(ident_in, 32)
            for layer in range(DEPTH):
                L = layer + 1
                if layer == 0:
                    scale_tokens(0)
                for s in range(2):
                    hi_of(act, layer, "A", s)
                if layer > 0:
                    scale_tokens(2 * layer)
                turned_hi(ht_turned, 8 * layer, lambda k: par("norm1", layer * KD + k))
                for s in range(2, 5):
                    hi_of(act, layer, "A", s)
                act.wait_ge(conv_y, L)
                nc.scalar.activation(w4b[:, :, :], w4b[:, :, :], ACT.Silu).then_inc(conv_act, 1)
                hi_of(act, layer, "A", 5)
                if layer == 0:
                    act.wait_ge(consts_in, 16)
                act.wait_ge(row_abs, L)
                nc.scalar.activation(rowt[:, 2, :], rowt[:, 3, :], ACT.Exp, scale=-1.0).then_inc(row_exp, 1)
                act.wait_ge(row_exp, L)
                nc.scalar.activation(rowt[:, 3, :], rowt[:, 2, :], ACT.Ln, bias=ones[0:MH, 0:1]).then_inc(row_ln, 1)
                with act.Fori(0, (N_LOOP - 2) // 3) as i:
                    for s in range(6, 6 + ROUND):
                        hi_of(act, layer, "A", s, i)

                def silu_rg():
                    act.wait_ge(z_out, layer * Q_G + Z_DQ // C)
                    nc.scalar.activation(z[:, :, Z_RG:Z_DQ], z[:, :, Z_RG:Z_DQ], ACT.Silu).then_inc(rg_act, 1)

                def da_squares():
                    act.wait_ge(z_out, layer * Q_G + Z_DV // C)
                    act.wait_ge(rot_step, L * TT * ROT_STEPS)
                    nc.scalar.activation(w2[:, :], z[:, 0, Z_DQ:Z_DV], ACT.Square)
                    nc.scalar.activation(w1[:, 0:BLK * 4], z[:, 1, Z_DQ:Z_DV], ACT.Square).then_inc(dsq, 1)

                def col_exp_():
                    act.wait_ge(col_sb, L)
                    nc.scalar.activation(emcol, emcol, ACT.Exp).then_inc(col_exp, 1)

                def ret_turned():
                    act.wait_ge(rqk_t, L)
                    act.wait_ge(dsum, L)
                    for b in range(4):
                        m = nc.scalar.activation(qk[:, 2 * b:2 * b + 2, :],
                                                 ps[:, 4 + b, :].rearrange("p (c s) -> p c s", c=2), ACT.Copy)
                    m.then_inc(rqk_sb, 1)

                def ret_squares():
                    act.wait_ge(rpv_mm, L)
                    for t in range(TT):
                        m = nc.scalar.activation(big2[:, t, :], ps[:, 4 + t, :], ACT.Square)
                    m.then_inc(rpv_sq, 1)

                def da_turned(g):
                    act.wait_ge(dqk_t, layer * NG + g + 1)
                    for b, w in enumerate(("qn", "kn")):
                        m = nc.scalar.activation(qk[:, 2 * b:2 * b + 2, :],
                                                 ps[:, 4 + b, :].rearrange("p (c s) -> p c s", c=2), ACT.Copy,
                                                 scale=par(w, layer))
                    m.then_inc(dqk_sb, 1)

                def da_exp(g):
                    for h in range(GH):
                        if h % 2 == 0:
                            act.wait_ge(dsc_sb, 2 * (layer * NG + g) + h // 2 + 1)
                        for t, o in enumerate((slice(0, P), slice(P, BLK))):
                            m = nc.scalar.activation(blk2[:, h, o], blk2[:, h, o], ACT.Exp, bias=dneg[:, g, t, h:h + 1],
                                                     accum_out=dl[:, g, t, h:h + 1])
                        if h % 2 == 1:
                            m.then_inc(dexp, 1)

                def da_turned_p(g):
                    act.wait_ge(dp_t, layer * NG + g + 1)
                    for h in range(GH):
                        m = nc.scalar.activation(blkz[:, h // 2, h % 2, :], ps[:, 4 + h, 0:BLK], ACT.Copy)
                    m.then_inc(dp_sb, 1)

                def ml_decay():
                    act.wait_ge(mdw_in, L)
                    for h in range(MH):
                        for t, o in enumerate((slice(0, S), slice(S, BLK))):
                            m = nc.scalar.activation(blkm[:, h // 2, h % 2, o], blkm[:, h // 2, h % 2, o], ACT.Exp,
                                                     bias=ccol[:, t, h:h + 1])
                    m.then_inc(mdw, 1)

                def gate_out(q, func=ACT.Copy):
                    wait_used(act, layer, "A", 3 + 2 * q)
                    _, c, n = chunk(q)
                    for t in range(TT):
                        m = nc.scalar.activation(z[:, t, c:c + n], ps[:, pair(q) + t, 0:n], func)
                    m.then_inc(g_out, 1)

                def gate_sigmoids():
                    act.wait_ge(g_out, layer * N_G + N_G - 2)
                    v = z[:, :, Z_G:Z_G + (N_G - 2) * C]
                    nc.scalar.activation(v, v, ACT.Sigmoid).then_inc(sig_ok, 1)

                def da_logs():
                    act.wait_ge(dexp, 2 * L * NG)
                    nc.scalar.activation(dco[:, :, :, :], dl[:, :, :, :], ACT.Ln).then_inc(dln, 1)

                def da_weights():
                    act.wait_ge(dlse, L)
                    nc.scalar.activation(dco[:, :, :, :], dco[:, :, :, :], ACT.Exp).then_inc(dwt, 1)

                def ml_squares():
                    act.wait_ge(mh_sb, L)
                    nc.scalar.activation(w1[:, 0:TT * 512], big2[:, :, :].rearrange("p t n -> p (t n)"),
                                         ACT.Square).then_inc(msq, 1)

                def sigmoid_mo():
                    act.wait_ge(z_out, L * Q_G)
                    nc.scalar.activation(z[:, :, Z_MO:Z_G], z[:, :, Z_MO:Z_G], ACT.Sigmoid).then_inc(mo_act, 1)

                def out_hi(n, bank, dst, k0, scale):
                    act.wait_ge(ot_t, layer * 5 + n + 1)
                    for kk in range(2):
                        src = ps[:, bank, kk * S:(kk + 1) * S]
                        m = nc.scalar.activation(dst[:, k0 + kk, :], src, ACT.Copy, scale=scale(kk)) if scale else \
                            nc.scalar.activation(dst[:, k0 + kk, :], src, ACT.Copy)
                    m.then_inc(ot_hi, 1)

                def ret_out_hi():
                    out_hi(0, 6, ahi, 0, lambda k: par("retn", layer * 4 + k))
                    out_hi(1, 7, ahi, 2, lambda k: par("retn", layer * 4 + 2 + k))

                silu_rg()
                da_squares()
                behind = {
                    (Q_HALF, 0): (ret_turned, col_exp_),
                    (Q_MV, 0): (ret_squares,),
                    (Q_MO, 0): (lambda: da_turned(0), ret_out_hi), (Q_MO, 1): (sigmoid_mo, lambda: da_exp(0),),
                    (Q_G, 0): (lambda: da_turned_p(0),), (Q_G, 1): (lambda: da_turned(1), lambda: gate_out(Q_G)),
                    (Q_G + 1, 0): (lambda: da_exp(1),), (Q_G + 1, 1): (lambda: da_turned_p(1), lambda: gate_out(Q_G + 1)),
                    (Q_G + 2, 0): (lambda: da_turned(2),), (Q_G + 2, 1): (lambda: da_exp(2), lambda: gate_out(Q_G + 2)),
                    (Q_G + 3, 0): (lambda: da_turned_p(2),), (Q_G + 3, 1): (ml_decay, da_logs, lambda: gate_out(Q_G + 3)),
                    (Q_G + 4, 0): (da_weights,),
                    (Q_G + 4, 1): (lambda: gate_out(Q_G + 4, ACT.Sigmoid), gate_sigmoids),
                    (Q_G + 5, 1): (lambda: gate_out(Q_G + 5, ACT.Sigmoid),),
                }
                for h in range(2):
                    hi_of(act, layer, "A", 2 + 2 * Q_HALF + h)
                for q in range(Q_HALF, N_Q):
                    for h in range(2):
                        hi_of(act, layer, "A", 4 + 2 * q + h)
                        for step in behind.get((q, h), ()):
                            step()
                ml_squares()

                wait_used(act, layer, "A", S_BR - 1)
                out_hi(2, 7, hhi, 4, None)
                for s in range(S_BR + 2, S_BR + 4):
                    hi_of(act, layer, "A", s)
                out_hi(3, 4, hhi, 0, lambda k: par("mln", layer * 4 + k))
                out_hi(4, 5, hhi, 2, lambda k: par("mln", layer * 4 + 2 + k))
                for s in range(S_BR + 4, S_BR + 7):
                    hi_of(act, layer, "A", s)
                for half in range(2):
                    turned_hi(yt_turned, 4 * layer, None, (2 * half, 2 * half + 1))
                    hi_of(act, layer, "A", S_BR + 7 + half)
                for s in range(3):
                    hi_of(act, layer, "B", s)
                scale_tokens(2 * layer + 1)
                turned_hi(ht_turned, 8 * layer + 4, lambda k: par("norm2", layer * KD + k))

                if layer == 0:
                    def f_silu(s, i, r=0, n=C):
                        wait_used(act, 0, "B", s, r)
                        if s > 1:
                            act.wait_ge(a_ok, i * 2)
                        for t in range(TT):
                            nc.scalar.activation(sil_sb[:, t, 0:n], ps[:, t, 0:n], ACT.Silu).then_inc(silu, 1)

                    def f_hi(i, n=4):
                        for t in range(TT):
                            act.wait_ge(a_t, i * 2 + t + 1)
                            nc.scalar.activation(ahi[:, 0:n, t * P:(t + 1) * P],
                                                 ps[:, 4 + t, 0:n * P].rearrange("p (k c) -> p k c", k=n),
                                                 ACT.Copy).then_inc(a_hi, 1)

                    def f_round(s, i, r=0, n=C):
                        for k in range(4):
                            hi_of(act, 0, "B", s + k, r)
                        f_hi(i - 1)
                        hi_of(act, 0, "B", s + 4, r)
                        f_silu(s + 1, i, r, n)
                        hi_of(act, 0, "B", s + 5, r)

                    f_silu(1, 0)
                    hi_of(act, 0, "B", 3)
                    f_round(4, 1)
                    with act.Fori(0, F_CHUNKS - 2) as i:
                        f_round(10, i + 2, i)
                    f_round(F_SLOTS - 8, F_CHUNKS, n=HALF)
                    for s in (2, 1):
                        hi_of(act, 0, "B", F_SLOTS - s)
                    f_hi(F_CHUNKS, n=HALF // P)
                    continue

                act.wait_ge(lg_d, 1)
                nc.scalar.activation(v12[:, :, 2:3], v12[:, :, 2:3], ACT.Exp).then_inc(lg_e, 1)

                def gathered_hi(n):
                    act.wait_ge(gather_mm, n + 1)
                    for k in range(KD):
                        m = nc.scalar.activation(hhi[:, k, 0:CAP], ps[:, 5 + k // 4, k % 4 * P:(k % 4 + 1) * P], ACT.Copy,
                                                 scale=par("norm2", KD + k))
                    m.then_inc(gt_hi, 1)

                def e_silu(s, n, r):
                    wait_used(act, 1, "B", s, r)
                    act.wait_ge(a_ok, n + F_TILES)
                    nc.scalar.activation(sil_sb[:, 0, :], ps[:, 0, :], ACT.Silu).then_inc(silu, 1)

                def e_hi(n):
                    act.wait_ge(a_t, n + (F_TILES + 1))
                    nc.scalar.activation(ahi[:, :, 0:CAP], ps[:, 2, :].rearrange("p (k c) -> p k c", k=4),
                                         ACT.Copy).then_inc(a_hi, 1)

                def e_rest(j):
                    n0 = j * E_CHUNKS
                    e_silu(1, n0, n0)
                    hi_of(act, 1, "B", 3, n0)
                    for k in range(2):
                        hi_of(act, 1, "B", 4 + k, n0)
                    act.wait_ge(spread_t, j + 1)
                    nc.scalar.activation(spread[:, :], ps[:, 7, 0:S], ACT.Copy).then_inc(spread_sb, 1)

                    def e_round(s, n, r, ahead):
                        for k in range(ahead, 4):
                            hi_of(act, 1, "B", s + k, r)
                        e_hi(n - 1)
                        hi_of(act, 1, "B", s + 4, r)
                        e_silu(s + 1, n, r)
                        hi_of(act, 1, "B", s + 5, r)
                    e_round(4, n0 + 1, n0, 2)
                    with act.Fori(0, E_CHUNKS - 2) as i:
                        e_round(10, i + n0 + 2, i + n0, 0)
                    for s in (2, 1):
                        hi_of(act, 1, "B", E_SLOTS - s, n0)
                    e_hi(n0 + (E_CHUNKS - 1))

                gathered_hi(0)
                act.wait_ge(route_ok, 1)
                last = act.value_load(eid[0:1, 14:15], min_val=NE - 1, max_val=ITEMS - 1)
                with act.Fori(0, last) as j:
                    e_rest(j)
                    n1 = j * E_CHUNKS + E_CHUNKS
                    wait_used(act, 1, "B", E_SLOTS - 5, j * E_CHUNKS)
                    gathered_hi(j + 1)
                    for s in range(3):
                        hi_of(act, 1, "B", s, n1)
                e_rest(last)

        @block.vector
        def _(dve):
            V = nc.vector
            chained = [0]

            def link(ins):
                chained[0] += 1
                ins.then_inc(dve_chain, 1)
                dve.wait_ge(dve_chain, chained[0])

            def inverse_root(out, total, n, last=link):
                width = 1
                for d in out.shape[1:]:
                    width *= d
                v, w = root[:, 0:width], root[:, 64:64 + width]
                if len(out.shape) == 3:
                    v, w = (u.rearrange("p (t n) -> p t n", t=out.shape[1]) for u in (v, w))
                link(V.tensor_scalar(v, total, 1.0 / n, EPS, ALU.mult, ALU.add))
                link(V.tensor_scalar(out.bitcast(I32), v.bitcast(I32), 1, None, ALU.logical_shift_right))
                link(V.tensor_scalar(out.bitcast(I32), out.bitcast(I32), -1.0, float(0x5F3759DF), ALU.mult, ALU.add))
                for n in range(3):
                    link(V.scalar_tensor_tensor(out=w, in0=out, scalar=-0.5, in1=out, op0=ALU.mult, op1=ALU.mult))
                    link(V.tensor_tensor(w, w, v, ALU.mult))
                    (last if n == 2 else link)(V.scalar_tensor_tensor(out=out, in0=w, scalar=1.5, in1=out, op0=ALU.add,
                                                                      op1=ALU.mult))

            def squares(half):
                for t in range(TT):
                    v = x[:, t, half * C:(half + 1) * C]
                    m = V.tensor_tensor_reduce(out=w1t[:, t, half * C:(half + 1) * C], in0=v, in1=v, scale=1.0,
                                               scalar=0.0, op0=ALU.mult, op1=ALU.add,
                                               accum_out=ssh[:, half, t:t + 1])
                if half:
                    link(m)

            def normalise(n):
                link(V.tensor_tensor(ss2, ssh[:, 0, :], ssh[:, 1, :], ALU.add))
                inverse_root(rstd2, ss2, D, last=lambda ins: ins.then_inc(rstd_ok, 1))
                dve.wait_ge(rstd_ok, n + 1)
                V.tensor_scalar(w1t[:, 0, :], x[:, 0, :], rstd2[:, 0:1], None, ALU.mult).then_inc(tok_ready, 1)

            def minus_hi(out, src, scale, hi):
                if scale is None:
                    return V.tensor_tensor(out, src, hi.bitcast(F32), ALU.subtract)
                return V.scalar_tensor_tensor(out=out, in0=src, scalar=scale, in1=hi.bitcast(F32),
                                              op0=ALU.mult, op1=ALU.subtract)

            def turned_lo(n, scale, banks=range(4)):
                for b in banks:
                    dve.wait_ge(ht_hi, 4 * n + b + 1)
                    for kk in range(2):
                        k = 2 * b + kk
                        m = minus_hi(hlo[:, k, :], ps[:, 4 + b, kk * S:(kk + 1) * S], scale and scale(k), hhi[:, k, :])
                    m.then_inc(ht_lo, 1)

            def wide(v, n):
                return v.unsqueeze(len(v.shape)).to_broadcast(list(v.shape) + [n])

            link(V.memset(w4a[:, :, :], 0.0))
            dve.wait_ge(x_in, 16)
            dve.wait_ge(ident_in, 32)
            for layer in range(DEPTH):
                L = layer + 1
                if layer == 0:
                    squares(0)
                    squares(1)
                normalise(2 * layer)
                turned_lo(3 * layer, lambda k: par("norm1", layer * KD + k))

                def lo_a(s, r=0):
                    if shared("A", s):
                        lo_of(dve, layer, "A", s, r)

                lo_a(2)
                wait_used(dve, layer, "A", 1)
                V.tensor_copy(w4a[:, :, TAPS - 1:], ps[:, 0:4, 0:S]).then_inc(conv_pad, 1)
                lo_a(3)
                lo_a(4)
                dve.wait_ge(conv_pad, L)
                for j in range(TAPS):
                    for c in range(4):
                        tap = par("conv", (layer * 4 + c) * TAPS + j)
                        if j == 0:
                            m = V.tensor_scalar(w4b[:, c, :], w4a[:, c, 0:S], tap, None, ALU.mult)
                        else:
                            m = V.scalar_tensor_tensor(out=w4b[:, c, :], in0=w4a[:, c, j:j + S], scalar=tap,
                                                       in1=w4b[:, c, :], op0=ALU.mult, op1=ALU.add)
                    if j < TAPS - 1:
                        link(m)
                m.then_inc(conv_y, 1)
                dve.wait_ge(z8_mm, L)
                V.tensor_copy(z8, ps[:, 6, 0:16].rearrange("p (t n) -> p t n", t=TT)).then_inc(z8_sb, 1)

                def z_copy(q, r=0):
                    wait_used(dve, layer, "A", 3 + 2 * q, r)
                    _, c, n = chunk(q)
                    dst = z[:, :, c:c + n] if isinstance(r, int) else z[:, :, bass.ds(r * (3 * C) + c, n)]
                    V.tensor_copy(dst, ps[:, pair(q):pair(q) + 2, 0:n]).then_inc(z_out, 1)
                lo_a(5)
                z_copy(0)

                if layer == 0:
                    dve.wait_ge(consts_in, 16)
                dve.wait_ge(row_t, L)
                R = lambda n: rowt[:, n, :]
                V.tensor_scalar(R(0), ps[0:MH, 7, 0:S], par("ib", layer)[0:MH], None, ALU.add)
                link(V.tensor_scalar(R(1), ps[0:MH, 7, S:2 * S], par("fb", layer)[0:MH], None, ALU.add))
                V.scalar_tensor_tensor(out=R(3), in0=R(1), scalar=-1.0, in1=R(1), op0=ALU.mult, op1=ALU.max).then_inc(row_abs, 1)
                dve.wait_ge(row_exp, L)
                link(V.tensor_scalar(R(4), R(2), 1.0, None, ALU.add))
                link(V.tensor_scalar(R(5), R(4), 1.0, None, ALU.subtract))
                link(V.tensor_tensor(R(5), R(2), R(5), ALU.subtract))
                link(V.reciprocal(R(4), R(4)))
                link(V.tensor_tensor(R(5), R(5), R(4), ALU.mult))
                dve.wait_ge(row_ln, L)
                link(V.tensor_tensor(R(3), R(3), R(5), ALU.add))
                V.scalar_tensor_tensor(out=R(1), in0=R(1), scalar=0.0, in1=R(3), op0=ALU.min, op1=ALU.subtract)
                link(V.memset(R(5), 1.0))
                link(V.tensor_tensor_scan(R(4), R(5), R(1), 0.0, ALU.mult, ALU.add))
                link(V.tensor_tensor(rows[:, 0, :], R(0), R(4), ALU.subtract))
                link(V.tensor_tensor_scan(R(2), rows[:, 0, :], rows[:, 0, :], 0.0, ALU.max, ALU.max))
                V.tensor_scalar(rows[:, 1, :], R(2), -1.0, None, ALU.mult)
                V.scalar_tensor_tensor(out=rows[:, 2, :], in0=R(4), scalar=-1.0, in1=R(2), op0=ALU.mult,
                                       op1=ALU.subtract).then_inc(rows_ok, 1)

                def rotate(t):
                    def step(n, ins):
                        ins.then_inc(rot_step, 1)
                        dve.wait_ge(rot_step, t * ROT_STEPS + (layer * TT * ROT_STEPS + n))
                    dve.wait_ge(z_out, t * 3 + (layer * Q_G + 2))
                    v = z[:, bass.ds(t, 1), 0:Z_RV].rearrange("p t (h f d) -> p (t h) f d", f=2, d=64)
                    x1, x2 = v[:, :, 0, :], v[:, :, 1, :]
                    cos, sin = (rot[:, bass.ds(t, 1), f, :].to_broadcast([P, 8, 64]) for f in range(2))
                    A, B, Cc = (w2[:, n * 512:(n + 1) * 512].rearrange("p (h d) -> p h d", d=64) for n in range(3))
                    V.tensor_tensor(A, x1, cos, ALU.mult)
                    V.tensor_tensor(Cc, x1, sin, ALU.mult)
                    step(1, V.tensor_tensor(B, x2, sin, ALU.mult))
                    step(2, V.tensor_tensor(x1, A, B, ALU.subtract))
                    step(3, V.tensor_tensor(A, x2, cos, ALU.mult))
                    step(4, V.tensor_tensor(x2, Cc, A, ALU.add))

                with dve.Fori(0, (N_LOOP - 2) // 3) as i:
                    for q in (2, 3, 4):
                        for h in range(2):
                            lo_a(2 + 2 * q + h, i)
                        z_copy(q - 1, i)
                        if q == 2:
                            rotate(i)
                z_copy(N_LOOP - 1)
                dve.wait_ge(col_t, L)
                V.tensor_copy(st[:, 20:36], ps[:, 7, 0:16]).then_inc(col_sb, 1)

                dve.wait_ge(dsq, L)
                V.tensor_reduce(dss[:, 0, :], w2[:, :].rearrange("p (h d) -> p h d", d=DH), AX, ALU.add)
                V.tensor_reduce(dss[:, 1, :], w1[:, 0:BLK * 4].rearrange("p (h d) -> p h d", d=DH), AX,
                                ALU.add).then_inc(dsum, 1)
                dve.wait_ge(dsum, L)
                inverse_root(drs, dss, DH)
                for t in range(TT):
                    v = z[:, t, Z_DQ:Z_DV].rearrange("p (h d) -> p h d", d=DH)
                    m = V.tensor_tensor(v, v, wide(drs[:, t, :], DH), ALU.mult)
                m.then_inc(dn_ok, 1)
                z_copy(Q_HALF)

                dve.wait_ge(rsc_mm, L)
                V.tensor_tensor(blk2, ps[:, 4:8, 0:BLK], decay, ALU.mult).then_inc(rsc_sb, 1)
                z_copy(Q_MV)
                dve.wait_ge(rpv_sq, L)
                link(V.tensor_reduce(rss, big2.rearrange("p t (h d) -> p (t h) d", d=RDV), AX, ALU.add))
                inverse_root(rrs, rss, RDV)
                link(V.tensor_tensor(big2.rearrange("p t (h d) -> p t h d", d=RDV),
                                     ps[:, 4:6, :].rearrange("p t (h d) -> p t h d", d=RDV),
                                     wide(rrs.rearrange("p (t h) -> p t h", t=TT), RDV), ALU.mult))
                dve.wait_ge(rg_act, L)
                V.tensor_tensor(z[:, :, Z_RG:Z_DQ], big2, z[:, :, Z_RG:Z_DQ], ALU.mult).then_inc(ro_out, 1)

                def da_masked(g):
                    dve.wait_ge(dsc_mm, layer * NG + g + 1)
                    for h in (slice(0, 2), slice(2, 4)):
                        link(V.scalar_tensor_tensor(out=blk2[:, h, :], in0=ps[:, 4 + h.start:4 + h.stop, 0:BLK],
                                                    scalar=DH ** -0.5,
                                                    in1=damask[:, g, :].unsqueeze(1).to_broadcast([P, 2, BLK]),
                                                    op0=ALU.mult, op1=ALU.add))
                        V.tensor_reduce(dneg[:, g, 0, h], blk2[:, h, 0:P], AX, ALU.max)
                        link(V.tensor_reduce(dneg[:, g, 1, h], blk2[:, h, P:BLK], AX, ALU.max))
                        V.tensor_scalar(dneg[:, g, :, h], dneg[:, g, :, h], -1.0, None, ALU.mult).then_inc(dsc_sb, 1)

                def da_keep(g):
                    dve.wait_ge(dpv_mm, layer * NG + g + 1)
                    V.tensor_copy(z[:, :, Z_DQ + g * GH * DH:Z_DQ + (g + 1) * GH * DH],
                                  ps[:, 6:8, 0:GH * DH]).then_inc(dpv_sb, 1)

                def out_lo(n, bank, hi, lo, k0, scale):
                    dve.wait_ge(ot_hi, layer * 5 + n + 1)
                    for kk in range(2):
                        m = minus_hi(lo[:, k0 + kk, :], ps[:, bank, kk * S:(kk + 1) * S], scale and scale(kk),
                                     hi[:, k0 + kk, :])
                    m.then_inc(ot_lo, 1)
                out_lo(0, 6, ahi, alo, 0, lambda k: par("retn", layer * 4 + k))
                out_lo(1, 7, ahi, alo, 2, lambda k: par("retn", layer * 4 + 2 + k))
                z_copy(Q_MO)
                da_masked(0)
                da_keep(0)
                da_masked(1)
                da_keep(1)
                da_masked(2)
                da_keep(2)
                dve.wait_ge(msel_mm, L)
                sp_ = ps[:, 4:6, :].rearrange("p a (b s) -> p a b s", b=2)
                for a_ in range(2):
                    V.tensor_tensor(blkm[:, a_, :, 0:S], sp_[:, a_], mlmask[:, 0:S].unsqueeze(1).to_broadcast([P, 2, S]),
                                    ALU.add)
                    m = V.tensor_tensor(blkm[:, a_, :, S:BLK], sp_[:, a_, :, P:S],
                                        mlmask[:, S:BLK].unsqueeze(1).to_broadcast([P, 2, P]), ALU.add)
                m.then_inc(mdw_in, 1)
                dve.wait_ge(dln, L)
                G = lambda v, g: v[:, g, :, :].rearrange("p t h -> p (t h)")
                over = dtmp.unsqueeze(1).to_broadcast([P, NG, 8])
                flat = lambda v: v.rearrange("p g t h -> p g (t h)")
                link(V.tensor_tensor(flat(dco), flat(dco), flat(dneg), ALU.subtract))
                link(V.tensor_tensor(dtmp, G(dco, 0), G(dco, 1), ALU.max))
                link(V.tensor_tensor(dtmp, dtmp, G(dco, 2), ALU.max))
                V.tensor_tensor(flat(dco), flat(dco), over, ALU.subtract).then_inc(dlse, 1)
                dve.wait_ge(dwt, L)
                link(V.tensor_tensor(dtmp, G(dco, 0), G(dco, 1), ALU.add))
                link(V.tensor_tensor(dtmp, dtmp, G(dco, 2), ALU.add))
                link(V.tensor_tensor(flat(dl), flat(dl), over, ALU.mult))
                link(V.reciprocal(flat(dl), flat(dl)))
                link(V.tensor_tensor(flat(dco), flat(dco), flat(dl), ALU.mult))
                og = [z[:, :, Z_DQ + g * GH * DH:Z_DQ + (g + 1) * GH * DH].rearrange("p t (h d) -> p t h d", d=DH)
                      for g in range(NG)]
                for g in range(NG):
                    m = V.tensor_tensor(og[g], og[g], wide(dco[:, g, :, :], DH), ALU.mult)
                link(m)
                link(V.tensor_tensor(og[0], og[0], og[1], ALU.add))
                V.tensor_tensor(og[0], og[0], og[2], ALU.add).then_inc(do_out, 1)
                dve.wait_ge(msc_mm, L)
                dve.wait_ge(mdw, L)
                for a_ in range(2):
                    m = V.scalar_tensor_tensor(out=blkm[:, a_], in0=ps[:, 4 + 2 * a_:6 + 2 * a_, 0:BLK], scalar=MDK ** -0.5,
                                               in1=blkm[:, a_], op0=ALU.mult, op1=ALU.mult)
                m.then_inc(msc_sb, 1)
                dve.wait_ge(mpv_mm, L)
                dve.wait_ge(col_exp, L)
                link(V.tensor_copy(mden, ps[:, 6, 0:8]))
                link(V.scalar_tensor_tensor(out=mden, in0=mden, scalar=-1.0, in1=mden, op0=ALU.mult, op1=ALU.max))
                link(V.tensor_tensor(mden, mden, emcol, ALU.max))
                link(V.reciprocal(mden, mden))
                V.tensor_tensor(big2.rearrange("p t (h d) -> p t h d", d=MDV),
                                ps[:, 4:6, :].rearrange("p t (h d) -> p t h d", d=MDV),
                                wide(mden.rearrange("p (t h) -> p t h", t=TT), MDV), ALU.mult).then_inc(mh_sb, 1)
                dve.wait_ge(msq, L)
                link(V.tensor_reduce(mss, w1[:, 0:TT * 512].rearrange("p (n d) -> p n d", d=MDV), AX, ALU.add))
                inverse_root(mrs, mss, MDV)
                big2h = big2.rearrange("p t (h d) -> p (t h) d", d=MDV)
                link(V.tensor_tensor(big2h, big2h, wide(mrs, MDV), ALU.mult))
                dve.wait_ge(mo_act, L)
                V.tensor_tensor(z[:, :, Z_MO:Z_G], big2, z[:, :, Z_MO:Z_G], ALU.mult).then_inc(mo_out, 1)

                out_lo(2, 7, hhi, hlo, 4, None)

                gated = lambda n: z[:, :, Z_G + n * C:Z_G + (n + 1) * C]

                def branch_out(n):
                    half = n % 2
                    if n == 2:
                        dve.wait_ge(br_half, L)
                    else:
                        wait_used(dve, layer, "A", S_BR + (0, 1, 0, 2, 3, 4)[n])
                    V.tensor_tensor(gated(n), gated(n), ps[:, 2 * (1 - half):2 * (1 - half) + 2, :],
                                    ALU.mult).then_inc(br_out, 1)
                    if n >= 2:
                        dve.wait_ge(br_out, layer * 6 + n + 1)
                        m = V.tensor_tensor(gated(half), gated(half), gated(n), ALU.add)
                        if n >= 4:
                            m.then_inc(tok_ready, 1)
                        else:
                            link(m)
                dve.wait_ge(sig_ok, L)
                branch_out(0)
                out_lo(3, 4, hhi, hlo, 0, lambda k: par("mln", layer * 4 + k))
                out_lo(4, 5, hhi, hlo, 2, lambda k: par("mln", layer * 4 + 2 + k))
                branch_out(1)
                branch_out(2)
                branch_out(3)
                dve.wait_ge(g_out, L * N_G)
                branch_out(4)
                turned_lo(3 * layer + 1, None, (0, 1))
                branch_out(5)
                turned_lo(3 * layer + 1, None, (2, 3))
                for half in range(2):
                    wait_used(dve, layer, "A", S_BR + 6 + 2 * half)
                    v = x[:, :, half * C:(half + 1) * C]
                    link(V.tensor_tensor(v, v, ps[:, 2 * (1 - half):2 * (1 - half) + 2, :], ALU.add))
                    squares(half)
                normalise(2 * layer + 1)
                turned_lo(3 * layer + 2, lambda k: par("norm2", layer * KD + k))

                if layer == 0:
                    def lo_(s, r=0):
                        lo_of(dve, 0, "B", s, r)

                    def f_mult(s, i, r=0, n=C):
                        wait_used(dve, 0, "B", s, r)
                        dve.wait_ge(silu, i * 2 + 2)
                        if s > 3:
                            dve.wait_ge(a_t, i * 2)
                        for t in range(TT):
                            V.tensor_tensor(act_sb[:, t, 0:n], sil_sb[:, t, 0:n], ps[:, 2 + t, 0:n],
                                            ALU.mult).then_inc(a_ok, 1)

                    def f_lo(i, n=4):
                        for t in range(TT):
                            dve.wait_ge(a_hi, i * 2 + t + 1)
                            minus_hi(alo[:, 0:n, t * P:(t + 1) * P],
                                     ps[:, 4 + t, 0:n * P].rearrange("p (k c) -> p k c", k=n), None,
                                     ahi[:, 0:n, t * P:(t + 1) * P]).then_inc(a_lo, 1)

                    def f_sum(s, half, r=0):
                        wait_used(dve, 0, "B", s, r)
                        for t in range(TT):
                            v = x[:, t, half * C:(half + 1) * C]
                            V.tensor_tensor(v, v, ps[:, 6 - 2 * half + t, :], ALU.add).then_inc(d_out, 1)

                    def f_round(s, i, r=0, before=True):
                        lo_(s, r)
                        f_mult(s - 3 if before else s - 1, i - 1, r)
                        lo_(s + 1, r)
                        if before:
                            f_sum(s - 2, 0, r)
                        lo_(s + 2, r)
                        if before:
                            f_sum(s - 1, 1, r)
                        lo_(s + 3, r)
                        f_lo(i - 1)
                        lo_(s + 4, r)
                        lo_(s + 5, r)

                    for s in range(4):
                        lo_(s)
                    f_round(4, 1, before=False)
                    with dve.Fori(0, F_CHUNKS - 2) as i:
                        f_round(10, i + 2, i)
                    s0 = F_SLOTS - 8
                    f_round(s0, F_CHUNKS)
                    lo_(s0 + 6)
                    f_mult(s0 + 3, F_CHUNKS, n=HALF)
                    lo_(s0 + 7)
                    f_sum(s0 + 4, 0)
                    f_sum(s0 + 5, 1)
                    f_lo(F_CHUNKS, HALF // P)
                    f_sum(s0 + 6, 0)
                    dve.wait_ge(d_out, F_SUMS - 2)
                    squares(0)
                    f_sum(s0 + 7, 1)
                    dve.wait_ge(d_out, F_SUMS)
                    squares(1)
                    continue

                for s in range(2):
                    lo_of(dve, 1, "B", s)
                V.memset(yacc, 0.0).then_inc(y_zero, 1)
                V.memset(spread, 0.0).then_inc(spread_sb, 1)
                V.memset(posx[:, :, :], -1000.0)
                V.memset(gatex[:, :, :], 0.0)
                link(V.memset(eidf, 0.0))
                link(V.tensor_copy(eidf[:, 0:NE], iota[:, 0:NE]))

                dve.wait_ge(lg_mm, 1)
                link(V.tensor_tensor(lg, ps[:, 0, 0:16].rearrange("p (t n) -> p t n", t=TT),
                                     par("rb", 0, NE).unsqueeze(1).to_broadcast([P, TT, NE]), ALU.add))

                def first_max(src, v, m, cum):
                    link(V.tensor_reduce(v, src, AX, ALU.max))
                    link(V.tensor_tensor(m, src, v.to_broadcast([P, TT, NE]), ALU.is_equal))
                    for t in range(TT):
                        c = V.tensor_tensor_scan(cum[:, t, :], ones[:, 0:NE], m[:, t, :], 0.0, ALU.mult, ALU.add)
                    link(c)
                    link(V.scalar_tensor_tensor(out=m, in0=cum, scalar=1.0, in1=m, op0=ALU.is_equal, op1=ALU.mult))

                first_max(lg, v12[:, :, 0:1], m1, rt)
                link(V.scalar_tensor_tensor(out=rtmp, in0=m1, scalar=-1e30, in1=lg, op0=ALU.mult, op1=ALU.add))
                first_max(rtmp, v12[:, :, 1:2], m2, rt)
                V.tensor_tensor(v12[:, :, 2:3], v12[:, :, 1:2], v12[:, :, 0:1], ALU.subtract).then_inc(lg_d, 1)
                V.tensor_tensor(rt, m1, m2, ALU.add).then_inc(sel_ok, 1)
                dve.wait_ge(lg_e, 1)
                link(V.tensor_scalar(v12[:, :, 3:4], v12[:, :, 2:3], 1.0, None, ALU.add))
                link(V.reciprocal(v12[:, :, 3:4], v12[:, :, 3:4]))
                link(V.tensor_tensor(v12[:, :, 2:3], v12[:, :, 2:3], v12[:, :, 3:4], ALU.mult))
                V.tensor_tensor(m1, m1, v12[:, :, 3:4].to_broadcast([P, TT, NE]), ALU.mult)
                link(V.tensor_tensor(m2, m2, v12[:, :, 2:3].to_broadcast([P, TT, NE]), ALU.mult))
                link(V.tensor_tensor(gatex[:, :, 0:NE], m1, m2, ALU.add))
                dve.wait_ge(cnt_mm, 1)
                dve.wait_ge(sel_ok, 1)
                link(V.scalar_tensor_tensor(out=posx[:, :, 0:NE], in0=ps[:, 1, 0:16].rearrange("p (t n) -> p t n", t=TT),
                                            scalar=1000.0, in1=rt, op0=ALU.add, op1=ALU.mult))
                link(V.tensor_scalar(posx[:, :, 0:NE], posx[:, :, 0:NE], 1000.0, None, ALU.subtract))
                def picks(n):
                    for t in range(TT):
                        p_ = posx[:, t, bass.ds(n, 1)]
                        V.tensor_scalar(pickg[:, t, :], iota, p_, gatex[:, t, bass.ds(n, 1)], ALU.is_equal, ALU.mult)
                        m = V.tensor_scalar(pick[:, t, :], iota, p_, None, ALU.is_equal)
                    m.then_inc(pick_ok, 1)
                picks(0)

                link(V.tensor_scalar(big, ps[:, 1, 16:24], float(CAP), None, ALU.is_gt))
                link(V.tensor_tensor_scan(rank, ones[:, 0:NE], big, 0.0, ALU.mult, ALU.add))
                V.tensor_scalar(eidf[:, 14:15], rank[:, NE - 1:NE], float(NE - 1), None, ALU.add)
                link(V.tensor_scalar(eidf[:, 15:16], rank[:, NE - 1:NE], float(NE), None, ALU.add))

                def second(n):
                    link(V.scalar_tensor_tensor(out=selx, in0=rank, scalar=float(n + 1), in1=big,
                                                op0=ALU.is_equal, op1=ALU.mult))

                def pick_sum(src, dst):
                    link(V.tensor_tensor_reduce(out=cnt, in0=selx, in1=src, scale=1.0, scalar=0.0, op0=ALU.mult,
                                                op1=ALU.add, accum_out=dst))
                for n in range(EXTRA):
                    second(n)
                    pick_sum(iota[:, 0:NE], eidf[:, NE + n:NE + n + 1])
                V.tensor_copy(eid[:, :], eidf[0:1, :]).then_inc(route_ok, 1)

                def second_places():
                    for n in range(EXTRA):
                        second(n)
                        for t in range(TT):
                            pick_sum(posx[:, t, 0:NE], posx[:, t, NE + n:NE + n + 1])
                            pick_sum(gatex[:, t, 0:NE], gatex[:, t, NE + n:NE + n + 1])
                    link(V.tensor_scalar(posx[:, :, NE:NE + EXTRA], posx[:, :, NE:NE + EXTRA], float(CAP), None,
                                         ALU.subtract))

                def e_mult(s, n, r):
                    wait_used(dve, 1, "B", s, r)
                    dve.wait_ge(silu, n + (F_TILES + 1))
                    dve.wait_ge(a_t, n + F_TILES)
                    V.tensor_tensor(act_sb[:, 0, :], sil_sb[:, 0, :], ps[:, 1, :], ALU.mult).then_inc(a_ok, 1)

                def e_lo(n):
                    dve.wait_ge(a_hi, n + (F_TILES + 1))
                    minus_hi(alo[:, :, 0:CAP], ps[:, 2, :].rearrange("p (k c) -> p k c", k=4), None,
                             ahi[:, :, 0:CAP]).then_inc(a_lo, 1)

                def e_sum(s, half, r):
                    wait_used(dve, 1, "B", s, r)
                    v = yacc[:, half * C:(half + 1) * C]
                    V.tensor_tensor(v, v, ps[:, 3 + half, :], ALU.add).then_inc(d_out, 1)

                def e_lo_tokens(j):
                    dve.wait_ge(gt_hi, j + 1)
                    for k in range(KD):
                        m = minus_hi(hlo[:, k, 0:CAP], ps[:, 5 + k // 4, k % 4 * P:(k % 4 + 1) * P],
                                     par("norm2", KD + k), hhi[:, k, 0:CAP])
                    m.then_inc(gt_lo, 1)

                def scattered(n):
                    for k, bank in enumerate((7, 3, 4, 2)):
                        dve.wait_ge(scat_mm, n * 4 + k + 1)
                        v = x[:, k // 2, k % 2 * C:(k % 2 + 1) * C]
                        V.tensor_tensor(v, v, ps[:, bank, :], ALU.add).then_inc(d_out, 1)
                    V.memset(yacc, 0.0).then_inc(y_zero, 1)

                def lo_(s, r):
                    lo_of(dve, 1, "B", s, r)

                def e_round(s, n, r, before=True):
                    lo_(s, r)
                    e_mult(s - 3 if before else s - 1, n - 1, r)
                    lo_(s + 1, r)
                    if before:
                        e_sum(s - 2, 0, r)
                    lo_(s + 2, r)
                    if before:
                        e_sum(s - 1, 1, r)
                    lo_(s + 3, r)
                    e_lo(n - 1)
                    lo_(s + 4, r)
                    lo_(s + 5, r)

                def e_rest(j):
                    n0 = j * E_CHUNKS
                    for s in (2, 3):
                        lo_(s, n0)
                    scattered(j)
                    dve.wait_ge(y_zero, j + 2)
                    e_round(4, n0 + 1, n0, before=False)
                    dve.wait_ge(spread_t, j + 1)
                    picks(j + 1)
                    with dve.Fori(0, E_CHUNKS - 2) as i:
                        e_round(10, i + n0 + 2, i + n0)
                    lo_(E_SLOTS - 2, n0)
                    e_mult(E_SLOTS - 5, n0 + (E_CHUNKS - 1), n0)
                    lo_(E_SLOTS - 1, n0)
                    e_sum(E_SLOTS - 4, 0, n0)
                    e_sum(E_SLOTS - 3, 1, n0)
                    e_lo(n0 + (E_CHUNKS - 1))

                e_lo_tokens(0)
                second_places()
                dve.wait_ge(route_ok, 1)
                last = dve.value_load(eid[0:1, 14:15], min_val=NE - 1, max_val=ITEMS - 1)
                with dve.Fori(0, last) as j:
                    e_rest(j)
                    n0, n1 = j * E_CHUNKS, j * E_CHUNKS + E_CHUNKS
                    lo_(0, n1)
                    e_lo_tokens(j + 1)
                    e_sum(E_SLOTS - 2, 0, n0)
                    lo_(1, n1)
                    e_sum(E_SLOTS - 1, 1, n0)
                e_rest(last)
                e_sum(E_SLOTS - 2, 0, last * E_CHUNKS)
                e_sum(E_SLOTS - 1, 1, last * E_CHUNKS)
                scattered(last + 1)
                dve.wait_ge(y_zero, last + 3)
                V.memset(cnt, 0.0).then_inc(x_end, 1)


def _constants():
    f = np.float32
    c = np.zeros((P, N_CONST), f)

    def put(name, v):
        lo, hi = CONST[name]
        c[:v.shape[0], lo:hi] = v.reshape(v.shape[0], -1)
    put("ident", np.eye(P, dtype=f))
    half = RDV // 2
    inv = np.power(f(10000.0), -np.arange(half, dtype=f) / f(half)).astype(f)
    ang = (np.arange(S, dtype=f)[:, None] * inv[None, :]).astype(f).astype(np.float64)
    rot = np.stack([np.cos(ang), np.sin(ang)], 1).astype(f)
    put("rot", rot.reshape(TT, P, 2, half).transpose(1, 0, 2, 3))
    i = np.arange(S)
    rel = i[None, :] - i[:, None]
    log_gamma = np.log1p(-np.exp2(-5.0 - np.arange(RH)))
    decay = np.where(rel >= 0, np.exp(log_gamma[:, None, None] * np.maximum(rel, 0)), 0.0) * RDV ** -0.5
    put("decay", np.concatenate([decay[:, :P, :], decay[:, P:, P:]], 2).transpose(1, 0, 2).astype(f))
    ok = np.stack([(rel.T >= 0) & (rel.T % d == 0) & (rel.T <= w) for w, d in GROUPS])
    mask = np.where(ok, 0.0, -1e30).astype(f)
    put("damask", np.concatenate([mask[:, :P, :P], mask[:, P:, :]], 2).transpose(1, 0, 2))
    ml = np.where(rel >= 0, 0.0, -1e30).astype(f)
    put("mlmask", np.concatenate([ml[:P, :], ml[P:, P:]], 1))
    put("tri", np.triu(np.ones((P, P), f), 1))
    put("ones", np.ones((P, P), f))
    put("iota", np.broadcast_to(np.arange(P, dtype=f), (P, P)))
    put("sel", np.repeat(np.eye(MH, dtype=f), P, 1))
    return c


def _small(w):
    s = np.zeros((P, N_SMALL), np.float32)

    def put(name, v):
        lo, hi = SMALL[name]
        s[:v.shape[0], lo:hi] = v.reshape(v.shape[0], -1)
    tiles = lambda v: v.reshape(DEPTH, -1, P).transpose(2, 0, 1)
    for name, v in (("norm1", "norm1_w"), ("norm2", "norm2_w"), ("retn", "ret_norm_w"), ("mln", "ml_norm_w")):
        put(name, tiles(w[v]))
    for name, v in (("qn", "da_q_norm_w"), ("kn", "da_k_norm_w")):
        put(name, np.concatenate([w[v], w[v]], 1).T)
    put("conv", w["ml_conv_w"].reshape(DEPTH, TAPS, 4, P).transpose(3, 0, 2, 1))
    put("ib", w["ml_i_bias"].T)
    put("fb", w["ml_f_bias"].T)
    put("rb", np.broadcast_to(w["moe_b_router"], (P, NE)))
    put("gates", w["w_in"][:, :, IN_GATES:IN_G].reshape(DEPTH, KD, P, 8).transpose(2, 0, 1, 3))
    put("router", w["moe_w_router"][0].reshape(KD, P, NE).transpose(1, 0, 2))
    return s


_WHOLE = ["x", "w_in", "w_br_ret", "w_br_da", "w_br_ml", "w_out", "ffn_w_gate", "ffn_w_up", "ffn_w_down",
          "moe_w_gate", "moe_w_up", "moe_w_down"]


def kernel(**inputs):
    from concourse import bacc
    from concourse.bass_utils import run_bass_kernel_spmd

    w = {name: np.ascontiguousarray(v) for name, v in inputs.items()}
    arrays = {name: w[name] for name in _WHOLE}
    arrays["const"], arrays["small"] = _constants(), _small(w)
    nc = bacc.Bacc("TRN2", target_bir_lowering=False, num_devices=1)
    a = {name: nc.dram_tensor(f"in_{name}_dram", v.shape, mybir.dt.from_np(v.dtype), kind="ExternalInput").ap()
         for name, v in arrays.items()}
    a["out"] = nc.dram_tensor("out_dram", w["x"].shape, F32, kind="ExternalOutput").ap()
    build(nc, a)
    r = run_bass_kernel_spmd(nc, [{f"in_{name}_dram": v for name, v in arrays.items()}], core_ids=[0])
    return r.results[0]["out_dram"]
```
